# Optimizing a Trainium2 kernel written in Bass

```python
import math, functools
import jax, jax.numpy as jnp
from jax import lax
import numpy as np

D_MODEL = 1024
BATCH = 1
SEQ = 512
DEPTH = 2
DEC_BATCH = 8
DEC_SEQ = 1
PAST_LEN = 2048
PAGE_SIZE = 128

N_A_LAYERS = DEPTH // 2
N_B_LAYERS = DEPTH - N_A_LAYERS
HEAD_DIM = 64
D_MEM = D_MODEL // 4
N_MEM_HEADS = D_MEM // HEAD_DIM
N_MEM_TOK = 256
D_RNN = D_MODEL - D_MEM
N_LRU_BLOCKS = D_RNN // HEAD_DIM
LRU_BLOCK = D_RNN // N_LRU_BLOCKS
CONV_W = 4
LRU_C = 8.0
N_HEADS = D_RNN // HEAD_DIM
N_KV_GROUPS = 4
HEADS_PER_GROUP = N_HEADS // N_KV_GROUPS
CMP_LEN = 32
CMP_STRIDE = 16
CMP_HID = 2 * HEAD_DIM
SEL_LEN = 64
N_SEL = 16
WINDOW = 512
N_BUCKETS = 32
MAX_DISTANCE = 1024
N_GROUPS = 4
EXPERTS_PER_GROUP = 8
N_EXPERTS = N_GROUPS * EXPERTS_PER_GROUP
D_EXPERT = 128
TOP_K_IN_GROUP = 2
ALPHA = (2 * DEPTH) ** 0.25
BETA = (8 * DEPTH) ** -0.25
Q_BLOCK = 128
LN_EPS = 1e-5
NEG = -1e30
FORCE = 1e9
SCALE = HEAD_DIM ** -0.5
D_IN_A = 2 * D_RNN + D_MEM
D_IN_B = N_HEADS * HEAD_DIM + 3 * N_HEADS + D_MEM
D_KV_SHARED = 3 * 2 * N_KV_GROUPS * HEAD_DIM

kernel_name = 'yoco_hawk_nsa_hmoe_decoder_step'

def layer_norm(x, g, b):
    xf = x.astype(jnp.float32)
    mu = jnp.mean(xf, axis=-1, keepdims=True)
    var = jnp.mean(jnp.square(xf - mu), axis=-1, keepdims=True)
    y = (xf - mu) * lax.rsqrt(var + LN_EPS) * g.astype(jnp.float32) + b.astype(jnp.float32)
    return y.astype(x.dtype)

def post_norm(x, sub, g, b):
    return layer_norm(ALPHA * x + sub.astype(x.dtype), g, b)

def masked_softmax(logits, mask):
    p = jax.nn.softmax(jnp.where(mask, logits, NEG), axis=-1)
    return jnp.where(mask, p, 0.0)

def rel_bucket(dist):
    n = jnp.maximum(dist, 0)
    max_exact = N_BUCKETS // 2
    nf = jnp.maximum(n, 1).astype(jnp.float32)
    large = max_exact + (jnp.log(nf / max_exact) / math.log(MAX_DISTANCE / max_exact)
                         * (N_BUCKETS - max_exact)).astype(jnp.int32)
    large = jnp.minimum(large, N_BUCKETS - 1)
    return jnp.where(n < max_exact, n, large)

def bias_qk(tab, dist):
    q_len, k_len = dist.shape
    b = tab[rel_bucket(dist)].reshape(q_len, k_len, N_KV_GROUPS, HEADS_PER_GROUP)
    return b.transpose(0, 2, 3, 1).astype(jnp.float32)

def mem_attn(qm, mk, mv):
    bsz, t_len, _ = qm.shape
    q = qm.reshape(bsz, t_len, N_MEM_HEADS, HEAD_DIM)
    logits = jnp.einsum('bthd,bmhd->bhtm', q, mk).astype(jnp.float32) * SCALE
    p = jax.nn.softmax(logits, axis=-1).astype(mv.dtype)
    return jnp.einsum('bhtm,bmhd->bthd', p, mv).reshape(bsz, t_len, D_MEM)

def rglru(xr, cw, cb, wrg, brg, wig, big, lam, conv_buf, h0):
    bsz, t_len, _ = xr.shape
    xp = jnp.concatenate([conv_buf.astype(xr.dtype), xr], axis=1)
    xc = cb + sum(xp[:, k:k + t_len] * cw[k] for k in range(CONV_W))
    xb = xc.reshape(bsz, t_len, N_LRU_BLOCKS, LRU_BLOCK)
    r = jax.nn.sigmoid((jnp.einsum('btni,nij->btnj', xb, wrg).reshape(bsz, t_len, D_RNN) + brg).astype(jnp.float32))
    i = jax.nn.sigmoid((jnp.einsum('btni,nij->btnj', xb, wig).reshape(bsz, t_len, D_RNN) + big).astype(jnp.float32))
    log_a = -LRU_C * r * jax.nn.softplus(-lam.astype(jnp.float32))
    a = jnp.exp(log_a)
    u = jnp.sqrt(-jnp.expm1(2.0 * log_a)) * i * xc.astype(jnp.float32)

    def step(h, au):
        a_t, u_t = au
        h = a_t * h + u_t
        return h, h

    h_t, hs = lax.scan(step, h0.astype(jnp.float32), (jnp.swapaxes(a, 0, 1), jnp.swapaxes(u, 0, 1)))
    return jnp.swapaxes(hs, 0, 1).astype(xr.dtype), h_t, xp[:, t_len:]

def mixer_a(x, w_in, cw, cb, wrg, brg, wig, big, lam, conv_buf, h0, mk, mv, wo):
    proj = x @ w_in
    gate = jax.nn.gelu(proj[..., :D_RNN])
    y, h_t, buf = rglru(proj[..., D_RNN:2 * D_RNN], cw, cb, wrg, brg, wig, big, lam, conv_buf, h0)
    mix = jnp.concatenate([gate * y, mem_attn(proj[..., 2 * D_RNN:], mk, mv)], axis=-1)
    return mix @ wo, h_t, buf

def shared_kv(h, w_kv):
    bsz, t_len, _ = h.shape
    kv = (h @ w_kv).reshape(bsz, t_len, 3, 2, N_KV_GROUPS, HEAD_DIM)
    return kv[:, :, 0], kv[:, :, 1], kv[:, :, 2]

def compress(rows, pe, w1, b1, w2):
    bsz, t_len = rows.shape[:2]
    n_chunk = t_len // CMP_STRIDE
    r = CMP_LEN // CMP_STRIDE
    nc = n_chunk - r + 1
    chunks = rows[:, :n_chunk * CMP_STRIDE].reshape(bsz, n_chunk, CMP_STRIDE, N_KV_GROUPS, HEAD_DIM)
    blocks = jnp.concatenate([chunks[:, m:m + nc] for m in range(r)], axis=2)
    blocks = blocks + pe[None, None, :, None, :]
    flat = blocks.transpose(0, 1, 3, 2, 4).reshape(bsz, nc, N_KV_GROUPS, CMP_LEN * HEAD_DIM)
    return jax.nn.gelu(flat @ w1 + b1) @ w2

def to_sel_blocks(rows):
    bsz, t_len = rows.shape[:2]
    ns = -(-t_len // SEL_LEN)
    rows = jnp.pad(rows, ((0, 0), (0, ns * SEL_LEN - t_len), (0, 0), (0, 0)))
    return rows.reshape(bsz, ns, SEL_LEN, N_KV_GROUPS, HEAD_DIM).transpose(0, 3, 1, 2, 4)

def cmp_branch(q, q_pos, comp_k, comp_v, tab):
    nc = comp_k.shape[1]
    c_end = jnp.arange(nc) * CMP_STRIDE + (CMP_LEN - 1)
    dist = q_pos[:, None] - c_end[None, :]
    logits = jnp.einsum('bqghd,bcgd->bqghc', q, comp_k).astype(jnp.float32) * SCALE + bias_qk(tab, dist)[None]
    p = masked_softmax(logits, (dist >= 0)[None, :, None, None, :])
    return jnp.einsum('bqghc,bcgd->bqghd', p.astype(comp_v.dtype), comp_v), p

def sel_branch(q, q_pos, p_cmp, ks_g, vs_g, tab):
    bsz, q_len = q.shape[:2]
    nc = p_cmp.shape[-1]
    ns = ks_g.shape[2]
    c_start = jnp.arange(nc) * CMP_STRIDE
    s_start = jnp.arange(ns) * SEL_LEN
    cover = ((c_start[:, None] < s_start[None, :] + SEL_LEN)
             & (c_start[:, None] + CMP_LEN > s_start[None, :])).astype(jnp.float32)
    imp = jnp.einsum('bqgc,cs->bqgs', p_cmp.sum(3), cover)
    cur = q_pos // SEL_LEN
    blk = jnp.arange(ns)
    forced = (blk[None] == 0) | (blk[None] == cur[:, None]) | (blk[None] == cur[:, None] - 1)
    valid = s_start[None] <= q_pos[:, None]
    score = jnp.where(forced[None, :, None, :], FORCE, imp)
    score = jnp.where(valid[None, :, None, :], score, NEG)
    k_sel = min(N_SEL, ns)
    top_val, idx = lax.top_k(score, k_sel)
    idx = idx.transpose(0, 2, 1, 3)
    ok = (top_val > 0.5 * NEG).transpose(0, 2, 1, 3)
    gather = jax.vmap(jax.vmap(lambda blocks, ix: blocks[ix]))
    flat = idx.reshape(bsz, N_KV_GROUPS, q_len * k_sel)
    k_g = gather(ks_g, flat).reshape(bsz, N_KV_GROUPS, q_len, k_sel, SEL_LEN, HEAD_DIM)
    v_g = gather(vs_g, flat).reshape(bsz, N_KV_GROUPS, q_len, k_sel, SEL_LEN, HEAD_DIM)
    pos = idx[..., None] * SEL_LEN + jnp.arange(SEL_LEN)
    dist = q_pos[None, None, :, None, None] - pos
    mask = (dist >= 0) & ok[..., None]
    tab_g = tab.reshape(N_BUCKETS, N_KV_GROUPS, HEADS_PER_GROUP).transpose(1, 0, 2)
    bias = tab_g[jnp.arange(N_KV_GROUPS)[None, :, None, None, None], rel_bucket(dist)]
    logits = (jnp.einsum('bqghd,bgqksd->bgqhks', q, k_g).astype(jnp.float32) * SCALE
              + bias.transpose(0, 1, 2, 5, 3, 4).astype(jnp.float32))
    shp = logits.shape
    p = masked_softmax(logits.reshape(shp[0], shp[1], shp[2], shp[3], -1),
                       mask.reshape(bsz, N_KV_GROUPS, q_len, 1, -1)).reshape(shp)
    return jnp.einsum('bgqhks,bgqksd->bqghd', p.astype(v_g.dtype), v_g)

def win_branch(q, q_pos, kw, vw, kw_pos, tab):
    dist = q_pos[:, None] - kw_pos[None, :]
    mask = (dist >= 0) & (dist < WINDOW) & (kw_pos[None, :] >= 0)
    logits = jnp.einsum('bqghd,bkgd->bqghk', q, kw).astype(jnp.float32) * SCALE + bias_qk(tab, dist)[None]
    p = masked_softmax(logits, mask[None, :, None, None, :])
    return jnp.einsum('bqghk,bkgd->bqghd', p.astype(vw.dtype), vw)

def nsa_core(q, gate_logits, q_pos, comp_k, comp_v, ks_g, vs_g, kw, vw, kw_pos, tab):
    o_c, p_c = cmp_branch(q, q_pos, comp_k, comp_v, tab)
    o_s = sel_branch(q, q_pos, p_c, ks_g, vs_g, tab)
    o_w = win_branch(q, q_pos, kw, vw, kw_pos, tab)
    bsz, q_len = q.shape[:2]
    g = jax.nn.sigmoid(gate_logits.astype(jnp.float32)).reshape(bsz, q_len, N_KV_GROUPS, HEADS_PER_GROUP, 3)
    o = g[..., 0:1] * o_c + g[..., 1:2] * o_s + g[..., 2:3] * o_w
    return o.reshape(bsz, q_len, N_HEADS * HEAD_DIM).astype(q.dtype)

def nsa_prompt(q, gl, comp_k, comp_v, ks_g, vs_g, kw_pad, tab):
    bsz, t_len = q.shape[:2]

    def block(i):
        qs = i * Q_BLOCK
        qb = lax.dynamic_slice_in_dim(q, qs, Q_BLOCK, axis=1)
        gb = lax.dynamic_slice_in_dim(gl, qs, Q_BLOCK, axis=1)
        kwb = lax.dynamic_slice_in_dim(kw_pad, qs, WINDOW + Q_BLOCK, axis=1)
        q_pos = qs + jnp.arange(Q_BLOCK)
        kw_pos = qs - WINDOW + jnp.arange(WINDOW + Q_BLOCK)
        return nsa_core(qb, gb, q_pos, comp_k, comp_v, ks_g, vs_g, kwb[:, :, 0], kwb[:, :, 1], kw_pos, tab)

    out = lax.map(block, jnp.arange(t_len // Q_BLOCK))
    return out.transpose(1, 0, 2, 3).reshape(bsz, t_len, N_HEADS * HEAD_DIM)

def nsa_decode(q, gl, q_pos, comp_k, comp_v, ks_g, vs_g, kw, kw_pos, tab):
    return nsa_core(q, gl, q_pos, comp_k, comp_v, ks_g, vs_g, kw[:, :, 0], kw[:, :, 1], kw_pos, tab)

def mixer_b(x, w_in, nsa_fn, mk, mv, wo):
    bsz, t_len, _ = x.shape
    proj = x @ w_in
    nq = N_HEADS * HEAD_DIM
    q = proj[..., :nq].reshape(bsz, t_len, N_KV_GROUPS, HEADS_PER_GROUP, HEAD_DIM)
    gl = proj[..., nq:nq + 3 * N_HEADS]
    mix = jnp.concatenate([nsa_fn(q, gl), mem_attn(proj[..., nq + 3 * N_HEADS:], mk, mv)], axis=-1)
    return mix @ wo

def hmoe(x, wg, bg, we, be, w_gate, w_up, w_down):
    shp = x.shape
    xf = x.reshape(-1, shp[-1])
    lg = (xf @ wg + bg).astype(jnp.float32)
    grp = jnp.argmax(lg, axis=-1)
    g_w = jnp.take_along_axis(jax.nn.softmax(lg, axis=-1), grp[:, None], axis=1)
    le = (xf @ we + be).astype(jnp.float32).reshape(-1, N_GROUPS, EXPERTS_PER_GROUP)
    le_g = jnp.take_along_axis(le, grp[:, None, None], axis=1)[:, 0]
    tv, ti = lax.top_k(le_g, TOP_K_IN_GROUP)
    w = g_w * jax.nn.softmax(tv, axis=-1)
    e_idx = grp[:, None] * EXPERTS_PER_GROUP + ti
    combine = jnp.einsum('nk,nke->ne', w, jax.nn.one_hot(e_idx, N_EXPERTS, dtype=jnp.float32))
    hdn = jax.nn.silu(jnp.einsum('nd,edf->nef', xf, w_gate)) * jnp.einsum('nd,edf->nef', xf, w_up)
    out = jnp.einsum('nef,efd->nd', hdn * combine[..., None].astype(hdn.dtype), w_down)
    return out.reshape(shp)

def gather_pages(pool, page_table):
    g = pool[page_table]
    return g.reshape((g.shape[0], g.shape[1] * g.shape[2]) + g.shape[3:])

def setup_inputs(seed: int = 0) -> dict:
    key = jax.random.key(seed)
    keys = iter(jax.random.split(key, 48))
    f32 = jnp.float32

    def nrm(shape, scale):
        return jax.random.normal(next(keys), shape, f32) * scale

    n_pages = PAST_LEN // PAGE_SIZE
    n_used = DEC_BATCH * n_pages
    n_pool = n_used + max(1, n_used // 4)
    perm = jax.random.permutation(next(keys), n_pool)
    page_table = perm[:n_used].reshape(DEC_BATCH, n_pages).astype(jnp.int32)
    w_buf = min(WINDOW, PAST_LEN)
    kv_scale = jnp.array([1.0, BETA], f32)
    col_a = jnp.concatenate([jnp.ones((D_RNN,), f32), jnp.full((D_RNN,), BETA, f32), jnp.ones((D_MEM,), f32)])
    u = jax.random.uniform(next(keys), (N_A_LAYERS, D_RNN), f32, 0.9, 0.999)
    s = u ** (1.0 / LRU_C)
    lru_lambda = jnp.log(s) - jnp.log1p(-s)
    dm = D_MODEL ** -0.5
    return {
        'x_prompt': nrm((BATCH, SEQ, D_MODEL), 1.0),
        'x_sample': nrm((DEC_BATCH, DEC_SEQ, D_MODEL), 1.0),
        'mem_prompt': nrm((BATCH, N_MEM_TOK, D_MODEL), 1.0),
        'cache_cmp_kv': nrm((n_pool, PAGE_SIZE, 2, N_KV_GROUPS, HEAD_DIM), 1.0),
        'cache_slc_kv': nrm((n_pool, PAGE_SIZE, 2, N_KV_GROUPS, HEAD_DIM), 1.0),
        'cache_win_kv': nrm((DEC_BATCH, w_buf, 2, N_KV_GROUPS, HEAD_DIM), 1.0),
        'cache_mem_kv': nrm((DEPTH, DEC_BATCH, N_MEM_TOK, 2, N_MEM_HEADS, HEAD_DIM), 1.0),
        'state_lru_h': nrm((N_A_LAYERS, DEC_BATCH, D_RNN), 0.5),
        'state_conv': nrm((N_A_LAYERS, DEC_BATCH, CONV_W - 1, D_RNN), 1.0),
        'page_table': page_table,
        'w_in_a': nrm((N_A_LAYERS, D_MODEL, D_IN_A), dm) * col_a,
        'conv_w': nrm((N_A_LAYERS, CONV_W, D_RNN), CONV_W ** -0.5),
        'conv_b': nrm((N_A_LAYERS, D_RNN), 0.01),
        'w_rg': nrm((N_A_LAYERS, N_LRU_BLOCKS, LRU_BLOCK, LRU_BLOCK), LRU_BLOCK ** -0.5),
        'b_rg': nrm((N_A_LAYERS, D_RNN), 0.01),
        'w_ig': nrm((N_A_LAYERS, N_LRU_BLOCKS, LRU_BLOCK, LRU_BLOCK), LRU_BLOCK ** -0.5),
        'b_ig': nrm((N_A_LAYERS, D_RNN), 0.01),
        'lru_lambda': lru_lambda,
        'w_in_b': nrm((N_B_LAYERS, D_MODEL, D_IN_B), dm),
        'w_kv_shared': (nrm((D_MODEL, 3, 2, N_KV_GROUPS * HEAD_DIM), dm) * kv_scale[None, None, :, None]).reshape(D_MODEL, D_KV_SHARED),
        'cmp_pe': nrm((2, CMP_LEN, HEAD_DIM), 0.1),
        'cmp_w1': nrm((2, CMP_LEN * HEAD_DIM, CMP_HID), (CMP_LEN * HEAD_DIM) ** -0.5),
        'cmp_b1': nrm((2, CMP_HID), 0.01),
        'cmp_w2': nrm((2, CMP_HID, HEAD_DIM), CMP_HID ** -0.5),
        'rel_bias': nrm((N_BUCKETS, N_HEADS), 0.5),
        'w_mem_kv': (nrm((DEPTH, D_MODEL, 2, D_MEM), dm) * kv_scale[:, None]).reshape(DEPTH, D_MODEL, 2 * D_MEM),
        'w_out': nrm((DEPTH, D_MODEL, D_MODEL), dm * BETA),
        'ln1_g': 1.0 + nrm((DEPTH, D_MODEL), 0.02),
        'ln1_b': nrm((DEPTH, D_MODEL), 0.02),
        'ln2_g': 1.0 + nrm((DEPTH, D_MODEL), 0.02),
        'ln2_b': nrm((DEPTH, D_MODEL), 0.02),
        'w_router_g': nrm((DEPTH, D_MODEL, N_GROUPS), dm),
        'b_router_g': nrm((DEPTH, N_GROUPS), 0.01),
        'w_router_e': nrm((DEPTH, D_MODEL, N_EXPERTS), dm),
        'b_router_e': nrm((DEPTH, N_EXPERTS), 0.01),
        'w_exp_gate': nrm((DEPTH, N_EXPERTS, D_MODEL, D_EXPERT), dm),
        'w_exp_up': nrm((DEPTH, N_EXPERTS, D_MODEL, D_EXPERT), dm),
        'w_exp_down': nrm((DEPTH, N_EXPERTS, D_EXPERT, D_MODEL), D_EXPERT ** -0.5 * BETA),
    }

def reference(x_prompt, x_sample, mem_prompt, cache_cmp_kv, cache_slc_kv, cache_win_kv, cache_mem_kv,
              state_lru_h, state_conv, page_table, w_in_a, conv_w, conv_b, w_rg, b_rg, w_ig, b_ig, lru_lambda,
              w_in_b, w_kv_shared, cmp_pe, cmp_w1, cmp_b1, cmp_w2, rel_bias, w_mem_kv, w_out,
              ln1_g, ln1_b, ln2_g, ln2_b, w_router_g, b_router_g, w_router_e, b_router_e,
              w_exp_gate, w_exp_up, w_exp_down):
    bp, t_len, _ = x_prompt.shape
    p_mem_kv = jnp.einsum('bmd,lde->lbme', mem_prompt, w_mem_kv).reshape(
        DEPTH, bp, mem_prompt.shape[1], 2, N_MEM_HEADS, HEAD_DIM)
    x = x_prompt
    lru_p, conv_p = [], []
    for l in range(DEPTH):
        mk, mv = p_mem_kv[l, :, :, 0], p_mem_kv[l, :, :, 1]
        if l < N_A_LAYERS:
            sub, h_t, buf = mixer_a(x, w_in_a[l], conv_w[l], conv_b[l], w_rg[l], b_rg[l], w_ig[l], b_ig[l],
                                    lru_lambda[l], jnp.zeros((bp, CONV_W - 1, D_RNN), x.dtype),
                                    jnp.zeros((bp, D_RNN), jnp.float32), mk, mv, w_out[l])
            lru_p.append(h_t.astype(x_prompt.dtype))
            conv_p.append(buf)
        else:
            if l == N_A_LAYERS:
                p_cmp_kv, p_slc_kv, p_win_rows = shared_kv(x, w_kv_shared)
                nsa_p = functools.partial(
                    nsa_prompt,
                    comp_k=compress(p_cmp_kv[:, :, 0], cmp_pe[0], cmp_w1[0], cmp_b1[0], cmp_w2[0]),
                    comp_v=compress(p_cmp_kv[:, :, 1], cmp_pe[1], cmp_w1[1], cmp_b1[1], cmp_w2[1]),
                    ks_g=to_sel_blocks(p_slc_kv[:, :, 0]), vs_g=to_sel_blocks(p_slc_kv[:, :, 1]),
                    kw_pad=jnp.pad(p_win_rows, ((0, 0), (WINDOW, 0), (0, 0), (0, 0), (0, 0))), tab=rel_bias)
            sub = mixer_b(x, w_in_b[l - N_A_LAYERS], nsa_p, mk, mv, w_out[l])
        x = post_norm(x, sub, ln1_g[l], ln1_b[l])
        x = post_norm(x, hmoe(x, w_router_g[l], b_router_g[l], w_router_e[l], b_router_e[l],
                              w_exp_gate[l], w_exp_up[l], w_exp_down[l]), ln2_g[l], ln2_b[l])
    y_prompt = x
    p_win_kv = p_win_rows[:, t_len - min(WINDOW, t_len):]
    p_lru_h = jnp.stack(lru_p)
    p_conv = jnp.stack(conv_p)

    bd, s_len, _ = x_sample.shape
    past = page_table.shape[1] * cache_cmp_kv.shape[1]
    w_buf = cache_win_kv.shape[1]
    q_pos = past + jnp.arange(s_len)
    x = x_sample
    lru_s, conv_s = [], []
    for l in range(DEPTH):
        mk, mv = cache_mem_kv[l, :, :, 0], cache_mem_kv[l, :, :, 1]
        if l < N_A_LAYERS:
            sub, h_t, buf = mixer_a(x, w_in_a[l], conv_w[l], conv_b[l], w_rg[l], b_rg[l], w_ig[l], b_ig[l],
                                    lru_lambda[l], state_conv[l], state_lru_h[l], mk, mv, w_out[l])
            lru_s.append(h_t.astype(state_lru_h.dtype))
            conv_s.append(buf)
        else:
            if l == N_A_LAYERS:
                s_cmp_kv, s_slc_kv, s_win_rows = shared_kv(x, w_kv_shared)
                cmp_all = jnp.concatenate([gather_pages(cache_cmp_kv, page_table), s_cmp_kv.astype(cache_cmp_kv.dtype)], axis=1)
                slc_all = jnp.concatenate([gather_pages(cache_slc_kv, page_table), s_slc_kv.astype(cache_slc_kv.dtype)], axis=1)
                kw_all = jnp.concatenate([cache_win_kv, s_win_rows.astype(cache_win_kv.dtype)], axis=1)
                nsa_s = functools.partial(
                    nsa_decode, q_pos=q_pos,
                    comp_k=compress(cmp_all[:, :, 0], cmp_pe[0], cmp_w1[0], cmp_b1[0], cmp_w2[0]),
                    comp_v=compress(cmp_all[:, :, 1], cmp_pe[1], cmp_w1[1], cmp_b1[1], cmp_w2[1]),
                    ks_g=to_sel_blocks(slc_all[:, :, 0]), vs_g=to_sel_blocks(slc_all[:, :, 1]),
                    kw=kw_all, kw_pos=past - w_buf + jnp.arange(w_buf + s_len), tab=rel_bias)
            sub = mixer_b(x, w_in_b[l - N_A_LAYERS], nsa_s, mk, mv, w_out[l])
        x = post_norm(x, sub, ln1_g[l], ln1_b[l])
        x = post_norm(x, hmoe(x, w_router_g[l], b_router_g[l], w_router_e[l], b_router_e[l],
                              w_exp_gate[l], w_exp_up[l], w_exp_down[l]), ln2_g[l], ln2_b[l])
    y_sample = x
    s_win_kv = kw_all[:, kw_all.shape[1] - w_buf:]
    s_lru_h = jnp.stack(lru_s)
    s_conv = jnp.stack(conv_s)
    return (y_prompt, y_sample, p_cmp_kv, p_slc_kv, p_win_kv, p_mem_kv, p_lru_h, p_conv,
            s_cmp_kv, s_slc_kv, s_win_kv, s_lru_h, s_conv)


_drawn_inputs = setup_inputs


def setup_inputs(seed=0):
    import zlib

    import numpy as np

    out = dict(_drawn_inputs(seed))
    spreads = {}
    factors = {'cache_cmp_kv': 4.784,
     'cache_slc_kv': 5.792,
     'b_rg': 21.796,
     'b_ig': 8.0,
     'cmp_pe': 5.21,
     'cmp_b1': 8.0,
     'rel_bias': 5.321,
     'b_router_g': 6.285,
     'b_router_e': 7.967}
    for name, (base, spread) in spreads.items():
        noise = np.random.default_rng([zlib.crc32(name.encode()), seed]).standard_normal(out[name].shape)
        drawn = base * np.exp(spread * noise) if base else spread * noise
        out[name] = __import__('jax').numpy.asarray(drawn.astype(out[name].dtype))
    for name, factor in factors.items():
        out[name] = (out[name] * factor).astype(out[name].dtype)
    return out
```

```python
import math
from contextlib import ExitStack

import numpy as np

import concourse.bass as bass
from concourse import mybir

F32 = mybir.dt.float32
I32 = mybir.dt.int32
ALU = mybir.AluOpType
ACT = mybir.ActivationFunctionType
AX = mybir.AxisListType

P = 128
D = 1024
KT = D // P
T = 512
B = 8
TOK = T + B
HALF = TOK // 2
QT = T // P
RT = 104
NRT = TOK // RT
HD = 64
GRP = 4
HPG = 3
NH = GRP * HPG
RNN = 6
PAGES = 16
NPOOL = 160
NC = 127
NCP = 31
PAST = 2048
NSB = 33
NSEL = 16
EXPERTS = 32
EGRP = 4
EPG = 8
MEM = 256
ALPHA = 4 ** 0.25
SCALE = 0.125
NEG = -1e30
EPS = 1e-5
RING = 6
ROWS = B * NH
MROWS = B * 4

C_MEM, C_INA, C_OUT0, C_MOE0 = 0, 8, 22, 30
C_KV = C_MOE0 + 3 * EXPERTS
C_INB = C_KV + 12
C_OUT1 = C_INB + 9
C_MOE1 = C_OUT1 + 8
NCH = C_MOE1 + 3 * EXPERTS
PK = {}
_n = 0
for _name, _w in [("ln1g", 16), ("ln1b", 16), ("ln2g", 16), ("ln2b", 16), ("cb", 6), ("cw", 24), ("brg", 6),
                  ("big", 6), ("lam", 6), ("b1", 2), ("pe", 32), ("valid", 1), ("h0", 48), ("st", 144)]:
    PK[_name] = (_n, _n + _w)
    _n += _w
NPK = _n
ROWC = 2 * NSB + EGRP + EPG
U_OUT = [22, 22 + 8 + 64 + 21]


def chunk_plan():
    plan, lin = [], 0
    for c0, c1, layer in ((0, C_MOE0, 0), (C_KV, C_MOE1, 1)):
        for _ in range(c0, c1):
            plan.append(("lin", lin))
            lin += 1
        for e in range(EXPERTS):
            plan += [("lin", lin), ("lin", lin + 1)]
            lin += 2
            if e:
                plan.append(("down", EXPERTS * layer + e - 1))
        plan.append(("down", EXPERTS * layer + EXPERTS - 1))
    return plan


PLAN = chunk_plan()
U_MOE = [PLAN[C_MOE0][1], PLAN[C_MOE1][1]]


def attention_jobs():
    jobs = [(0, qt, "mem", h) for qt in range(QT) for h in range(4)]
    for qt in range(QT):
        for h in range(NH):
            jobs += [(1, qt, br, h) for br in ("cmp", "slc", "win")]
        jobs += [(1, qt, "mem", h) for h in range(4)]
    return jobs


JOBS = attention_jobs()
L_JOBS = [range(0, 16), range(16, len(JOBS))]



def bcast(ap, at, n):
    dims = [list(x) for x in ap.ap]
    dims.insert(at + 1, [0, n])
    return bass.AP(tensor=ap.tensor, offset=ap.offset, ap=dims)


def dram_rows(ap, n):
    return bass.AP(tensor=ap.tensor, offset=ap.offset, ap=[[0, n]] + [list(x) for x in ap.ap][1:])


def build(nc, dr):
    ctx = ExitStack()
    with ctx:
        def sb(name, shape, dt=F32):
            return ctx.enter_context(nc.sbuf_tensor("sb_" + name, shape, dt))

        def sem(name):
            return ctx.enter_context(nc.semaphore(name))

        ring = sb("ring", [P, RING, D])
        X = sb("X", [P, KT, TOK])
        R = sb("R", [P, KT, TOK])
        MIX = sb("MIX", [P, KT, TOK])
        compK = sb("compK", [P, B, 2, P])
        compV = sb("compV", [P, B, 256])
        memK = sb("memK", [P, 2, 2, MEM])
        memV = sb("memV", [P, 2, 2, 256])
        bias96 = sb("bias96", [ROWS, PAST + 8])
        pk = sb("pk", [P, NPK])
        rowc = sb("rowc", [P, ROWC])
        ident = sb("ident", [P, P])
        onesD = sb("onesD", [P, P])
        wr = sb("wr", [P, 2, KT, 36])
        rb = sb("rb", [P, 2, 36])
        tabx = sb("tabx", [33, NH])
        tab96 = sb("tab96", [32, ROWS])
        cover = sb("cover", [P, NSB])
        w2s = sb("w2s", [P, 2, 64])
        pages = sb("pages", [1, P], I32)
        b1e = sb("b1e", [P, 2])
        st = sb("st", [P, 64])
        jst = sb("jst", [P, 4, 8])
        sp8 = sb("sp8", [P, 6, 6])
        xtail = sb("xtail", [P, RNN, 3 + B])
        AR = 23988
        arena = sb("arena", [P, AR])
        PS = ctx.enter_context(nc.psum_tensor("PS", [P, 8, 512], F32))

        def ar(off, *dims):
            n = int(np.prod(dims))
            assert off + n <= AR, (off, dims)
            v = arena[:, off:off + n]
            if len(dims) == 1:
                return v
            names = "abcde"[:len(dims)]
            pat = f"p ({' '.join(names)}) -> p {' '.join(names)}"
            return v.rearrange(pat, **{names[i]: dims[i] for i in range(1, len(dims))})

        def pcol(name, i, n=1):
            a = PK[name][0] + i
            return pk[:, a:a + n]

        Rf = R[:, :, :].rearrange("p a b -> p (a b)")
        Mf = MIX[:, :, :].rearrange("p a b -> p (a b)")
        memT = Mf[:, 0:2048].rearrange("p (k t) -> p k t", k=KT)
        w1p = ar(0, 2, 16, P)
        ccb = [ar(4096 + 8192 * i, PAGES, 8, 64) for i in range(2)]
        p2 = [Mf[:, 512 * i:512 * i + 512] for i in range(2)]
        hsb = [Mf[:, 1024 + 512 * i:1536 + 512 * i] for i in range(2)]
        ohp, ohc, ohd = Rf[0:33, 0:640], Rf[0:33, 640:1632], Rf[0:32, 1632:1632 + PAST + 8]
        rrow = Mf[0:NH, 2100:2740]
        cmpB = ar(22500, QT, NCP, NH)
        gateT = ar(0, RNN, TOK)
        xrT = ar(3120, RNN, TOK)
        rT = ar(6240, RNN, TOK)
        iT = ar(9360, RNN, TOK)
        xcT = ar(12480, RNN, TOK)
        mq0 = ar(15600, 2, TOK)
        wbd = Rf[:, 0:1536].rearrange("p (w t j) -> p w t j", w=2, t=RNN)
        qT = ar(0, 6, TOK)
        mq1 = ar(3120, 2, TOK)
        KT_ = {"slc": ar(4160, 2, TOK), "win": ar(5200, 2, TOK)}
        VT_ = {"slc": ar(6240, 5, 256), "win": ar(7520, 5, 256)}
        kcT = ar(8800, 2, NCP)
        vcp = ar(8864, 256)
        gates = ar(9120, 5, 36)
        g96 = ar(9300, 3)
        w1h = ar(10800, 2, 32, P)
        cmpT = ar(18992, 2, 2, TOK)
        hgp = ar(21072, 2, 2, 2 * NCP)
        QZ = ar(10800, 1632)
        kvb1 = ar(12976, 4096)
        L96 = ar(17072, PAST + 8)
        Lw = ar(19128, T + 8)
        Lc = ar(19648, P)
        SEL = ar(19776, 5, 36)
        PTd = ar(20040, 25, ROWS)
        cube = ar(20040, NSB, NSB)
        tri = ar(21129, NSB, NSB)
        S3 = ar(22344, ROWS)
        vrow_parts = [(0, 0, B, Mf[0:1, 0:2048]), (1, 0, 6, Mf[0:1, 2048:3584]), (1, 6, B, Mf[0:1, 3640:4152])]

        def vrow(i, b, pair):
            for part, b0, b1, v in vrow_parts:
                if part == i and b0 <= b < b1:
                    a = (b - b0) * 256 + pair * P
                    return v[:, a:a + P]
        TH = ar(10800, NH, T)
        Sb = [ar(16944 + 512 * i, T) for i in range(2)]
        Pb = [ar(17968 + 512 * i, T) for i in range(2)]
        PTb = [ar(18992 + 512 * i, T) for i in range(2)]
        mixTM = [ar(20016 + 1024 * i, D) for i in range(2)]
        QZM = [ar(20272, 544), ar(12432, 544)]
        LM = [ar(21296, MEM), ar(17072, MEM)]
        PTM = [ar(21552, 2, MROWS), ar(17328, 2, MROWS)]
        sg = [ar(520 * i, TOK) for i in range(2)]
        hid = [ar(1040 + 520 * i, TOK) for i in range(2)]
        cb = [ar(2080 + 520 * i, TOK) for i in range(2)]
        LG = ar(3120, NRT, 36)
        M1 = ar(3300, NRT, EGRP, EPG)
        M2 = ar(3460, NRT, EGRP, EPG)
        OG = ar(3620, NRT, EGRP)
        TG = ar(3640, NRT, EGRP)
        LE = ar(3660, NRT, EPG)
        O1 = ar(3700, NRT, EPG)
        O2 = ar(3740, NRT, EPG)
        T8 = ar(3780, NRT, EPG)
        SC = ar(3820, 12, NRT)
        combT = ar(3900, TOK)
        rs = ar(4440, TOK)

        CONSTS = [(X[:], dr["xT"]), (memT, dr["memT"]), (pk[:], dr["pk"]), (rowc[:], dram_rows(dr["rowc"], P)),
                  (ident[:], dr["ident"]), (wr[:], dr["wr"]), (rb[:], dram_rows(dr["rb"], P)),
                  (tabx[0:32, :], dr["tab"]), (tab96[:], dr["tab96"]), (cover[0:NC, :], dr["cover"]),
                  (w2s[:], dr["w2s"]), (ohp, dr["ohp"]), (ohc, dr["ohc"]), (ohd, dr["ohd"])]

        const_in = sem("const_in")
        pages_in = sem("pages_in")
        w1_in = sem("w1_in")
        rd_stored = sem("rd_stored")
        memset_done = sem("memset_done")
        w_land = [sem(f"w_land{i}") for i in range(RING)]
        w_used = sem("w_used")
        lin_act = sem("lin_act")
        lin_dve = sem("lin_dve")
        tab_ready = sem("tab_ready")
        tab_moved = sem("tab_moved")
        cc_land = [sem("cc_land0"), sem("cc_land1")]
        cmp_ab = sem("cmp_ab")
        p2_done = sem("p2_done")
        hs_done = sem("hs_done")
        hg_done = sem("hg_done")
        cmp_w2 = sem("cmp_w2")
        cmp_out = sem("cmp_out")
        lam_exp = sem("lam_exp")
        lam_abs = sem("lam_abs")
        conv_done = sem("conv_done")
        gmm_done = sem("gmm_done")
        gate_sig = sem("gate_sig")
        la_done = sem("la_done")
        at_done = sem("at_done")
        u2_done = sem("u2_done")
        sq_done = sem("sq_done")
        lru_done = sem("lru_done")
        bd_in = sem("bd_in")
        s_done = sem("s_done")
        max_done = sem("max_done")
        exp_done = sem("exp_done")
        pt_ready = sem("pt_ready")
        pt_done = sem("pt_done")
        v_done = sem("v_done")
        o_done = sem("o_done")
        mt_ready = sem("mt_ready")
        mt_done = sem("mt_done")
        kv_land = [sem("kv_land0"), sem("kv_land1")]
        kv_used = sem("kv_used")
        qz_done = sem("qz_done")
        dm_max, dm_exp, dm_p = sem("dm_max"), sem("dm_exp"), sem("dm_probs")
        dm_t, dm_pt, dm_out = sem("dm_turned"), sem("dm_moved"), sem("dm_out")
        dc_s, dc_max, dc_exp, dc_p = sem("dc_scores"), sem("dc_max"), sem("dc_exp"), sem("dc_probs")
        dc_t, dc_sum, dc_imp = sem("dc_turned"), sem("dc_headsum"), sem("dc_importance")
        ds_s, ds_max, ds_exp, ds_p = sem("ds_scores"), sem("ds_max"), sem("ds_exp"), sem("ds_probs")
        ds_t, ds_pt, ds_o, ds_out = sem("ds_turned"), sem("ds_moved"), sem("ds_values"), sem("ds_out")
        mu_ready = sem("mu_ready")
        xm_ready = sem("xm_ready")
        sqr_ready = sem("sqr_ready")
        var_ready = sem("var_ready")
        ve_ready = sem("ve_ready")
        std_ready = sem("std_ready")
        nrm_ready = sem("nrm_ready")
        x_ready = sem("x_ready")
        lg_ready = sem("lg_ready")
        rmax_ready = sem("rmax_ready")
        rexp_ready = sem("rexp_ready")
        cmb_ready = sem("cmb_ready")
        cmbt_ready = sem("cmbt_ready")
        cmbs_ready = sem("cmbs_ready")
        comb_stored = sem("comb_stored")
        cb_land = [sem("cb_land0"), sem("cb_land1")]
        sg_done = sem("sg_done")
        sgc_done = sem("sgc_done")
        hid_done = sem("hid_done")
        dn_done = sem("dn_done")
        acc_done = sem("acc_done")
        w1h_in = sem("w1h_in")
        cp_h = sem("cp_h")
        cp_g = sem("cp_g")
        cp_o = sem("cp_o")
        cp_done = sem("cp_done")
        g_stored = sem("g_stored")
        g96_in = sem("g96_in")
        vrow_in = sem("vrow_in")
        th_in = sem("th_in")
        tri_in = sem("tri_in")
        stores = sem("stores")
        dve_chain = sem("dve_chain")

        def at_least(eng, s, v):
            if not (isinstance(v, int) and v <= 0):
                eng.wait_ge(s, v)

        lin_order = [c for c in range(NCH) if c < C_MOE0 or C_KV <= c < C_MOE1]
        lin_index = {c: i for i, c in enumerate(lin_order)}
        lin_engine = ["dve" if C_OUT0 <= c < C_MOE0 or C_OUT1 <= c < C_MOE1 else "act" for c in lin_order]

        def lin_moved(eng, i):
            at_least(eng, lin_act, lin_engine[:max(i, 0)].count("act"))
            at_least(eng, lin_dve, lin_engine[:max(i, 0)].count("dve"))

        def lin_bank(c):
            return 2 * (lin_index[c] % 2)

        both = [(0, HALF), (HALF, HALF)]
        tiles5 = [(i * P, P) for i in range(QT)] + [(T, B)]

        def halves(ap):
            return ap.rearrange("p (h t) -> p h t", h=2)

        FILLS = ([("mem", 0)] * 4 + [("mem", 1)] * 4 + [("slck", b) for b in range(B)] +
                 [("wink", 0), ("wink", 4), ("winv", 0), ("winv", 4)] + [("slcv", b) for b in range(B)])
        F_SLCK, F_WINK, F_WINV, F_SLCV = 8, 16, 18, 20

        def fill_landed(eng, f):
            eng.wait_ge(kv_land[f % 2], sum(256 if FILLS[g][0][:3] == "slc" else 16 for g in range(f % 2, f + 1, 2)))

        mem_half = [Rf[:, 2048 * i:2048 * i + 2048].rearrange("p (b x) -> p b x", b=4) for i in range(2)]
        kv_bufs = [Rf[:, 0:4096], kvb1]

        def job_tiles(j):
            layer, qt, br, h = JOBS[j]
            return {"cmp": 1, "mem": 2}.get(br, qt + 1)

        def job_nk(j):
            layer, qt, br, h = JOBS[j]
            return {"cmp": NCP, "mem": MEM}.get(br, (qt + 1) * P)

        def job_place(j):
            layer, qt, br, h = JOBS[j]
            qs = slice(qt * P, qt * P + P)
            if br == "mem":
                r0, pair = 64 * (h % 2), h // 2
                return (mq0, mq1)[layer][r0:r0 + 64, pair, qs], memK[r0:r0 + 64, layer, pair, :]
            g, hh = divmod(h, HPG)
            r0, pair = 64 * (g % 2), g // 2
            q = qT[r0:r0 + 64, pair * HPG + hh, qs]
            if br == "cmp":
                return q, kcT[r0:r0 + 64, pair, :]
            return q, KT_[br][r0:r0 + 64, pair, 0:job_nk(j)]

        def job_value(j, kt):
            layer, qt, br, h = JOBS[j]
            g = h // HPG
            if br == "mem":
                return memV[:, layer, kt, h * 64:h * 64 + 64]
            if br == "cmp":
                return vcp[0:NCP, g * 64:g * 64 + 64]
            return VT_[br][:, kt, g * 64:g * 64 + 64]

        def job_column(j):
            layer, qt, br, h = JOBS[j]
            if br == "mem":
                return (0 if layer == 0 else 768) + h * 64
            g, hh = divmod(h, HPG)
            return ((g // 2) * HPG + hh) * P + 64 * (g % 2)

        def last_job(layer, qt):
            return max(j for j in L_JOBS[layer] if JOBS[j][1] == qt)

        LASTS = {last_job(layer, qt): (layer, qt) for layer in range(2) for qt in range(QT)}

        block = ctx.enter_context(nc.Block())

        @block.sync
        def _(sp):
            sp.dma_start(pages[:], dr["pages"]).then_inc(pages_in, 16)

            def slot_free(c):
                if c >= RING:
                    kind, n = PLAN[c - RING]
                    sp.wait_ge(w_used, n + 1) if kind == "lin" else sp.wait_ge(acc_done, KT * (n + 1))

            def load_chunk(c):
                slot_free(c)
                sp.dma_start(ring[:, c % RING, :], dr["wstream"][c]).then_inc(w_land[c % RING], 16)

            def fill_pages(buf, landed, pool, b):
                for j in range(PAGES):
                    pg = sp.value_load(pages[0:1, bass.ds(b * PAGES + j, 1)], min_val=0, max_val=NPOOL - 1)
                    sp.dma_start(buf[:, j], pool[bass.ds(pg, 1)].rearrange("o p j -> (o p) j")).then_inc(landed, 16)

            ccf = [v.rearrange("p a b c -> p a (b c)") for v in ccb]
            for c in range(RING):
                load_chunk(c)
            sp.wait_ge(pages_in, 16)
            for b in range(2):
                fill_pages(ccf[b], cc_land[b], dr["cc"], b)
            load_chunk(6)
            load_chunk(7)
            with sp.Fori(0, 3) as i:
                for u in range(2):
                    sp.wait_ge(cmp_ab, i * 4 + 2 * u + 2)
                    fill_pages(ccf[u], cc_land[u], dr["cc"], i * 2 + 2 + u)
            for c in range(C_INA, C_OUT0):
                load_chunk(c)

            def mem_fills(layer):
                for n, (kind, b0) in enumerate((("k", 0), ("k", 4), ("v", 0), ("v", 4))):
                    f = 4 * layer + n
                    at_least(sp, kv_used, f - 1)
                    sp.dma_start(mem_half[f % 2], dr["mem" + kind][layer, b0:b0 + 4].rearrange("b p x -> p b x")
                                 ).then_inc(kv_land[f % 2], 16)

            sp.wait_ge(gmm_done, 12)
            mem_fills(0)
            for c in range(C_OUT0, C_MOE0):
                load_chunk(c)

            def comb(layer, e, parity):
                at_least(sp, hid_done, e + EXPERTS * layer - 1)
                row = dr["combd"][layer][bass.ds(e, 1), :]
                sp.dma_start(cb[parity], dram_rows(row, P)).then_inc(cb_land[parity], 16)

            def moe_loads(layer, c0):
                u0, a0 = U_MOE[layer], KT * EXPERTS * layer
                load_chunk(c0)
                load_chunk(c0 + 1)
                if layer == 0:
                    sp.wait_ge(lin_dve, KT)
                    sp.dma_start(w1h, dr["w1h"]).then_inc(w1h_in, 16)
                sp.wait_ge(comb_stored, 16 * (layer + 1))
                comb(layer, 0, 0)
                for u in range(6):
                    load_chunk(c0 + 2 + u)
                    if u % 3 == 1:
                        comb(layer, 1 + u // 3, (1 + u // 3) % 2)
                with sp.Fori(1, 15) as i:
                    for u in range(6):
                        if u % 3 == 2:
                            sp.wait_ge(acc_done, i * 16 + a0 + (-8 if u == 2 else 0))
                        else:
                            sp.wait_ge(w_used, i * 4 + u0 + {0: -1, 1: 0, 3: 1, 4: 2}[u])
                        c = c0 + 2 + u
                        sp.dma_start(ring[:, c % RING, :],
                                     dr["wstream"][bass.ds(i * 6 + c, 1)].rearrange("o p j -> (o p) j")
                                     ).then_inc(w_land[c % RING], 16)
                        if u % 3 == 1:
                            comb(layer, i * 2 + 1 + u // 3, (1 + u // 3) % 2)
                for c in range(c0 + 92, c0 + 96):
                    load_chunk(c)
                    if c == c0 + 93:
                        comb(layer, 31, 1)

            moe_loads(0, C_MOE0)
            for c in range(C_KV, C_OUT1):
                load_chunk(c)
            sp.wait_ge(x_ready, 2 * KT)
            mem_fills(1)
            sp.wait_ge(cp_done, 2)
            for f in range(8, len(FILLS)):
                kind, b0 = FILLS[f]
                buf, landed = kv_bufs[f % 2], kv_land[f % 2]
                sp.wait_ge(kv_used, max(f - 1, 8))
                if kind[:3] == "slc":
                    fill_pages(buf.rearrange("p (j x) -> p j x", j=PAGES), landed, dr[kind], b0)
                else:
                    sp.dma_start(buf.rearrange("p (b x) -> p b x", b=4),
                                 dr[kind][b0:b0 + 4].rearrange("b p x -> p b x")).then_inc(landed, 16)
            sp.wait_ge(ds_out, 1)
            sp.wait_ge(rd_stored, 32)
            rows = dr["rd_rows"]
            sp.dma_start(TH, bass.AP(tensor=rows.tensor, offset=rows.offset + 127,
                                     ap=[[NH * 640 - 1, P], [640, NH], [1, T]])).then_inc(th_in, 16)
            for c in range(C_OUT1, C_MOE1):
                load_chunk(c)
            moe_loads(1, C_MOE1)

        @block.gpsimd
        def _(pool):
            pool.dma_start(dr["o_winold"], dr["winnat"][:, 1:, :]).then_inc(stores, 16)
            pool.wait_ge(tab_moved, 1)
            pool.dma_start(dr["rd"], rrow).then_inc(rd_stored, 16)
            pool.wait_ge(rd_stored, 16)
            pool.dma_start(dr["rd_rows"], dram_rows(dr["rd"].rearrange("(o h) m -> o (h m)", o=1), P)
                           ).then_inc(rd_stored, 16)
            lin_moved(pool, 8)
            pool.dma_start(dr["o_memk"], memK[:]).then_inc(stores, 16)
            pool.dma_start(dr["o_memv"], memV[:]).then_inc(stores, 16)
            pool.wait_ge(const_in, 16 * len(CONSTS))
            pool.dma_start(dr["o_st"], pcol("st", 0, 144)).then_inc(stores, 16)
            pool.wait_ge(tab_ready, 4)
            pool.dma_start(wbd, dr["wbd"]).then_inc(bd_in, 16)
            pool.wait_ge(conv_done, RNN)
            pool.dma_start(dr["o_xr"], xtail[:]).then_inc(stores, 16)
            pool.wait_ge(lru_done, 1)
            pool.dma_start(dr["o_h"], rT[:, :, T - 1:TOK]).then_inc(stores, 16)
            lin_moved(pool, lin_index[C_KV] + 12)
            pool.dma_start(dr["o_cmp"], cmpT).then_inc(stores, 16)
            for i, br in enumerate(("slc", "win")):
                pool.dma_start(dr["o_k"][i], KT_[br]).then_inc(stores, 16)
                pool.dma_start(dr["o_v"][i], VT_[br][:, 0:QT, :]).then_inc(stores, 16)
                pool.dma_start(dr["o_vd"][i], VT_[br][0:B, QT, :]).then_inc(stores, 16)
            pool.wait_ge(stores, 16 * 13)
            pool.wait_ge(cp_done, 2)
            for i, b0, b1, v in vrow_parts:
                pool.dma_start(v, dr["o_vd"][i, b0:b1].rearrange("(o b) c -> o (b c)", o=1)).then_inc(vrow_in, 16)
            pool.dma_start(tri[0:ROWS], dram_rows(dr["tri"], ROWS)).then_inc(tri_in, 16)
            pool.wait_ge(x_ready, 4 * KT)
            pool.dma_start(dr["o_y"], X[:]).then_inc(stores, 16)
            pool.wait_ge(stores, 16 * 14)

        @block.tensor
        def _(pe):
            def fm_unit(c, src, widths):
                lin_moved(pe, lin_index[c] - 1)
                pe.wait_ge(w_land[c % RING], 16 * (c // RING + 1))
                bank = lin_bank(c)
                for k in range(KT):
                    for hf, (a, n) in enumerate(widths):
                        mm = pe.matmul(PS[:, bank + hf, 0:n], ring[:, c % RING, k * P:k * P + P],
                                       src[:, k, a:a + n], start=(k == 0), stop=(k == KT - 1))
                mm.then_inc(w_used, 1)

            def tm_unit(c, src, tiles, cols):
                lin_moved(pe, lin_index[c] - 1)
                pe.wait_ge(w_land[c % RING], 16 * (c // RING + 1))
                bank = lin_bank(c)
                for t, (a, n) in enumerate(tiles):
                    o = PS[0:n, bank, t * P:t * P + cols] if t < 4 else PS[0:n, bank + 1, 0:cols]
                    for k in range(KT):
                        mm = pe.matmul(o, src[:, k, a:a + n], ring[:, c % RING, k * P:k * P + cols],
                                       start=(k == 0), stop=(k == KT - 1))
                mm.then_inc(w_used, 1)

            pe.wait_ge(const_in, 16 * len(CONSTS))
            pe.wait_ge(memset_done, 2)
            for c in range(8):
                if c % 4 < 2:
                    fm_unit(c, memT, [(0, MEM)])
                else:
                    tm_unit(c, memT, [(0, P), (P, P)], P)
            for i, (a, n) in enumerate(((0, 512), (512, 128))):
                mm = pe.matmul(PS[0:NH, 4 + i, 0:n], tabx[:], ohp[:, a:a + n], start=True, stop=True)
            mm.then_inc(tab_ready, 1)
            mm = pe.matmul(PS[0:ROWS, 6, 0:1], tab96[:], ohd[:, PAST:PAST + 1], start=True, stop=True)
            mm.then_inc(tab_ready, 1)
            lin_moved(pe, 8)
            for i in range(4):
                mm = pe.matmul(PS[0:ROWS, i, :], tab96[:], ohd[:, i * 512:i * 512 + 512], start=True, stop=True)
            mm.then_inc(tab_ready, 1)
            pe.wait_ge(tab_moved, 3)
            for qt in range(QT):
                for c in range(NCP):
                    a = qt * P - 16 * c - 31 + 511
                    mm = pe.matmul(PS[:, qt, c * NH:c * NH + NH], ohc[:, a:a + P], tabx[:], start=True, stop=True)
            mm.then_inc(tab_ready, 1)
            pe.wait_ge(w1_in, 16)
            for kv in range(2):
                for s in range(16):
                    mm = pe.matmul(PS[:, 5, kv:kv + 1], w1p[:, kv, s, :], pcol("pe", kv * 16 + s),
                                   start=(s == 0), stop=(s == 15))
            mm.then_inc(tab_ready, 1)
            pe.wait_ge(tab_moved, 4)

            def comp_ab(um, u, landed):
                kv = um % 2
                if kv == 0:
                    pe.wait_ge(cc_land[um // 2], landed)
                at_least(pe, hs_done, u - 1)
                v = ccb[um // 2][:, :, kv * 4:kv * 4 + 4, :].rearrange("p a g (c s) -> p g a c s", s=8)
                for h in range(2):
                    for s in range(8):
                        mm = pe.matmul(PS[:, 2 * kv + h, :], w1p[:, kv, 8 * h + s, :], v[:, :, :, :, s],
                                       start=(s == 0), stop=(s == 7))
                mm.then_inc(cmp_ab, 1)

            def comp_w2(um, u):
                kv = um % 2
                pe.wait_ge(hg_done, u + 1)
                at_least(pe, cmp_out, u - 1)
                hg = hsb[kv].rearrange("p (g c) -> p g c", g=4)
                for g in range(4):
                    if kv == 0:
                        r0 = 64 * (g % 2)
                        mm = pe.matmul(PS[r0:r0 + 64, 6, (g // 2) * P:(g // 2) * P + NC], w2s[:, 0, :],
                                       hg[:, g, 0:NC], start=True, stop=True)
                    else:
                        mm = pe.matmul(PS[0:NC, 7, g * 64:g * 64 + 64], hg[:, g, 0:NC], w2s[:, 1, :],
                                       start=True, stop=True)
                mm.then_inc(cmp_w2, 1)

            comp_ab(0, 0, 256)
            for um in range(4):
                comp_ab((um + 1) % 4, um + 1, 512 if um == 3 else 256)
                comp_w2(um, um)
            with pe.Fori(1, 3) as i:
                for um in range(4):
                    comp_ab((um + 1) % 4, i * 4 + (um + 1), i * 256 + (512 if um == 3 else 256))
                    comp_w2(um, i * 4 + um)
            for um in range(4):
                if um < 3:
                    comp_ab(um + 1, 13 + um, 1024)
                comp_w2(um, 12 + um)

            for c in range(C_INA, C_OUT0):
                fm_unit(c, X, both)
            pe.wait_ge(bd_in, 16)
            pe.wait_ge(cmp_out, 16)
            for n in range(12):
                pe.wait_ge(conv_done, n % 6 + 1)
                at_least(pe, gate_sig, n - 1)
                for hf, (a, m) in enumerate(both):
                    mm = pe.matmul(PS[:, 4 + 2 * (n % 2) + hf, 0:m], wbd[:, n // 6, n % 6, :],
                                   xcT[:, n % 6, a:a + m], start=True, stop=True)
                mm.then_inc(gmm_done, 1)

            def sample_mem(layer):
                f = 4 * layer
                pe.wait_ge(qz_done, 1 + layer)
                for b in range(B):
                    if b % 4 == 0:
                        fill_landed(pe, f + b // 4)
                    for pair in range(2):
                        mm = pe.matmul(PS[0:MROWS, 7, 0:MEM],
                                       QZM[layer][:, b * 64 + pair * 32:b * 64 + pair * 32 + 32],
                                       mem_half[b // 4][:, b % 4, pair * MEM:pair * MEM + MEM],
                                       start=(b == 0 and pair == 0), stop=(b == 7 and pair == 1))
                    if b % 4 == 3:
                        mm.then_inc(kv_used, 1)
                pe.wait_ge(dm_p, 1 + layer)
                for kt in range(2):
                    mm = pe.matmul(PS[:, 7, MEM + 32 * kt:MEM + 32 * kt + 32], LM[layer][0:MROWS, kt * P:kt * P + P],
                                   ident[0:MROWS, 0:MROWS], start=True, stop=True)
                mm.then_inc(dm_t, 1)
                pe.wait_ge(dm_pt, 1 + layer)
                for b in range(B):
                    if b % 4 == 0:
                        fill_landed(pe, f + 2 + b // 4)
                    for kt in range(2):
                        for pair in range(2):
                            n = b * 4 + pair * 2
                            mm = pe.matmul(PS[:, 6, n:n + 2],
                                           mem_half[b // 4][:, b % 4, kt * 256 + pair * P:kt * 256 + pair * P + P],
                                           PTM[layer][:, kt, n:n + 2], start=(n == 0 and kt == 0),
                                           stop=(b == 7 and kt == 1), skip_group_check=True)
                    if b % 4 == 3:
                        mm.then_inc(kv_used, 1)

            def job_s(j):
                at_least(pe, exp_done, j - 1)
                q, k = job_place(j)
                pe.matmul(PS[:, j % 2, 0:job_nk(j)], q, k, start=True, stop=True).then_inc(s_done, 1)

            def job_t(j):
                pe.wait_ge(exp_done, j + 1)
                at_least(pe, pt_done, j - 1)
                for kt in range(job_tiles(j)):
                    n = min(P, job_nk(j) - kt * P)
                    mm = pe.transpose(PS[0:n, 2 + j % 2, kt * P:kt * P + P], Pb[j % 2][:, kt * P:kt * P + n], ident[:])
                mm.then_inc(pt_ready, 1)

            def job_v(j):
                pe.wait_ge(pt_done, j + 1)
                at_least(pe, o_done, j - 1)
                last = job_tiles(j) - 1
                for kt in range(last + 1):
                    n = min(P, job_nk(j) - kt * P)
                    mm = pe.matmul(PS[:, 4 + j % 2, 0:64], PTb[j % 2][0:n, kt * P:kt * P + P], job_value(j, kt),
                                   start=(kt == 0), stop=(kt == last))
                mm.then_inc(v_done, 1)

            def mix_t(layer, qt):
                pe.wait_ge(o_done, last_job(layer, qt) + 1)
                at_least(pe, mt_done, QT * layer + qt)
                for t in range(2 if layer == 0 else KT):
                    mm = pe.transpose(PS[:, 6 + t // 4, (t % 4) * P:(t % 4) * P + P],
                                      mixTM[qt % 2][:, t * P:t * P + P], ident[:])
                mm.then_inc(mt_ready, 1)

            def prompt_attention(layer):
                js = L_JOBS[layer]
                for j in range(js.start, js.stop + 4):
                    if j in js:
                        job_s(j)
                    if j - 1 in js:
                        job_t(j - 1)
                    if j - 2 in js:
                        job_v(j - 2)
                    if j - 4 in js and j - 4 in LASTS:
                        mix_t(*LASTS[j - 4])

            def norm(n):
                pe.wait_ge(*((acc_done, KT * EXPERTS * (n // 2 + 1)) if n % 2 else (lin_dve, KT * (n // 2 + 1))))
                for hf, (a, m) in enumerate(both):
                    for k in range(KT):
                        mm = pe.matmul(PS[:, 4 + hf, 0:m], onesD[:], R[:, k, a:a + m], start=(k == 0), stop=(k == 7))
                    mm.then_inc(mu_ready, 1)
                for hf, (a, m) in enumerate(both):
                    pe.wait_ge(sqr_ready, 2 * n + hf + 1)
                    for k in range(KT):
                        mm = pe.matmul(PS[:, 6 + hf, 0:m], onesD[:], MIX[:, k, a:a + m], start=(k == 0), stop=(k == 7))
                    mm.then_inc(var_ready, 1)

            def gate_up(c, landed, ge):
                at_least(pe, hid_done, ge)
                for part in range(2):
                    slot = (c + part) % RING
                    pe.wait_ge(w_land[slot], landed[part])
                    for k in range(KT):
                        for hf, (a, m) in enumerate(both):
                            mm = pe.matmul(PS[:, 2 * part + hf, 0:m], ring[:, slot, k * P:k * P + P],
                                           X[:, k, a:a + m], start=(k == 0), stop=(k == KT - 1))
                    mm.then_inc(w_used, 1)

            def down(c, landed, parity, ge):
                slot = c % RING
                pe.wait_ge(w_land[slot], landed)
                pe.wait_ge(hid_done, ge + 1)
                for m in range(KT):
                    at_least(pe, acc_done, ge * KT + m - 1)
                    for hf, (a, w) in enumerate(both):
                        mm = pe.matmul(PS[:, 4 + 2 * (m % 2) + hf, 0:w], ring[:, slot, m * P:m * P + P],
                                       hid[parity][:, a:a + w], start=True, stop=True)
                    mm.then_inc(dn_done, 1)

            def moe(layer, c0):
                g0 = EXPERTS * layer
                at = lambda c: 16 * (c // RING + 1)
                pe.wait_ge(x_ready, KT * (2 * layer + 1))
                for rt in range(NRT):
                    for k in range(KT):
                        mm = pe.matmul(PS[0:RT, 4, rt * 36:rt * 36 + 36], X[:, k, rt * RT:rt * RT + RT],
                                       wr[:, layer, k, :], start=(k == 0), stop=(k == KT - 1))
                mm.then_inc(lg_ready, 1)
                gate_up(c0, [at(c0), at(c0 + 1)], g0)
                pe.wait_ge(cmb_ready, layer + 1)
                for rt in range(NRT):
                    o = PS[0:32, 5, rt * RT:rt * RT + RT] if rt < 4 else PS[0:32, 6, 0:RT]
                    mm = pe.transpose(o, M2[0:RT, rt].rearrange("p a b -> p (a b)"), ident[0:RT, 0:RT])
                mm.then_inc(cmbt_ready, 1)
                pe.wait_ge(cmbs_ready, layer + 1)

                def step(i, s, gi):
                    c = c0 + 2 + 3 * s
                    gate_up(c, [i * 16 + at(c), i * 16 + at(c + 1)], gi + 1 + s)
                    down(c + 2, i * 16 + at(c + 2), s, gi + s)

                for s in range(2):
                    step(0, s, g0)
                with pe.Fori(1, 15) as i:
                    for s in range(2):
                        step(i, s, i * 2 + g0)
                step(15, 0, g0 + 30)
                down(c0 + 95, at(c0 + 95), 1, g0 + 31)

            pe.wait_ge(gate_sig, 12)
            sample_mem(0)
            pe.wait_ge(dm_out, 1)
            prompt_attention(0)
            pe.wait_ge(mt_done, QT)
            pe.wait_ge(lru_done, 1)
            for c in range(C_OUT0, C_MOE0):
                fm_unit(c, MIX, both)
            norm(0)
            moe(0, C_MOE0)
            norm(1)

            pe.wait_ge(x_ready, 2 * KT)
            for n in range(12):
                if n in (6, 7, 10, 11):
                    tm_unit(C_KV + n, X, tiles5, P)
                else:
                    fm_unit(C_KV + n, X, both)
            for n in range(8):
                fm_unit(C_INB + n, X, both)
            tm_unit(C_INB + 8, X, tiles5, 36)
            pe.wait_ge(w1h_in, 16)
            lin_moved(pe, lin_index[C_KV] + 4)
            for kv in range(2):
                for g2 in range(2):
                    r0 = 64 * g2
                    for pos in range(32):
                        blocks = cmpT[r0:r0 + 64, kv, :, pos:pos + 16 * (NCP - 1) + 1:16]
                        mm = pe.matmul(PS[:, 4 + 2 * kv + g2, 0:2 * NCP], w1h[r0:r0 + 64, kv, pos, :],
                                       blocks, start=(pos == 0), stop=(pos == 31))
                mm.then_inc(cp_h, 1)
            pe.wait_ge(cp_g, 1)
            for g2 in range(2):
                mm = pe.matmul(PS[64 * g2:64 * g2 + 64, 4, P:P + 2 * NCP], w2s[:, 0, :], hgp[:, 0, g2, :],
                               start=True, stop=True)
            mm.then_inc(cp_o, 1)
            pe.wait_ge(cp_g, 2)
            for g in range(GRP):
                mm = pe.matmul(PS[0:NCP, 5, P + g * 64:P + g * 64 + 64],
                               hgp[:, 1, g % 2, (g // 2) * NCP:(g // 2) * NCP + NCP], w2s[:, 1, :],
                               start=True, stop=True)
            mm.then_inc(cp_o, 1)

            pe.wait_ge(cp_done, 2)
            sample_mem(1)
            pe.wait_ge(dm_out, 2)

            def qz(b, pair):
                return QZ[:, b * 192 + pair * 96:b * 192 + pair * 96 + ROWS]

            first, last = (0, 0), (B - 1, 1)
            for b in range(B):
                for pair in range(2):
                    mm = pe.matmul(PS[0:ROWS, 6, 0:NC], qz(b, pair), compK[:, b, pair, 0:NC],
                                   start=(b, pair) == first, stop=(b, pair) == last)
            mm.then_inc(dc_s, 1)
            for i, br in enumerate(("slc", "win")):
                for b in range(B):
                    for pair in range(2):
                        mm = pe.matmul(PS[0:ROWS, 5, i:i + 1], qz(b, pair), KT_[br][:, pair, T + b:T + b + 1],
                                       start=(b, pair) == first, stop=(b, pair) == last)
            for b in range(B):
                fill_landed(pe, F_SLCK + b)
                v = kv_bufs[(F_SLCK + b) % 2].rearrange("p (j a k) -> p j a k", j=PAGES, a=2)
                for pair in range(2):
                    for q4 in range(4):
                        mm = pe.matmul(PS[0:ROWS, q4, :], qz(b, pair), v[:, 4 * q4:4 * q4 + 4, pair, :],
                                       start=(b, pair) == first, stop=(b, pair) == last)
                mm.then_inc(kv_used, 1)
                if b == 1:
                    pe.wait_ge(dc_p, 1)
                    pe.transpose(PS[0:NC, 6, P:P + ROWS], Lc[0:ROWS, 0:NC], ident[0:ROWS, 0:ROWS]).then_inc(dc_t, 1)
                    pe.wait_ge(dc_sum, 1)
                    pe.matmul(PS[0:ROWS, 7, 0:NSB], S3[0:NC], cover[0:NC, :], start=True, stop=True
                              ).then_inc(dc_imp, 1)
            for b in range(B):
                if b % 4 == 0:
                    fill_landed(pe, F_WINK + b // 4)
                v = kv_bufs[(F_WINK + b // 4) % 2].rearrange("p (b j a k) -> p b j a k", b=4, j=4, a=2)[:, b % 4]
                for pair in range(2):
                    mm = pe.matmul(PS[0:ROWS, 4, :], qz(b, pair), v[:, :, pair, :],
                                   start=(b, pair) == first, stop=(b, pair) == last)
                if b % 4 == 3:
                    mm.then_inc(kv_used, 1)
            turns = ([(L96, P * t, P) for t in range(16)] + [(Lw, P * t, P) for t in range(4)] +
                     [(Lc, 0, NC), (L96, PAST, 1), (Lw, T, 1)])
            for t, (src, a, n) in enumerate(turns):
                if t == 0:
                    pe.wait_ge(ds_p, 1)
                if t == 16:
                    pe.wait_ge(ds_p, 2)
                mm = pe.transpose(PS[0:n, t // 5, (t % 5) * ROWS:(t % 5) * ROWS + ROWS], src[0:ROWS, a:a + n],
                                  ident[0:ROWS, 0:ROWS])
            mm.then_inc(ds_t, 1)
            pe.wait_ge(ds_pt, 1)

            def values(lhsT, tile, rows, b, pair, start=False, stop=False):
                n = b * 12 + pair * 6
                return pe.matmul(PS[:, 5, n:n + 6], lhsT, PTd[0:rows, tile, n:n + 6], start=start, stop=stop,
                                 skip_group_check=True)

            for b in range(B):
                for pair in range(2):
                    values(compV[0:NC, b, pair * P:pair * P + P], 20, NC, b, pair, start=(b, pair) == first)
            pe.wait_ge(vrow_in, 48)
            for i in range(2):
                for b in range(B):
                    for pair in range(2):
                        values(vrow(i, b, pair), 21 + i, 1, b, pair)
            for b in range(B):
                if b % 4 == 0:
                    fill_landed(pe, F_WINV + b // 4)
                v = kv_bufs[(F_WINV + b // 4) % 2].rearrange("p (b j x) -> p b j x", b=4, j=4)[:, b % 4]
                for t in range(4):
                    for pair in range(2):
                        mm = values(v[:, t, pair * P:pair * P + P], 16 + t, P, b, pair)
                if b % 4 == 3:
                    mm.then_inc(kv_used, 1)
            for b in range(B):
                fill_landed(pe, F_SLCV + b)
                v = kv_bufs[(F_SLCV + b) % 2].rearrange("p (j x) -> p j x", j=PAGES)
                for t in range(PAGES):
                    for pair in range(2):
                        mm = values(v[:, t, pair * P:pair * P + P], t, P, b, pair,
                                    stop=(b == B - 1 and t == PAGES - 1))
                mm.then_inc(kv_used, 1)

            prompt_attention(1)
            pe.wait_ge(mt_done, 2 * QT)
            pe.wait_ge(ds_out, 1)
            for c in range(C_OUT1, C_MOE1):
                fm_unit(c, MIX, both)
            norm(2)
            moe(1, C_MOE1)
            norm(3)

        @block.scalar
        def _(act):
            for dst, src in CONSTS:
                act.dma_start(dst, src).then_inc(const_in, 16)
            act.dma_start(w1p, dr["w1p"]).then_inc(w1_in, 16)

            def unit_ready(c):
                act.wait_ge(w_used, PLAN[c][1] + 1)
                return lin_bank(c)

            def move(out, in_, scale=1.0):
                return act.activation(out, in_, ACT.Copy, scale=scale)

            for c in range(8):
                bank = unit_ready(c)
                layer, kv, pair = c // 4, (c // 2) % 2, c % 2
                if kv == 0:
                    move(memK[:, layer, pair, :], PS[:, bank, 0:MEM]).then_inc(lin_act, 1)
                else:
                    move(memV[:, layer, :, pair * P:pair * P + P],
                         PS[:, bank, 0:MEM].rearrange("p (t x) -> p t x", t=2)).then_inc(lin_act, 1)
            act.wait_ge(lam_abs, 1)
            act.activation(sp8[:, 1, :], sp8[:, 0, :], ACT.Exp, scale=-1.0).then_inc(lam_exp, 1)

            def comp_p2(kv, u):
                act.wait_ge(cmp_ab, u + 1)
                at_least(act, hs_done, u - 1)
                act.activation(p2[kv], PS[:, 2 * kv + 1, :], ACT.Identity, bias=b1e[:, kv:kv + 1]).then_inc(p2_done, 1)

            def comp_gelu(kv, u):
                act.wait_ge(hs_done, u + 1)
                h = hsb[kv].rearrange("p (g c) -> p g c", g=4)[:, :, 0:NC]
                act.activation(h, h, ACT.Gelu_apprx_tanh).then_inc(hg_done, 1)

            act.wait_ge(tab_moved, 5)
            comp_p2(0, 0)
            with act.Fori(0, 7) as i:
                for um in range(2):
                    act.wait_ge(cmp_ab, i * 2 + um + 2)
                    act.wait_ge(hs_done, i * 2 + um)
                    kv = (um + 1) % 2
                    act.activation(p2[kv], PS[:, 2 * kv + 1, :], ACT.Identity, bias=b1e[:, kv:kv + 1]
                                   ).then_inc(p2_done, 1)
                    comp_gelu(um, i * 2 + um)
            comp_p2(1, 15)
            comp_gelu(0, 14)
            comp_gelu(1, 15)

            act.wait_ge(cmp_out, 16)
            for c in range(C_INA, C_OUT0):
                bank = unit_ready(c)
                src = PS[:, bank:bank + 2, 0:HALF]
                n = c - C_INA
                if n < 6:
                    act.activation(halves(gateT[:, n, :]), src, ACT.Gelu_apprx_tanh).then_inc(lin_act, 1)
                elif n < 12:
                    move(halves(xrT[:, n - 6, :]), src).then_inc(lin_act, 1)
                else:
                    move(halves(mq0[:, n - 12, :]), src, SCALE).then_inc(lin_act, 1)
            for n in range(12):
                act.wait_ge(gmm_done, n + 1)
                b0 = 4 + 2 * (n % 2)
                act.activation(halves((rT, iT)[n // 6][:, n % 6, :]), PS[:, b0:b0 + 2, 0:HALF], ACT.Sigmoid,
                               bias=pcol("brg" if n < 6 else "big", n % 6)).then_inc(gate_sig, 1)
            for t in range(RNN):
                act.wait_ge(la_done, t + 1)
                act.activation(xrT[:, t, :], rT[:, t, :], ACT.Exp)
                act.activation(rT[:, t, :], rT[:, t, :], ACT.Tanh).then_inc(at_done, 1)
            for t in range(RNN):
                act.wait_ge(u2_done, t + 1)
                act.activation(MIX[:, t, :], MIX[:, t, :], ACT.Sqrt, scale=-1.0).then_inc(sq_done, 1)

            def sample_mem(layer):
                act.wait_ge(dm_max, 1 + layer)
                act.activation(LM[layer][0:MROWS], PS[0:MROWS, 7, 0:MEM], ACT.Exp, bias=st[0:MROWS, 0:1],
                               accum_out=st[0:MROWS, 1:2]).then_inc(dm_exp, 1)

            def job_exp(j):
                act.wait_ge(max_done, j + 1)
                at_least(act, pt_ready, j - 1)
                nk = job_nk(j)
                src = PS[:, j % 2, 0:nk] if JOBS[j][2] == "mem" else Sb[j % 2][:, 0:nk]
                act.activation(Pb[j % 2][:, 0:nk], src, ACT.Exp, bias=jst[:, j % 4, 1:2],
                               accum_out=jst[:, j % 4, 2:3]).then_inc(exp_done, 1)

            def job_pt(j):
                act.wait_ge(pt_ready, j + 1)
                at_least(act, v_done, j - 1)
                n, w = min(P, job_nk(j)), P * job_tiles(j)
                move(PTb[j % 2][0:n, 0:w], PS[0:n, 2 + j % 2, 0:w]).then_inc(pt_done, 1)

            def mix_move(layer, qt):
                act.wait_ge(mt_ready, QT * layer + qt + 1)
                qs = slice(qt * P, qt * P + P)
                if layer == 0:
                    move(MIX[:, 6:8, qs], PS[:, 6, 0:MEM].rearrange("p (t x) -> p t x", t=2)).then_inc(mt_done, 1)
                else:
                    for i in range(2):
                        mv = move(MIX[:, 4 * i:4 * i + 4, qs], PS[:, 6 + i, :].rearrange("p (t x) -> p t x", t=4))
                    mv.then_inc(mt_done, 1)

            def prompt_attention(layer):
                js = L_JOBS[layer]
                for j in range(js.start, js.stop + 4):
                    if j in js:
                        job_exp(j)
                    if j - 1 in js:
                        job_pt(j - 1)
                    if j - 4 in js and j - 4 in LASTS:
                        mix_move(*LASTS[j - 4])

            def norm(n):
                for hf, (a, m) in enumerate(both):
                    act.wait_ge(xm_ready, 2 * n + hf + 1)
                    act.activation(MIX[:, :, a:a + m], R[:, :, a:a + m], ACT.Square).then_inc(sqr_ready, 1)
                for hf, (a, m) in enumerate(both):
                    act.wait_ge(ve_ready, 2 * n + hf + 1)
                    act.activation(rs[:, a:a + m], rs[:, a:a + m], ACT.Sqrt).then_inc(std_ready, 1)
                act.wait_ge(nrm_ready, 2 * n + 2)
                g, b = ("ln2g", "ln2b") if n % 2 else ("ln1g", "ln1b")
                for k in range(KT):
                    act.activation(X[:, k, :], R[:, k, :], ACT.Identity, bias=pcol(b, 8 * (n // 2) + k),
                                   scale=pcol(g, 8 * (n // 2) + k)).then_inc(x_ready, 1)

            def silu(parity, gates_used, ge):
                act.wait_ge(w_used, gates_used)
                at_least(act, hid_done, ge - 1)
                act.activation(halves(sg[parity]), PS[:, 0:2, 0:HALF], ACT.Silu).then_inc(sg_done, 1)

            def moe(layer):
                u0, g0 = U_MOE[layer], EXPERTS * layer
                act.wait_ge(rmax_ready, 1 + layer)
                act.activation(TG[0:RT], TG[0:RT], ACT.Exp)
                act.activation(SC[0:RT, 4, :], SC[0:RT, 3, :], ACT.Exp).then_inc(rexp_ready, 1)
                silu(0, u0 + 2, g0)
                act.wait_ge(cmbs_ready, 1 + layer)
                act.dma_start(dr["combd"][layer], combT[0:EXPERTS]).then_inc(comb_stored, 16)
                silu(1, u0 + 4, g0 + 1)
                with act.Fori(1, 16) as i:
                    for s in range(2):
                        silu(s, i * 4 + u0 + 2 * s + 2, i * 2 + g0 + s)

            sample_mem(0)
            prompt_attention(0)
            norm(0)
            moe(0)
            norm(1)

            for n in range(12):
                bank = unit_ready(C_KV + n)
                br, kv, pair = n // 4, (n // 2) % 2, n % 2
                src = PS[:, bank:bank + 2, 0:HALF]
                if br == 0:
                    move(halves(cmpT[:, kv, pair, :]), src).then_inc(lin_act, 1)
                elif kv == 0:
                    move(halves(KT_[("", "slc", "win")[br]][:, pair, :]), src).then_inc(lin_act, 1)
                else:
                    v = VT_[("", "slc", "win")[br]]
                    move(v[:, 0:QT, pair * P:pair * P + P], PS[:, bank, :].rearrange("p (t x) -> p t x", t=QT))
                    move(v[0:B, QT, pair * P:pair * P + P], PS[0:B, bank + 1, 0:P]).then_inc(lin_act, 1)
            for n in range(8):
                bank = unit_ready(C_INB + n)
                dst = qT[:, n, :] if n < 6 else mq1[:, n - 6, :]
                move(halves(dst), PS[:, bank:bank + 2, 0:HALF], SCALE).then_inc(lin_act, 1)
            bank = unit_ready(C_INB + 8)
            act.activation(gates[:, 0:QT, :], PS[:, bank, :].rearrange("p (t x) -> p t x", t=QT)[:, :, 0:36],
                           ACT.Sigmoid)
            act.activation(gates[0:B, QT, :], PS[0:B, bank + 1, 0:36], ACT.Sigmoid).then_inc(lin_act, 1)
            lin_moved(act, lin_index[C_INB + 8] + 1)
            act.dma_start(dr["gd"], gates[0:B, QT, :]).then_inc(g_stored, 16)
            for kv in range(2):
                act.wait_ge(cp_h, kv + 1)
                act.activation(hgp[:, kv], PS[:, 4 + 2 * kv:6 + 2 * kv, 0:2 * NCP],
                               ACT.Gelu_apprx_tanh, bias=b1e[:, kv:kv + 1]).then_inc(cp_g, 1)
            act.wait_ge(g_stored, 16)
            act.dma_start(g96[0:ROWS], dr["gd"].rearrange("b (h x) -> (b h) x", x=3)).then_inc(g96_in, 16)
            sample_mem(1)
            act.wait_ge(dc_max, 1)
            act.activation(Lc[0:ROWS, 0:NC], Lc[0:ROWS, 0:NC], ACT.Exp, bias=st[0:ROWS, 4:5],
                           accum_out=st[0:ROWS, 5:6]).then_inc(dc_exp, 1)
            act.wait_ge(ds_max, 1)
            act.activation(L96[0:ROWS, 0:PAST + 1], L96[0:ROWS, 0:PAST + 1], ACT.Exp, bias=st[0:ROWS, 8:9],
                           accum_out=st[0:ROWS, 9:10]).then_inc(ds_exp, 1)
            act.wait_ge(ds_max, 2)
            act.activation(Lw[0:ROWS, 0:T + 1], Lw[0:ROWS, 0:T + 1], ACT.Exp, bias=st[0:ROWS, 12:13],
                           accum_out=st[0:ROWS, 13:14]).then_inc(ds_exp, 1)
            prompt_attention(1)
            norm(2)
            moe(1)
            norm(3)

        @block.vector
        def _(dve):
            chain = [0]

            def link(ins):
                chain[0] += 1
                ins.then_inc(dve_chain, 1)
                dve.wait_ge(dve_chain, chain[0])

            dve.memset(onesD[:], 1.0 / D).then_inc(memset_done, 1)
            dve.memset(tabx[32:33, :], NEG).then_inc(memset_done, 1)
            dve.wait_ge(const_in, 16 * len(CONSTS))
            lam = pcol("lam", 0, 6)
            s = [sp8[:, i, :] for i in range(6)]
            link(dve.tensor_scalar(s[2], lam, -1.0, None, ALU.mult))
            dve.tensor_tensor(s[0], lam, s[2], ALU.max).then_inc(lam_abs, 1)
            dve.wait_ge(tab_ready, 1)
            dve.tensor_copy(rrow[:, 0:512], PS[0:NH, 4, 0:512])
            dve.tensor_copy(rrow[:, 512:640], PS[0:NH, 5, 0:128]).then_inc(tab_moved, 1)
            dve.wait_ge(tab_ready, 2)
            dve.tensor_copy(bias96[:, PAST:PAST + 1], PS[0:ROWS, 6, 0:1]).then_inc(tab_moved, 1)
            dve.wait_ge(tab_ready, 3)
            dve.tensor_copy(bias96[:, 0:PAST].rearrange("p (a b) -> p a b", a=4), PS[0:ROWS, 0:4, :]
                            ).then_inc(tab_moved, 1)
            dve.wait_ge(tab_ready, 4)
            dve.tensor_copy(cmpB.rearrange("p a b c -> p a (b c)"), PS[:, 0:4, 0:NCP * NH]).then_inc(tab_moved, 1)
            dve.wait_ge(tab_ready, 5)
            dve.tensor_tensor(b1e[:], PS[:, 5, 0:2], pcol("b1", 0, 2), ALU.add).then_inc(tab_moved, 1)

            dve.wait_ge(lam_exp, 1)
            link(dve.tensor_scalar(s[3], s[1], 2.0, None, ALU.add))
            link(dve.reciprocal(s[4], s[3]))
            link(dve.tensor_tensor(s[3], s[1], s[4], ALU.mult))
            link(dve.tensor_tensor(s[4], s[3], s[3], ALU.mult))
            link(dve.tensor_scalar(s[5], s[4], 1.0 / 17, None, ALU.mult))
            for k in range(7, 0, -1):
                link(dve.scalar_tensor_tensor(out=s[5], in0=s[5], scalar=1.0 / (2 * k + 1), in1=s[4],
                                              op0=ALU.add, op1=ALU.mult))
            link(dve.scalar_tensor_tensor(out=s[5], in0=s[5], scalar=1.0, in1=s[3], op0=ALU.add, op1=ALU.mult))
            link(dve.tensor_scalar(s[2], s[2], 0.0, None, ALU.max))
            link(dve.scalar_tensor_tensor(out=s[5], in0=s[5], scalar=2.0, in1=s[2], op0=ALU.mult, op1=ALU.add))
            link(dve.tensor_scalar(s[5], s[5], -8.0, None, ALU.mult))

            def comp_hs(kv, u):
                dve.wait_ge(p2_done, u + 1)
                at_least(dve, cmp_w2, u - 1)
                a = PS[:, 2 * kv, :].rearrange("p (g c) -> p g c", g=4)
                b = p2[kv].rearrange("p (g c) -> p g c", g=4)
                h = hsb[kv].rearrange("p (g c) -> p g c", g=4)
                dve.tensor_tensor(h[:, :, 0:NC], a[:, :, 0:NC], b[:, :, 1:NC + 1], ALU.add).then_inc(hs_done, 1)

            def comp_out(kv, u, b):
                dve.wait_ge(cmp_w2, u + 1)
                if kv == 0:
                    dve.tensor_copy(compK[:, bass.ds(b, 1), :, 0:NC].rearrange("p o a c -> p (o a) c"),
                                    PS[:, 6, 0:2 * P].rearrange("p (a c) -> p a c", a=2)[:, :, 0:NC]
                                    ).then_inc(cmp_out, 1)
                else:
                    dve.tensor_copy(compV[0:NC, bass.ds(b, 1), :].rearrange("p o x -> p (o x)"),
                                    PS[0:NC, 7, 0:256]).then_inc(cmp_out, 1)

            comp_hs(0, 0)
            comp_hs(1, 1)
            comp_out(0, 0, 0)
            with dve.Fori(1, 8) as i:
                comp_hs(0, i * 2)
                comp_out(1, i * 2 - 1, i - 1)
                comp_hs(1, i * 2 + 1)
                comp_out(0, i * 2, i)
            comp_out(1, 15, 7)

            for t in range(RNN):
                lin_moved(dve, lin_index[C_INA] + 7 + t)
                w = [pcol("cw", k * 6 + t) for k in range(4)]
                sx = pcol("st", t * 24, 24).rearrange("p (k b) -> p k b", k=3)
                link(dve.tensor_scalar(xcT[:, t, :], xrT[:, t, :], w[3], pcol("cb", t), ALU.mult, ALU.add))
                dve.tensor_copy(xtail[:, t, :], xrT[:, t, T - 3:TOK])
                for k in range(3):
                    d = 3 - k
                    dve.scalar_tensor_tensor(out=xcT[:, t, T:TOK], in0=sx[:, k, :], scalar=w[k],
                                             in1=xcT[:, t, T:TOK], op0=ALU.mult, op1=ALU.add).then_inc(dve_chain, 1)
                    chain[0] += 1
                    link(dve.scalar_tensor_tensor(out=xcT[:, t, d:T], in0=xrT[:, t, 0:T - d], scalar=w[k],
                                                  in1=xcT[:, t, d:T], op0=ALU.mult, op1=ALU.add)) if k < 2 else \
                        dve.scalar_tensor_tensor(out=xcT[:, t, d:T], in0=xrT[:, t, 0:T - d], scalar=w[k],
                                                 in1=xcT[:, t, d:T], op0=ALU.mult, op1=ALU.add).then_inc(conv_done, 1)

            def sample_queries(layer):
                z, q = QZM[layer], (mq0, mq1)[layer]
                link(dve.memset(z, 0.0))
                for h2 in range(2):
                    r0 = 64 * h2
                    for pair in range(2):
                        v = z[r0:r0 + 64].rearrange("p (b x) -> p b x", x=68)
                        ins = dve.tensor_copy(v[:, :, pair * 34 + h2:pair * 34 + h2 + 1],
                                              q[r0:r0 + 64, pair, T:TOK].rearrange("p (b o) -> p b o", o=1))
                return ins

            def sample_mem(layer):
                L = LM[layer][0:MROWS]
                dve.wait_ge(kv_used, 4 * layer + 2)
                dve.tensor_reduce(st[0:MROWS, 0:1], PS[0:MROWS, 7, 0:MEM], AX.X, ALU.max, negate=True
                                  ).then_inc(dm_max, 1)
                dve.wait_ge(dm_exp, 1 + layer)
                link(dve.reciprocal(st[0:MROWS, 2:3], st[0:MROWS, 1:2]))
                dve.tensor_scalar(L, L, st[0:MROWS, 2:3], None, ALU.mult).then_inc(dm_p, 1)
                dve.wait_ge(dm_t, 1 + layer)
                dve.tensor_copy(PTM[layer], PS[:, 7, MEM:MEM + 64].rearrange("p (t x) -> p t x", t=2)
                                ).then_inc(dm_pt, 1)
                dve.wait_ge(kv_used, 4 * layer + 4)
                for h2 in range(2):
                    r0 = 64 * h2
                    v = PS[r0:r0 + 64, 6, 0:MROWS].rearrange("p (b a x) -> p a b x", a=2, x=2)
                    ins = dve.tensor_copy(MIX[r0:r0 + 64, 6:8, T:TOK], v[:, :, :, h2])
                ins.then_inc(dm_out, 1)

            def job_max(j):
                layer, qt, br, h = JOBS[j]
                dve.wait_ge(s_done, j + 1)
                at_least(dve, exp_done, j - 1)
                nk, sj = job_nk(j), jst[:, j % 4]
                if br == "mem":
                    dve.tensor_reduce(sj[:, 1:2], PS[:, j % 2, 0:nk], AX.X, ALU.max, negate=True).then_inc(max_done, 1)
                    return
                bias = cmpB[:, qt, :, h] if br == "cmp" else TH[:, h, T - nk:T]
                link(dve.tensor_tensor_reduce(out=Sb[j % 2][:, 0:nk], in0=PS[:, j % 2, 0:nk], in1=bias, scale=1.0,
                                              scalar=-3.0e38, op0=ALU.add, op1=ALU.max, accum_out=sj[:, 0:1]))
                dve.tensor_scalar(sj[:, 1:2], sj[:, 0:1], -1.0, None, ALU.mult).then_inc(max_done, 1)

            def job_out(j):
                layer, qt, br, h = JOBS[j]
                dve.wait_ge(v_done, j + 1)
                sj = jst[:, j % 4]
                link(dve.reciprocal(sj[:, 3:4], sj[:, 2:3]))
                coef = sj[:, 3:4]
                if br != "mem":
                    n = 3 * h + ("cmp", "slc", "win").index(br)
                    coef = sj[:, 4:5]
                    if br == "cmp" and qt == 0:
                        link(dve.tensor_scalar(coef, sj[:, 3:4], gates[:, qt, n:n + 1], pcol("valid", 0),
                                               ALU.mult, ALU.mult))
                    else:
                        link(dve.tensor_scalar(coef, sj[:, 3:4], gates[:, qt, n:n + 1], None, ALU.mult))
                if j == L_JOBS[layer].start or j - 1 in LASTS:
                    at_least(dve, mt_ready, QT * layer + qt - 1)
                out = mixTM[qt % 2][:, job_column(j):job_column(j) + 64]
                o = PS[:, 4 + j % 2, 0:64]
                if br in ("mem", "cmp"):
                    dve.tensor_scalar(out, o, coef, None, ALU.mult).then_inc(o_done, 1)
                else:
                    dve.wait_ge(o_done, j)
                    dve.scalar_tensor_tensor(out=out, in0=o, scalar=coef, in1=out, op0=ALU.mult, op1=ALU.add
                                             ).then_inc(o_done, 1)

            def prompt_attention(layer):
                js = L_JOBS[layer]
                for j in range(js.start, js.stop + 2):
                    if j in js:
                        job_max(j)
                    if j - 2 in js:
                        job_out(j - 2)

            def out_units(c0):
                for m in range(KT):
                    dve.wait_ge(w_used, PLAN[c0 + m][1] + 1)
                    bank = lin_bank(c0 + m)
                    dve.scalar_tensor_tensor(out=halves(R[:, m, :]), in0=halves(X[:, m, :]), scalar=ALPHA,
                                             in1=PS[:, bank:bank + 2, 0:HALF], op0=ALU.mult, op1=ALU.add
                                             ).then_inc(lin_dve, 1)

            def norm(n):
                for hf, (a, m) in enumerate(both):
                    dve.wait_ge(mu_ready, 2 * n + hf + 1)
                    dve.tensor_tensor(R[:, :, a:a + m], R[:, :, a:a + m], bcast(PS[:, 4 + hf, 0:m], 0, KT),
                                      ALU.subtract).then_inc(xm_ready, 1)
                for hf, (a, m) in enumerate(both):
                    dve.wait_ge(var_ready, 2 * n + hf + 1)
                    dve.tensor_scalar(rs[:, a:a + m], PS[:, 6 + hf, 0:m], EPS, None, ALU.add).then_inc(ve_ready, 1)
                dve.wait_ge(xm_ready, 2 * n + 2)
                for hf, (a, m) in enumerate(both):
                    dve.wait_ge(std_ready, 2 * n + hf + 1)
                    link(dve.reciprocal(rs[:, a:a + m], rs[:, a:a + m]))
                    dve.tensor_tensor(R[:, :, a:a + m], R[:, :, a:a + m], bcast(rs[:, a:a + m], 0, KT),
                                      ALU.mult).then_inc(nrm_ready, 1)

            def router(layer):
                rampg = bcast(rowc[0:RT, 2 * NSB:2 * NSB + EGRP], 0, NRT)
                ramp8 = bcast(rowc[0:RT, 2 * NSB + EGRP:ROWC], 0, NRT)
                dve.wait_ge(lg_ready, 1 + layer)
                lg = LG[0:RT]
                sc = [SC[0:RT, i, :] for i in range(12)]
                og, tg, le, o1, o2, t8 = OG[0:RT], TG[0:RT], LE[0:RT], O1[0:RT], O2[0:RT], T8[0:RT]
                link(dve.tensor_tensor(lg, PS[0:RT, 4, 0:NRT * 36].rearrange("p (t x) -> p t x", t=NRT),
                                       bcast(rb[0:RT, layer, :], 0, NRT), ALU.add))

                def top(vals, width, ramp, onehot, tmp, mx, mr):
                    link(dve.tensor_reduce(mx, vals, AX.X, ALU.max))
                    link(dve.tensor_tensor(tmp, vals, bcast(mx, 1, width), ALU.is_equal))
                    link(dve.tensor_tensor(tmp, tmp, ramp, ALU.mult))
                    link(dve.tensor_reduce(mr, tmp, AX.X, ALU.max))
                    link(dve.tensor_tensor(onehot, tmp, bcast(mr, 1, width), ALU.is_equal))

                top(lg[:, :, 0:EGRP], EGRP, rampg, og, tg, sc[0], sc[1])
                lex = lg[:, :, EGRP:36].rearrange("p t (g e) -> p t g e", g=EGRP)
                m1 = M1[0:RT]
                link(dve.tensor_tensor(m1, lex, bcast(og, 2, EPG), ALU.mult))
                link(dve.tensor_reduce(le, m1.rearrange("p t g e -> p t e g"), AX.X, ALU.add))
                top(le, EPG, ramp8, o1, t8, sc[2], sc[1])
                link(dve.scalar_tensor_tensor(out=le, in0=o1, scalar=NEG, in1=le, op0=ALU.mult, op1=ALU.add))
                top(le, EPG, ramp8, o2, t8, sc[5], sc[1])
                link(dve.tensor_tensor(sc[3], sc[5], sc[2], ALU.subtract))
                dve.tensor_tensor(tg, lg[:, :, 0:EGRP], bcast(sc[0], 1, EGRP), ALU.subtract).then_inc(rmax_ready, 1)
                dve.wait_ge(rexp_ready, 1 + layer)
                link(dve.tensor_reduce(sc[6], tg, AX.X, ALU.add))
                link(dve.reciprocal(sc[7], sc[6]))
                link(dve.tensor_scalar(sc[8], sc[4], 1.0, None, ALU.add))
                link(dve.reciprocal(sc[9], sc[8]))
                link(dve.tensor_tensor(sc[10], sc[9], sc[7], ALU.mult))
                link(dve.tensor_tensor(sc[11], sc[10], sc[4], ALU.mult))
                link(dve.tensor_tensor(o1, o1, bcast(sc[10], 1, EPG), ALU.mult))
                link(dve.tensor_tensor(o2, o2, bcast(sc[11], 1, EPG), ALU.mult))
                link(dve.tensor_tensor(o1, o1, o2, ALU.add))
                for g in range(EGRP):
                    ins = dve.tensor_tensor(M2[0:RT, :, g, :], o1, bcast(og[:, :, g], 1, EPG), ALU.mult)
                ins.then_inc(cmb_ready, 1)
                dve.tensor_scalar(R[:], X[:], ALPHA, None, ALU.mult).then_inc(dve_chain, 1)
                chain[0] += 1
                dve.wait_ge(cmbt_ready, 1 + layer)
                dve.tensor_copy(combT[0:EXPERTS, 0:4 * RT], PS[0:EXPERTS, 5, 0:4 * RT])
                dve.tensor_copy(combT[0:EXPERTS, 4 * RT:TOK], PS[0:EXPERTS, 6, 0:RT]).then_inc(cmbs_ready, 1)
                dve.wait_ge(dve_chain, chain[0])

            def hidden(parity, ge, landed):
                dve.wait_ge(sg_done, ge + 1)
                dve.wait_ge(cb_land[parity], landed)
                dve.tensor_tensor(sg[parity], sg[parity], cb[parity], ALU.mult).then_inc(sgc_done, 1)
                dve.wait_ge(sgc_done, ge + 1)
                at_least(dve, dn_done, ge * KT - KT)
                dve.tensor_tensor(halves(hid[parity]), halves(sg[parity]), PS[:, 2:4, 0:HALF], ALU.mult
                                  ).then_inc(hid_done, 1)

            def accumulate(ge):
                for m in range(KT):
                    dve.wait_ge(dn_done, ge * KT + m + 1)
                    bank = 4 + 2 * (m % 2)
                    dve.tensor_tensor(halves(R[:, m, :]), halves(R[:, m, :]), PS[:, bank:bank + 2, 0:HALF], ALU.add
                                      ).then_inc(acc_done, 1)

            def moe(layer):
                g0, l0 = EXPERTS * layer, 256 * layer
                hidden(0, g0, l0 + 16)
                hidden(1, g0 + 1, l0 + 16)
                accumulate(g0)
                with dve.Fori(1, 16) as i:
                    hidden(0, i * 2 + g0, i * 16 + l0 + 16)
                    accumulate(i * 2 + g0 - 1)
                    hidden(1, i * 2 + g0 + 1, i * 16 + l0 + 16)
                    accumulate(i * 2 + g0)
                accumulate(g0 + 31)

            lin_moved(dve, lin_index[C_OUT0])
            sample_queries(0).then_inc(qz_done, 1)
            for t in range(RNN):
                dve.wait_ge(gate_sig, t + 1)
                dve.tensor_scalar(rT[:, t, :], rT[:, t, :], sp8[:, 5, t:t + 1], None, ALU.mult).then_inc(la_done, 1)
            for t in range(RNN):
                dve.wait_ge(at_done, t + 1)
                u = MIX[:, t, :]
                link(dve.tensor_tensor(u, xrT[:, t, :], xrT[:, t, :], ALU.mult))
                link(dve.scalar_tensor_tensor(out=u, in0=u, scalar=1.0, in1=rT[:, t, :], op0=ALU.add, op1=ALU.mult))
                dve.tensor_scalar(u, u, -1.0e-34, None, ALU.min).then_inc(u2_done, 1)
            dve.wait_ge(gate_sig, 12)
            for t in range(RNN):
                link(dve.tensor_tensor(iT[:, t, :], iT[:, t, :], xcT[:, t, :], ALU.mult))
                dve.wait_ge(sq_done, t + 1)
                link(dve.tensor_tensor(iT[:, t, :], iT[:, t, :], MIX[:, t, :], ALU.mult))
                h0 = pcol("h0", t * 8, 8)
                link(dve.tensor_tensor_scan(rT[:, t, 0:T], xrT[:, t, 0:T], iT[:, t, 0:T], 0.0, ALU.mult, ALU.add))
                link(dve.tensor_tensor(rT[:, t, T:TOK], xrT[:, t, T:TOK], h0, ALU.mult))
                link(dve.tensor_tensor(rT[:, t, T:TOK], rT[:, t, T:TOK], iT[:, t, T:TOK], ALU.add))
                ins = dve.tensor_tensor(MIX[:, t, :], gateT[:, t, :], rT[:, t, :], ALU.mult)
            ins.then_inc(lru_done, 1)
            sample_mem(0)
            prompt_attention(0)
            out_units(C_OUT0)
            norm(0)
            dve.wait_ge(x_ready, KT)
            dve.wait_ge(stores, 16 * 6)
            router(0)
            moe(0)
            norm(1)

            dve.wait_ge(cp_o, 1)
            dve.tensor_copy(kcT, PS[:, 4, P:P + 2 * NCP].rearrange("p (a c) -> p a c", a=2)).then_inc(cp_done, 1)
            dve.wait_ge(cp_o, 2)
            dve.tensor_copy(vcp[0:NCP], PS[0:NCP, 5, P:P + 256]).then_inc(cp_done, 1)
            lin_moved(dve, lin_index[C_OUT1])
            link(dve.memset(QZ, 0.0))
            for g2 in range(2):
                r0 = 64 * g2
                v = QZ[r0:r0 + 64].rearrange("p (b x) -> p b x", x=204)
                for pair in range(2):
                    a = pair * 102 + g2 * HPG
                    dve.tensor_copy(v[:, :, a:a + HPG],
                                    qT[r0:r0 + 64, pair * HPG:pair * HPG + HPG, T:TOK].rearrange("p h b -> p b h"))
            sample_queries(1).then_inc(qz_done, 1)
            dve.wait_ge(stores, 16 * 13)
            sample_mem(1)
            dve.wait_ge(dc_s, 1)
            r = slice(0, ROWS)
            s1 = lambda i: st[r, i:i + 1]
            link(dve.tensor_tensor(Lc[r, 0:NC], PS[r, 6, 0:NC], bias96[:, 31:31 + 16 * (NC - 1) + 1:16], ALU.add))
            dve.tensor_reduce(s1(4), Lc[r, 0:NC], AX.X, ALU.max, negate=True).then_inc(dc_max, 1)
            dve.wait_ge(dc_exp, 1)
            link(dve.reciprocal(s1(6), s1(5)))
            dve.tensor_scalar(Lc[r, 0:NC], Lc[r, 0:NC], s1(6), None, ALU.mult).then_inc(dc_p, 1)
            dve.wait_ge(dc_t, 1)
            link(dve.tensor_reduce(st[0:NC, 16:48], PS[0:NC, 6, P:P + ROWS].rearrange("p (r h) -> p r h", h=HPG),
                                   AX.X, ALU.add))
            dve.tensor_copy(S3[0:NC].rearrange("p (r h) -> p r h", h=HPG), bcast(st[0:NC, 16:48], 1, HPG)
                            ).then_inc(dc_sum, 1)
            dve.wait_ge(g96_in, 16)
            dve.tensor_scalar(Lc[r, 0:NC], Lc[r, 0:NC], g96[r, 0:1], None, ALU.mult)
            dve.wait_ge(dc_imp, 1)
            dve.wait_ge(tri_in, 16)
            score, sel = SEL[r, 0, 0:NSB], SEL[r, 1, 0:NSB]
            r1, r2 = SEL[r, 2, 0:NSB], SEL[r, 3, 0:NSB]
            link(dve.tensor_tensor(r1, PS[r, 7, 0:NSB], rowc[r, 0:NSB], ALU.mult))
            link(dve.tensor_tensor(score, r1, rowc[r, NSB:2 * NSB], ALU.add))
            link(dve.tensor_tensor(cube[r], bcast(score, 0, NSB), bcast(score, 1, NSB), ALU.is_gt))
            link(dve.tensor_reduce(r1, cube[r], AX.X, ALU.add))
            link(dve.tensor_tensor(cube[r], bcast(score, 0, NSB), bcast(score, 1, NSB), ALU.is_equal))
            link(dve.tensor_tensor(cube[r], cube[r], tri[r], ALU.mult))
            link(dve.tensor_reduce(r2, cube[r], AX.X, ALU.add))
            link(dve.tensor_tensor(r1, r1, r2, ALU.add))
            link(dve.tensor_scalar(sel, r1, float(NSEL), NEG, ALU.is_ge, ALU.mult))
            dve.wait_ge(kv_used, F_SLCK + B)
            link(dve.tensor_tensor(L96[r, 0:PAST].rearrange("p (a b) -> p a b", a=4), PS[r, 0:4, :],
                                   bias96[:, 0:PAST].rearrange("p (a b) -> p a b", a=4), ALU.add))
            link(dve.tensor_tensor(L96[r, 0:PAST].rearrange("p (s x) -> p s x", x=64),
                                   L96[r, 0:PAST].rearrange("p (s x) -> p s x", x=64),
                                   bcast(sel[:, 0:NSB - 1], 1, 64), ALU.add))
            link(dve.tensor_tensor(L96[r, PAST:PAST + 1], PS[r, 5, 0:1], bias96[:, PAST:PAST + 1], ALU.add))
            dve.tensor_reduce(s1(8), L96[r, 0:PAST + 1], AX.X, ALU.max, negate=True).then_inc(ds_max, 1)
            dve.wait_ge(kv_used, F_WINK + 2)
            link(dve.tensor_tensor(Lw[r, 0:T], PS[r, 4, :], bias96[:, PAST - T:PAST], ALU.add))
            link(dve.tensor_tensor(Lw[r, T:T + 1], PS[r, 5, 1:2], bias96[:, PAST:PAST + 1], ALU.add))
            link(dve.memset(Lw[r, 0:1], NEG))
            dve.tensor_reduce(s1(12), Lw[r, 0:T + 1], AX.X, ALU.max, negate=True).then_inc(ds_max, 1)
            for i, (L, n) in enumerate(((L96, PAST + 1), (Lw, T + 1))):
                a = 8 + 4 * i
                dve.wait_ge(ds_exp, i + 1)
                link(dve.reciprocal(s1(a + 2), s1(a + 1)))
                link(dve.tensor_tensor(s1(a + 3), s1(a + 2), g96[r, i + 1:i + 2], ALU.mult))
                dve.tensor_scalar(L[r, 0:n], L[r, 0:n], s1(a + 3), None, ALU.mult).then_inc(ds_p, 1)
            dve.wait_ge(ds_t, 1)
            dve.tensor_copy(PTd[:, 0:20].rearrange("p (a b) x -> p a (b x)", a=4), PS[:, 0:4, 0:5 * ROWS])
            dve.tensor_copy(PTd[0:NC, 20], PS[0:NC, 4, 0:ROWS])
            dve.tensor_copy(PTd[0:1, 21:23].rearrange("p a x -> p (a x)"), PS[0:1, 4, ROWS:3 * ROWS]
                            ).then_inc(ds_pt, 1)
            dve.wait_ge(kv_used, len(FILLS))
            for g2 in range(2):
                r0 = 64 * g2
                v = PS[r0:r0 + 64, 5, 0:ROWS].rearrange("p (b x) -> p b x", x=NH)
                for pair in range(2):
                    a = pair * 6 + g2 * HPG
                    ins = dve.tensor_copy(MIX[r0:r0 + 64, pair * HPG:pair * HPG + HPG, T:TOK],
                                          v[:, :, a:a + HPG].rearrange("p b h -> p h b"))
            ins.then_inc(ds_out, 1)
            dve.wait_ge(th_in, 16)
            prompt_attention(1)
            out_units(C_OUT1)
            norm(2)
            dve.wait_ge(x_ready, 3 * KT)
            router(1)
            moe(1)
            norm(3)


def bucket(dist):
    n = np.maximum(dist, 0)
    nf = np.maximum(n, 1).astype(np.float32)
    large = 16 + (np.log(nf / np.float32(16)) / np.float32(math.log(64)) * np.float32(16)).astype(np.int32)
    return np.where(n < 16, n, np.minimum(large, 31))


def one_hot(dist, rows):
    at = np.where(dist < 0, 32, bucket(dist))
    return (np.arange(rows)[:, None] == at[None, :]).astype(np.float32)


def chunk(w):
    out = np.zeros((KT, P, P), np.float32)
    out[:, :, :w.shape[1]] = w.reshape(KT, P, -1)
    return out.transpose(1, 0, 2).reshape(P, D)


def fm(a):
    return a.T.reshape(-1, P, a.shape[0]).transpose(1, 0, 2)


def kernel(**inputs):
    import concourse.bacc as bacc
    from concourse.bass_utils import run_bass_kernel_spmd

    x = {k: np.asarray(v) for k, v in inputs.items()}
    f = np.ascontiguousarray
    perm = np.arange(768).reshape(2, 2, HPG, HD).transpose(0, 2, 1, 3).reshape(-1)

    w = np.empty((NCH, P, D), np.float32)
    n = 0

    def put(*blocks):
        nonlocal n
        for blk in blocks:
            w[n] = blk
            n += 1

    def columns(a):
        return [chunk(a[:, i:i + P]) for i in range(0, a.shape[1], P)]

    def experts(layer):
        down = x["w_exp_down"][layer]
        for e in range(EXPERTS):
            put(chunk(x["w_exp_gate"][layer, e]), chunk(x["w_exp_up"][layer, e]))
            if e:
                put(down[e - 1])
        put(down[EXPERTS - 1])

    for layer in range(2):
        put(*columns(x["w_mem_kv"][layer]))
    put(*columns(x["w_in_a"][0]))
    put(*columns(x["w_out"][0]))
    experts(0)
    put(*columns(x["w_kv_shared"]))
    wb = x["w_in_b"][0]
    put(*columns(wb[:, :768][:, perm]), *columns(wb[:, 804:1060]), *columns(wb[:, 768:804]))
    put(*columns(x["w_out"][1][np.concatenate([perm, np.arange(768, D)])]))
    experts(1)
    assert n == NCH

    def cols(a):
        return a.reshape(-1, P).T

    pk = np.empty((P, NPK), np.float32)
    w1 = x["cmp_w1"]
    valid = (np.arange(P) >= 31).astype(np.float32)[:, None]
    parts = {"ln1g": cols(x["ln1_g"]), "ln1b": cols(x["ln1_b"]), "ln2g": cols(x["ln2_g"]), "ln2b": cols(x["ln2_b"]),
             "cb": cols(x["conv_b"][0]), "cw": cols(x["conv_w"][0]), "brg": cols(x["b_rg"][0]),
             "big": cols(x["b_ig"][0]), "lam": cols(x["lru_lambda"][0]), "b1": x["cmp_b1"].T,
             "pe": x["cmp_pe"].reshape(32, P).T, "valid": valid,
             "h0": fm(x["state_lru_h"][0]).reshape(P, -1),
             "st": x["state_conv"][0].transpose(2, 1, 0).reshape(RNN, P, 3, B).transpose(1, 0, 2, 3).reshape(P, -1)}
    for k, v in parts.items():
        pk[:, PK[k][0]:PK[k][1]] = v

    def block_diagonal(a):
        out = np.zeros((P, RNN, P), np.float32)
        for t in range(RNN):
            out[:64, t, :64], out[64:, t, 64:] = a[2 * t], a[2 * t + 1]
        return out

    blocks = np.arange(NSB)
    forced = (blocks == 0) | (blocks >= NSB - 2)
    rowc = np.concatenate([~forced, forced * 1e9, np.arange(EGRP, 0, -1), np.arange(EPG, 0, -1)]
                          ).astype(np.float32)[None]
    c0, s0 = np.arange(NC) * 16, blocks * 64
    cover = ((c0[:, None] < s0[None] + 64) & (c0[:, None] + 32 > s0[None])).astype(np.float32)
    tri = (blocks[None, :] < blocks[:, None]).astype(np.float32).reshape(1, NSB, NSB)

    cc, cs, cw, cm = x["cache_cmp_kv"], x["cache_slc_kv"], x["cache_win_kv"], x["cache_mem_kv"]
    wr = np.concatenate([x["w_router_g"], x["w_router_e"]], axis=2).reshape(2, KT, P, 36).transpose(2, 0, 1, 3)
    w1r = w1.reshape(2, 32, 64, P).transpose(2, 0, 1, 3)
    dram = {
        "pages": x["page_table"].reshape(1, P).astype(np.int32),
        "wstream": w,
        "xT": fm(np.concatenate([x["x_prompt"][0], x["x_sample"][:, 0]])),
        "memT": fm(x["mem_prompt"][0]),
        "pk": pk, "rowc": rowc, "ident": np.eye(P, dtype=np.float32), "wr": wr,
        "rb": np.concatenate([x["b_router_g"], x["b_router_e"]], axis=1)[None],
        "tab": x["rel_bias"], "tab96": np.tile(x["rel_bias"], (1, B)), "cover": cover,
        "w2s": x["cmp_w2"].transpose(1, 0, 2),
        "ohp": one_hot(511 - np.arange(640), 33), "ohc": one_hot(np.arange(992) - 511, 33),
        "ohd": one_hot(np.maximum(PAST - np.arange(PAST + 8), 0), 32),
        "tri": tri,
        "w1p": w1.reshape(2, 16, P, P).transpose(2, 0, 1, 3), "w1h": np.concatenate([w1r, w1r]),
        "wbd": np.stack([block_diagonal(x["w_rg"][0]), block_diagonal(x["w_ig"][0])], axis=1),
        "cc": cc.reshape(NPOOL, 64, 2, 2, GRP, HD).transpose(0, 2, 5, 3, 4, 1).reshape(NPOOL, P, 512),
        "slck": cs[:, :, 0].reshape(NPOOL, P, 2, 2, HD).transpose(0, 3, 4, 2, 1).reshape(NPOOL, P, 256),
        "slcv": cs[:, :, 1].reshape(NPOOL, P, 256),
        "wink": cw[:, :, 0].reshape(B, 4, P, 2, 2, HD).transpose(0, 4, 5, 1, 3, 2).reshape(B, P, 1024),
        "winv": cw[:, :, 1].reshape(B, 4, P, 256).transpose(0, 2, 1, 3).reshape(B, P, 1024),
        "winnat": cw.reshape(B, T, 512),
        "memk": cm[:, :, :, 0].reshape(2, B, MEM, 2, 2, HD).transpose(0, 1, 4, 5, 3, 2).reshape(2, B, P, 512),
        "memv": cm[:, :, :, 1].reshape(2, B, 2, P, 256).transpose(0, 1, 3, 2, 4).reshape(2, B, P, 512),
    }
    dram = {k: f(v) for k, v in dram.items()}
    outs = {"o_y": [P, KT, TOK], "o_memk": [P, 2, 2, MEM], "o_memv": [P, 2, 2, 256], "o_st": [P, 144],
            "o_xr": [P, RNN, 3 + B], "o_h": [P, RNN, 1 + B], "o_cmp": [P, 2, 2, TOK], "o_k": [2, P, 2, TOK],
            "o_v": [2, P, QT, 256], "o_vd": [2, B, 256], "o_winold": [B, T - 1, 512]}
    scratch = {"combd": [2, EXPERTS, TOK], "rd": [NH, 640], "rd_rows": [P, NH * 640], "gd": [B, 36]}

    nc = bacc.Bacc("TRN2", target_bir_lowering=False, num_devices=1)
    dr = {k: nc.dram_tensor(k, list(v.shape), mybir.dt.from_np(v.dtype), kind="ExternalInput").ap()
          for k, v in dram.items()}
    dr.update({k: nc.dram_tensor(k, s, F32, kind="ExternalOutput").ap() for k, s in outs.items()})
    dr.update({k: nc.dram_tensor(k, s, F32, kind="Internal").ap() for k, s in scratch.items()})
    build(nc, dr)
    res = run_bass_kernel_spmd(nc, [dram], core_ids=[0]).results[0]
    o = {k: np.asarray(res[k]).reshape(s) for k, s in outs.items()}

    def tokens(a):
        return a.transpose(2, 1, 0).reshape(a.shape[2], -1)

    y = tokens(o["o_y"])
    mem = np.stack([np.stack([tokens(o["o_memk"][:, layer]),
                              o["o_memv"][:, layer].transpose(1, 0, 2).reshape(MEM, 256)], axis=1)
                    for layer in range(2)]).reshape(2, 1, MEM, 2, 4, HD)
    cmp_ = np.stack([tokens(o["o_cmp"][:, 0]), tokens(o["o_cmp"][:, 1])], axis=1).reshape(TOK, 2, GRP, HD)
    rows = []
    for i in range(2):
        v = np.concatenate([o["o_v"][i].transpose(1, 0, 2).reshape(T, 256), o["o_vd"][i]])
        rows.append(np.stack([tokens(o["o_k"][i]), v], axis=1).reshape(TOK, 2, GRP, HD))
    slc, win = rows
    xr = tokens(o["o_xr"])
    h = tokens(o["o_h"])
    state = o["o_st"].reshape(P, RNN, 3, B).transpose(3, 2, 1, 0).reshape(B, 3, 768)
    s_win = np.concatenate([o["o_winold"].reshape(B, T - 1, 2, GRP, HD), win[T:, None]], axis=1)
    s_conv = np.concatenate([state[:, 1:], xr[3:, None]], axis=1)
    leaves = (y[None, :T], y[T:, None], cmp_[None, :T], slc[None, :T], win[None, :T], mem, h[None, :1],
              xr[None, None, :3], cmp_[T:, None], slc[T:, None], s_win, h[None, 1:], s_conv[None])
    return tuple(f(a) for a in leaves)
```

```python
import math
from contextlib import ExitStack

import numpy as np

import concourse.bass as bass
from concourse import mybir

F32 = mybir.dt.float32
I32 = mybir.dt.int32
ALU = mybir.AluOpType
ACT = mybir.ActivationFunctionType
AX = mybir.AxisListType

P = 128
D = 1024
KT = D // P
T = 512
B = 8
TOK = T + B
HALF = TOK // 2
QT = T // P
RT = 104
NRT = TOK // RT
HD = 64
GRP = 4
HPG = 3
NH = GRP * HPG
RNN = 6
PAGES = 16
NPOOL = 160
NC = 127
NCP = 31
NREL = NCP + 8 * (QT - 1)
PAST = 2048
NSB = 33
NSEL = 16
EXPERTS = 32
EGRP = 4
EPG = 8
MEM = 256
ALPHA = 4 ** 0.25
SCALE = 0.125
NEG = -1e30
EPS = 1e-5
RING = 6
ROWS = B * NH
MROWS = B * 4

SLOTS = 8
UNITS = SLOTS * EPG

C_MEM, C_INA, C_OUT0, C_MOE0 = 0, 8, 22, 30
C_KV = C_MOE0 + 3 * UNITS
C_INB = C_KV + 12
C_OUT1 = C_INB + 9
C_MOE1 = C_OUT1 + 8
C_MOE = [C_MOE0, C_MOE1]
N_USE = C_MOE1 + 3 * UNITS
D_MOE = [C_MOE0, C_MOE1 - 3 * (UNITS - EXPERTS)]
NCH = D_MOE[1] + 3 * EXPERTS
PK = {}
_n = 0
for _name, _w in [("ln1g", 16), ("ln1b", 16), ("ln2g", 16), ("ln2b", 16), ("cb", 6), ("cw", 24), ("brg", 6),
                  ("big", 6), ("lam", 6), ("b1", 2), ("pe", 32), ("valid", 1), ("h0", 48), ("st", 144)]:
    PK[_name] = (_n, _n + _w)
    _n += _w
NPK = _n
ROWC = 2 * NSB + EGRP + EPG
RK_UP, RK_128, RK_8, RK_T4, RK_T5, RK_TOK = 0, 104, 232, 240, 244, 249
NRK = RK_TOK + NRT


def attention_jobs():
    jobs = [(0, qt, "mem", h) for qt in range(QT) for h in range(4)]
    for qt in range(QT):
        for h in range(NH):
            jobs += [(1, qt, br, h) for br in ("cmp", "slc", "win")]
        jobs += [(1, qt, "mem", h) for h in range(4)]
    return jobs


JOBS = attention_jobs()
L_JOBS = [range(0, 16), range(16, len(JOBS))]
VALUE_JOBS = [16 + 18 * b + 12 for b in range(B)]



def bcast(ap, at, n):
    dims = [list(x) for x in ap.ap]
    dims.insert(at + 1, [0, n])
    return bass.AP(tensor=ap.tensor, offset=ap.offset, ap=dims)


def dram_rows(ap, n):
    return bass.AP(tensor=ap.tensor, offset=ap.offset, ap=[[0, n]] + [list(x) for x in ap.ap][1:])


def build(nc, dr):
    ctx = ExitStack()
    with ctx:
        def sb(name, shape, dt=F32):
            return ctx.enter_context(nc.sbuf_tensor("sb_" + name, shape, dt))

        def sem(name):
            return ctx.enter_context(nc.semaphore(name))

        ring = sb("ring", [P, RING, D])
        X = sb("X", [P, KT, TOK])
        R = sb("R", [P, KT, TOK])
        MIX = sb("MIX", [P, KT, TOK])
        compK = sb("compK", [P, B, 2, P])
        compV = sb("compV", [P, B, 256])
        memK = sb("memK", [P, 2, 2, MEM])
        memV = sb("memV", [P, 2, 2, 256])
        bias96 = sb("bias96", [P, PAST + 8])
        pk = sb("pk", [P, NPK])
        rowc = sb("rowc", [P, ROWC])
        ident = sb("ident", [P, P])
        onesD = sb("onesD", [P, P])
        wr = sb("wr", [P, 2, KT, 36])
        rb = sb("rb", [P, 2, 36])
        tabx = sb("tabx", [33, NH])
        tab96 = sb("tab96", [32, ROWS])
        cover = sb("cover", [P, NSB])
        w2s = sb("w2s", [P, 2, 64])
        pages = sb("pages", [1, P], I32)
        b1e = sb("b1e", [P, 2])
        slot_i = sb("slot_i", [P, NRT], I32)
        tok_i = sb("tok_i", [P, SLOTS], I32)
        place_i = sb("place_i", [1, SLOTS], I32)
        st = sb("st", [P, 64])
        jst = sb("jst", [P, 4, 8])
        sp8 = sb("sp8", [P, 6, 6])
        xtail = sb("xtail", [P, RNN, 3 + B])
        AR = 23988
        arena = sb("arena", [P, AR])
        PS = ctx.enter_context(nc.psum_tensor("PS", [P, 8, 512], F32))

        def ar(off, *dims):
            n = int(np.prod(dims))
            assert off + n <= AR, (off, dims)
            v = arena[:, off:off + n]
            if len(dims) == 1:
                return v
            names = "abcde"[:len(dims)]
            pat = f"p ({' '.join(names)}) -> p {' '.join(names)}"
            return v.rearrange(pat, **{names[i]: dims[i] for i in range(1, len(dims))})

        def pcol(name, i, n=1):
            a = PK[name][0] + i
            return pk[:, a:a + n]

        Rf = R[:, :, :].rearrange("p a b -> p (a b)")
        Mf = MIX[:, :, :].rearrange("p a b -> p (a b)")
        memT = Mf[:, 0:2048].rearrange("p (k t) -> p k t", k=KT)
        w1p = ar(0, 2, 16, P)
        ccb = [ar(4096 + 8192 * i, PAGES, 8, 64) for i in range(2)]
        p2 = [Mf[:, 512 * i:512 * i + 512] for i in range(2)]
        hsb = [Mf[:, 1024 + 512 * i:1536 + 512 * i] for i in range(2)]
        ohp, ohc, ohd = Rf[0:33, 0:640], Rf[0:33, 640:1632], Rf[0:32, 1632:1632 + PAST + 8]
        rrow = Mf[0:NH, 2100:2740]
        cmpB = ar(22500, NREL, NH)
        gateT = ar(0, RNN, TOK)
        xrT = ar(3120, RNN, TOK)
        rT = ar(6240, RNN, TOK)
        iT = ar(9360, RNN, TOK)
        xcT = ar(12480, RNN, TOK)
        mq0 = ar(15600, 2, TOK)
        wbd = Rf[:, 0:1536].rearrange("p (w t j) -> p w t j", w=2, t=RNN)
        qT = ar(0, 6, TOK)
        mq1 = ar(3120, 2, TOK)
        KT_ = {"slc": ar(4160, 2, TOK), "win": ar(5200, 2, TOK)}
        VT_ = {"slc": ar(6240, 5, 256), "win": ar(7520, 5, 256)}
        kcT = ar(8800, 2, NCP)
        vcp = ar(8864, 256)
        gates = ar(9120, 5, 36)
        g96 = ar(9300, 3)
        w1q = ar(10800, 2, 16, P)
        cmpZ = ar(14896, 2, GRP, T // 2)
        cmpT = ar(18992, 2, 2, TOK)
        hgp = ar(21072, 2, GRP, NCP)
        QZ = ar(10800, 1632)
        kvb1 = ar(12976, 4096)
        L96 = ar(17072, PAST + 8)
        Lw = ar(19128, T + 8)
        Lc = ar(19648, P)
        SEL = ar(19776, 5, 36)
        PTs = bias96[:, 0:PAGES * ROWS].rearrange("p (t r) -> p t r", t=PAGES)
        PTd = ar(20040, 7, ROWS)
        cube = ar(20040, NSB, NSB)
        tri = ar(21129, NSB, NSB)
        S3 = ar(22344, ROWS)
        vrow_parts = [(0, 0, B, Mf[0:1, 0:2048]), (1, 0, 6, Mf[0:1, 2048:3584]), (1, 6, B, Mf[0:1, 3640:4152])]

        def vrow(i, b):
            for part, b0, b1, v in vrow_parts:
                if part == i and b0 <= b < b1:
                    return v[:, (b - b0) * 256:(b - b0) * 256 + 256]
        TH = ar(10800, NH, T)
        Sb = [ar(16944 + 512 * i, T) for i in range(2)]
        Pb = [ar(17968 + 512 * i, T) for i in range(2)]
        PTb = [ar(18992 + 512 * i, T) for i in range(2)]
        mixTM = [ar(20016 + 1024 * i, D) for i in range(2)]
        QZM = [ar(20272, 544), ar(12432, 544)]
        LM = [ar(21296, MEM), ar(17072, MEM)]
        PTM = [ar(21552, 2, MROWS), ar(17328, 2, MROWS)]
        sg = [ar(P * i, P) for i in range(2)]
        hidm = [ar(256 + P * i, P) for i in range(2)]
        hidT = [ar(512 + P * i, P) for i in range(2)]
        RONE = ar(768, NRT, P)
        RHS = ar(1408, NRT, SLOTS, EPG + 1)
        V9 = ar(1768, NRT, EPG + 1)
        CP = ar(1820, SLOTS * (EPG + 1))
        OGX = ar(1900, NRT + 2, EGRP)
        QONE = ar(1928, NRT, SLOTS)
        N5 = ar(1970, EGRP, 5)
        NG = ar(1990, 2, EGRP)
        TG3 = ar(2000, SLOTS, 3)
        TGF = ar(2024, SLOTS)
        W5 = ar(2040, 6, NRT)
        LG = ar(3120, NRT, 36)
        M1 = ar(3300, NRT, EGRP, EPG)
        T20 = ar(3460, NRT, EGRP)
        OG = ar(3620, NRT, EGRP)
        TG = ar(3640, NRT, EGRP)
        LE = ar(3660, NRT, EPG)
        O1 = ar(3700, NRT, EPG)
        O2 = ar(3740, NRT, EPG)
        T8 = ar(3780, NRT, EPG)
        SC = ar(3820, 12, NRT)
        RK = ar(4960, NRK)
        XT = [ar(5300 + D * i, KT, P) for i in range(2)]
        xg = [ar(7348 + D * i, D) for i in range(2)]
        rows_tm = [Mf[:, D * i:D * i + D] for i in range(4)] + [ar(9396, D)]
        ytm = [ar(18992 + D * i, D) for i in range(2)]
        rs = ar(4440, TOK)

        CONSTS = [(X[:], dr["xT"]), (pk[:], dr["pk"]), (rowc[:], dram_rows(dr["rowc"], P)),
                  (ident[:], dr["ident"]), (wr[:], dr["wr"]), (rb[:], dram_rows(dr["rb"], P)),
                  (tabx[0:32, :], dr["tab"]), (tab96[:], dr["tab96"]), (cover[0:NC, :], dr["cover"]),
                  (w2s[:], dr["w2s"]), (ohp, dr["ohp"]), (ohc, dr["ohc"]), (ohd, dr["ohd"])]

        mem_in = sem("mem_in")
        const_in = sem("const_in")
        pages_in = sem("pages_in")
        w1_in = sem("w1_in")
        rd_stored = sem("rd_stored")
        memset_done = sem("memset_done")
        w_land = [sem(f"w_land{i}") for i in range(RING)]
        w_used = sem("w_used")
        lin_act = sem("lin_act")
        lin_dve = sem("lin_dve")
        tab_ready = sem("tab_ready")
        tab_moved = sem("tab_moved")
        cc_land = [sem("cc_land0"), sem("cc_land1")]
        cmp_ab = sem("cmp_ab")
        p2_done = sem("p2_done")
        hs_done = sem("hs_done")
        hg_done = sem("hg_done")
        cmp_w2 = sem("cmp_w2")
        cmp_out = sem("cmp_out")
        lam_exp = sem("lam_exp")
        lam_abs = sem("lam_abs")
        conv_done = sem("conv_done")
        gmm_done = sem("gmm_done")
        gate_sig = sem("gate_sig")
        la_done = sem("la_done")
        at_done = sem("at_done")
        u2_done = sem("u2_done")
        sq_done = sem("sq_done")
        lru_done = sem("lru_done")
        bd_in = sem("bd_in")
        s_done = sem("s_done")
        max_done = sem("max_done")
        exp_done = sem("exp_done")
        pt_ready = sem("pt_ready")
        pt_done = sem("pt_done")
        v_done = sem("v_done")
        o_done = sem("o_done")
        mt_ready = sem("mt_ready")
        mt_done = sem("mt_done")
        kv_land = [sem("kv_land0"), sem("kv_land1")]
        sv_added = sem("sv_added")
        os_moved = sem("os_moved")
        os_turned = sem("os_turned")
        sv_land = [sem("sv_land0"), sem("sv_land1")]
        kv_used = sem("kv_used")
        qz_done = sem("qz_done")
        dm_max, dm_exp, dm_p = sem("dm_max"), sem("dm_exp"), sem("dm_probs")
        dm_t, dm_pt, dm_out = sem("dm_turned"), sem("dm_moved"), sem("dm_out")
        dc_s, dc_max, dc_exp, dc_p = sem("dc_scores"), sem("dc_max"), sem("dc_exp"), sem("dc_probs")
        dc_t, dc_sum, dc_imp = sem("dc_turned"), sem("dc_headsum"), sem("dc_importance")
        ds_s, ds_max, ds_exp, ds_p = sem("ds_scores"), sem("ds_max"), sem("ds_exp"), sem("ds_probs")
        ds_t, ds_pt, ds_o, ds_out = sem("ds_turned"), sem("ds_moved"), sem("ds_values"), sem("ds_out")
        mu_ready = sem("mu_ready")
        xm_ready = sem("xm_ready")
        sqr_ready = sem("sqr_ready")
        var_ready = sem("var_ready")
        ve_ready = sem("ve_ready")
        std_ready = sem("std_ready")
        nrm_ready = sem("nrm_ready")
        x_ready = sem("x_ready")
        lg_ready = sem("lg_ready")
        rmax_ready = sem("rmax_ready")
        rexp_ready = sem("rexp_ready")
        rk_in = sem("rk_in")
        og_ready = sem("og_ready")
        rank_ready = sem("rank_ready")
        oneh_ready = sem("oneh_ready")
        slots_mm = sem("slots_mm")
        slots_ready = sem("slots_ready")
        xs_ready = sem("xs_ready")
        xs_moved = sem("xs_moved")
        x_stored = sem("x_stored")
        xg_land = [sem("xg_land0"), sem("xg_land1")]
        xt_ready = sem("xt_ready")
        xt_act = sem("xt_act")
        xt_dve = sem("xt_dve")
        sg_done = sem("sg_done")
        hid_done = sem("hid_done")
        ht_ready = sem("ht_ready")
        ht_moved = sem("ht_moved")
        y_act = sem("y_act")
        y_dve = sem("y_dve")
        y_stored = [sem("y_stored0"), sem("y_stored1")]
        yg_land = [sem(f"yg_land{i}") for i in range(NRT)]
        fin_ready = sem("fin_ready")
        acc_done = sem("acc_done")
        w1q_in = sem("w1q_in")
        z_done = sem("z_done")
        cp_h = sem("cp_h")
        cp_g = sem("cp_g")
        cp_o = sem("cp_o")
        cp_done = sem("cp_done")
        g_stored = sem("g_stored")
        g96_in = sem("g96_in")
        vrow_in = sem("vrow_in")
        th_in = sem("th_in")
        tri_in = sem("tri_in")
        stores = sem("stores")
        dve_chain = sem("dve_chain")

        def at_least(eng, s, v):
            if not (isinstance(v, int) and v <= 0):
                eng.wait_ge(s, v)

        lin_order = [c for c in range(N_USE) if c < C_MOE0 or C_KV <= c < C_MOE1]
        lin_index = {c: i for i, c in enumerate(lin_order)}
        lin_engine = ["dve" if C_OUT0 <= c < C_MOE0 or C_OUT1 <= c < C_MOE1 else "act" for c in lin_order]

        def lin_moved(eng, i):
            at_least(eng, lin_act, lin_engine[:max(i, 0)].count("act"))
            at_least(eng, lin_dve, lin_engine[:max(i, 0)].count("dve"))

        def lin_bank(c):
            return 2 * (lin_index[c] % 2)

        both = [(0, HALF), (HALF, HALF)]
        tiles5 = [(i * P, P) for i in range(QT)] + [(T, B)]

        def halves(ap):
            return ap.rearrange("p (h t) -> p h t", h=2)

        FILLS = ([("mem", 0)] * 4 + [("mem", 1)] * 4 + [("slck", b) for b in range(B)] +
                 [("wink", 0), ("wink", 4), ("winv", 0), ("winv", 4)] + [("slcv", b) for b in range(B)])
        F_SLCK, F_WINK, F_WINV, F_SLCV = 8, 16, 18, 20

        def fill_landed(eng, f):
            if f >= F_SLCV:
                eng.wait_ge(sv_land[f % 2], 256 * ((f - F_SLCV) // 2 + 1))
                return
            eng.wait_ge(kv_land[f % 2], sum(256 if FILLS[g][0][:3] == "slc" else 16 for g in range(f % 2, f + 1, 2)))

        mem_half = [Rf[:, 2048 * i:2048 * i + 2048].rearrange("p (b x) -> p b x", b=4) for i in range(2)]
        ring4 = ring[:, 0:4, :].rearrange("p s x -> p (s x)")

        OS = ring[:, 4:6, :].rearrange("p s x -> p (s x)")

        def kv_buf(f):
            return (ring4, Rf[:, 0:4096])[f % 2] if f >= F_SLCV else (Rf[:, 0:4096], kvb1)[f % 2]


        def job_tiles(j):
            layer, qt, br, h = JOBS[j]
            return {"cmp": 1, "mem": 2}.get(br, qt + 1)

        def job_nk(j):
            layer, qt, br, h = JOBS[j]
            return {"cmp": NCP, "mem": MEM}.get(br, (qt + 1) * P)

        def job_place(j):
            layer, qt, br, h = JOBS[j]
            qs = slice(qt * P, qt * P + P)
            if br == "mem":
                r0, pair = 64 * (h % 2), h // 2
                return (mq0, mq1)[layer][r0:r0 + 64, pair, qs], memK[r0:r0 + 64, layer, pair, :]
            g, hh = divmod(h, HPG)
            r0, pair = 64 * (g % 2), g // 2
            q = qT[r0:r0 + 64, pair * HPG + hh, qs]
            if br == "cmp":
                return q, kcT[r0:r0 + 64, pair, :]
            return q, KT_[br][r0:r0 + 64, pair, 0:job_nk(j)]

        def job_value(j, kt):
            layer, qt, br, h = JOBS[j]
            g = h // HPG
            if br == "mem":
                return memV[:, layer, kt, h * 64:h * 64 + 64]
            if br == "cmp":
                return vcp[0:NCP, g * 64:g * 64 + 64]
            return VT_[br][:, kt, g * 64:g * 64 + 64]

        def job_column(j):
            layer, qt, br, h = JOBS[j]
            if br == "mem":
                return (0 if layer == 0 else 768) + h * 64
            g, hh = divmod(h, HPG)
            return ((g // 2) * HPG + hh) * P + 64 * (g % 2)

        def last_job(layer, qt):
            return max(j for j in L_JOBS[layer] if JOBS[j][1] == qt)

        LASTS = {last_job(layer, qt): (layer, qt) for layer in range(2) for qt in range(QT)}

        def turns_before(layer, qt):
            return QT + 2 * qt if layer else qt

        def half_fill(eng, f, half):
            kind, b = FILLS[f]
            buf = kv_buf(f).rearrange("p (j x) -> p j x", j=PAGES)
            js = range(8 * half, 8 * half + 8)
            pgs = [eng.value_load(pages[0:1, bass.ds(b * PAGES + j, 1)], min_val=0, max_val=NPOOL - 1) for j in js]
            eng.wait_ge(kv_used, max(f - 1, 8) if f < F_SLCV else {0: 8, 1: F_WINV + 1}.get(f - F_SLCV, f - 1))
            for j, pg in zip(js, pgs):
                eng.dma_start(buf[:, j], dr[kind][bass.ds(pg, 1)].rearrange("o p j -> (o p) j")
                              ).then_inc((sv_land if f >= F_SLCV else kv_land)[f % 2], 16)

        def gate_place(u, b):
            return 3 * u - 1 if u else 0

        def down_place(u, b):
            return 3 * u + 4 - (2 if isinstance(b, int) and b * 16 + u == UNITS - 1 else 0)

        block = ctx.enter_context(nc.Block())

        @block.sync
        def _(sp):
            sp.dma_start(pages[:], dr["pages"]).then_inc(pages_in, 16)

            def slot_free(c):
                at_least(sp, w_used, c - RING + 1)

            def load_chunk(c):
                slot_free(c)
                row = c if c < C_MOE0 else c - 3 * (UNITS - EXPERTS)
                sp.dma_start(ring[:, c % RING, :], dr["wstream"][row]).then_inc(w_land[c % RING], 16)

            def fill_pages(buf, landed, pool, b):
                for j in range(PAGES):
                    pg = sp.value_load(pages[0:1, bass.ds(b * PAGES + j, 1)], min_val=0, max_val=NPOOL - 1)
                    sp.dma_start(buf[:, j], pool[bass.ds(pg, 1)].rearrange("o p j -> (o p) j")).then_inc(landed, 16)

            ccf = [v.rearrange("p a b c -> p a (b c)") for v in ccb]
            for c in range(RING):
                load_chunk(c)
            sp.wait_ge(pages_in, 16)
            fill_pages(ccf[0], cc_land[0], dr["cc"], 0)
            load_chunk(6)
            load_chunk(7)
            fill_pages(ccf[1], cc_land[1], dr["cc"], 1)
            with sp.Fori(0, 3) as i:
                for u in range(2):
                    sp.wait_ge(cmp_ab, i * 4 + 2 * u + 2)
                    fill_pages(ccf[u], cc_land[u], dr["cc"], i * 2 + 2 + u)
            for c in range(C_INA, C_OUT0):
                load_chunk(c)

            def mem_fills(layer):
                for n, (kind, b0) in enumerate((("k", 0), ("k", 4), ("v", 0), ("v", 4))):
                    f = 4 * layer + n
                    at_least(sp, kv_used, f - 1)
                    sp.dma_start(mem_half[f % 2], dr["mem" + kind][layer, b0:b0 + 4].rearrange("b p x -> p b x")
                                 ).then_inc(kv_land[f % 2], 16)

            sp.wait_ge(gmm_done, 12)
            mem_fills(0)
            for c in range(C_OUT0, C_MOE0):
                load_chunk(c)

            def moe_loads(layer):
                c0 = C_MOE[layer]
                if layer == 0:
                    sp.wait_ge(lin_dve, KT)
                    sp.dma_start(w1q, dr["w1p"]).then_inc(w1q_in, 16)
                for rt in range(NRT):
                    sp.wait_ge(xs_moved, 2 * (NRT * layer + rt) + 2)
                    sp.dma_start(dr["x_tm"][rt * RT:rt * RT + RT], rows_tm[rt][0:RT]).then_inc(x_stored, 16)
                sp.wait_ge(slots_ready, 1 + layer)

                def place(tile):
                    lo = D_MOE[layer]
                    return sp.value_load(place_i[0:1, bass.ds(tile, 1)], min_val=lo, max_val=lo + 3 * EPG * (EGRP - 1))

                def load(u, part, at, b):
                    c = c0 + (gate_place(u, b) + part if part < 2 else down_place(u, b))
                    sp.wait_ge(w_used, b * 48 + (c - RING + 1))
                    sp.dma_start(ring[:, c % RING, :],
                                 dr["wstream"][bass.ds(at + (3 * (u % EPG) + part), 1)].rearrange("o p j -> (o p) j")
                                 ).then_inc(w_land[c % RING], 16)

                def body(b):
                    at = [place(b * 2 + k) for k in range(3 if not (isinstance(b, int) and b == 3) else 2)]
                    for r in range(1, 17):
                        if r // 8 < len(at):
                            load(r, 0, at[r // 8], b)
                            load(r, 1, at[r // 8], b)
                        load(r - 1, 2, at[(r - 1) // 8], b)

                at0 = place(0)
                load(0, 0, at0, 0)
                load(0, 1, at0, 0)
                body(0)
                with sp.Fori(1, 3) as b:
                    body(b)
                body(3)

            moe_loads(0)
            for c in range(C_KV, C_OUT1):
                load_chunk(c)
            sp.wait_ge(x_ready, 2 * KT)
            mem_fills(1)
            sp.wait_ge(cp_done, 2)
            for f in range(8, F_SLCV):
                kind, b0 = FILLS[f]
                buf, landed = kv_buf(f), kv_land[f % 2]
                if kind[:3] == "slc":
                    half_fill(sp, f, 0)
                else:
                    sp.wait_ge(kv_used, max(f - 1, 8))
                    sp.dma_start(buf.rearrange("p (b x) -> p b x", b=4),
                                 dr[kind][b0:b0 + 4].rearrange("b p x -> p b x")).then_inc(landed, 16)
            sp.wait_ge(w_used, C_OUT1)
            for half in range(2):
                half_fill(sp, F_SLCV, half)
            sp.wait_ge(kv_used, F_SLCV)
            sp.wait_ge(rd_stored, 32)
            rows = dr["rd_rows"]
            sp.dma_start(TH, bass.AP(tensor=rows.tensor, offset=rows.offset + 127,
                                     ap=[[NH * 640 - 1, P], [640, NH], [1, T]])).then_inc(th_in, 16)
            for f in range(F_SLCV + 1, len(FILLS)):
                for half in range(2):
                    half_fill(sp, f, half)
            sp.wait_ge(os_turned, 1)
            for c in range(C_OUT1, C_MOE1):
                load_chunk(c)
            moe_loads(1)

        @block.gpsimd
        def _(pool):
            pool.dma_start(dr["o_winold"], dr["winnat"][:, 1:, :]).then_inc(stores, 16)
            pool.wait_ge(tab_moved, 1)
            pool.dma_start(dr["rd"], rrow).then_inc(rd_stored, 16)
            pool.wait_ge(rd_stored, 16)
            pool.dma_start(dr["rd_rows"], dram_rows(dr["rd"].rearrange("(o h) m -> o (h m)", o=1), P)
                           ).then_inc(rd_stored, 16)
            lin_moved(pool, 8)
            pool.dma_start(dr["o_memk"], memK[:]).then_inc(stores, 16)
            pool.dma_start(dr["o_memv"], memV[:]).then_inc(stores, 16)
            pool.wait_ge(const_in, 16 * len(CONSTS))
            pool.dma_start(dr["o_st"], pcol("st", 0, 144)).then_inc(stores, 16)
            pool.wait_ge(tab_ready, 4)
            pool.dma_start(wbd, dr["wbd"]).then_inc(bd_in, 16)
            pool.wait_ge(conv_done, RNN)
            pool.dma_start(dr["o_xr"], xtail[:]).then_inc(stores, 16)
            pool.wait_ge(lru_done, 1)
            pool.dma_start(dr["o_h"], rT[:, :, T - 1:TOK]).then_inc(stores, 16)

            def moe(layer):
                pool.wait_ge(lin_dve, KT * (layer + 1))
                pool.dma_start(RK, dr["rk"]).then_inc(rk_in, 16)
                pool.wait_ge(slots_ready, 1 + layer)
                pool.wait_ge(x_stored, 16 * NRT * (layer + 1))
                g0 = SLOTS * layer

                def store(i):
                    pool.wait_ge(y_act, g0 + i + 1)
                    pool.wait_ge(y_dve, g0 + i + 1)
                    pool.dma_start(dr["y_tm"][i * P:i * P + P], ytm[i % 2]).then_inc(y_stored[i % 2], 16)

                for i in range(SLOTS):
                    at_least(pool, xt_ready, g0 + i - 1)
                    pool.indirect_dma_start(out=xg[i % 2], out_offset=None, in_=dr["x_tm"],
                                            in_offset=bass.IndirectOffsetOnAxis(ap=tok_i[:, i:i + 1], axis=0)
                                            ).then_inc(xg_land[i % 2], 16)
                    if i >= 3:
                        store(i - 3)
                for i in range(SLOTS - 3, SLOTS):
                    store(i)
                for i in range(2):
                    pool.wait_ge(y_stored[i], 16 * (SLOTS // 2) * (layer + 1))
                for rt in range(NRT):
                    pool.indirect_dma_start(out=rows_tm[rt][0:RT], out_offset=None, in_=dr["y_tm"],
                                            in_offset=bass.IndirectOffsetOnAxis(ap=slot_i[0:RT, rt:rt + 1], axis=0)
                                            ).then_inc(yg_land[rt], 16)

            moe(0)
            lin_moved(pool, lin_index[C_KV] + 12)
            pool.dma_start(dr["o_cmp"], cmpT).then_inc(stores, 16)
            for i, br in enumerate(("slc", "win")):
                pool.dma_start(dr["o_k"][i], KT_[br]).then_inc(stores, 16)
                pool.dma_start(dr["o_v"][i], VT_[br][:, 0:QT, :]).then_inc(stores, 16)
                pool.dma_start(dr["o_vd"][i], VT_[br][0:B, QT, :]).then_inc(stores, 16)
            pool.wait_ge(stores, 16 * 13)
            pool.wait_ge(cp_done, 2)
            for i, b0, b1, v in vrow_parts:
                pool.dma_start(v, dr["o_vd"][i, b0:b1].rearrange("(o b) c -> o (b c)", o=1)).then_inc(vrow_in, 16)
            pool.dma_start(tri[0:ROWS], dram_rows(dr["tri"], ROWS)).then_inc(tri_in, 16)
            moe(1)
            pool.wait_ge(x_ready, 4 * KT)
            pool.dma_start(dr["o_y"], X[:]).then_inc(stores, 16)
            pool.wait_ge(stores, 16 * 14)

        @block.tensor
        def _(pe):
            def fm_unit(c, src, widths):
                lin_moved(pe, lin_index[c] - 1)
                pe.wait_ge(w_land[c % RING], 16 * (c // RING + 1))
                bank = lin_bank(c)
                for k in range(KT):
                    for hf, (a, n) in enumerate(widths):
                        mm = pe.matmul(PS[:, bank + hf, 0:n], ring[:, c % RING, k * P:k * P + P],
                                       src[:, k, a:a + n], start=(k == 0), stop=(k == KT - 1))
                mm.then_inc(w_used, 1)

            def tm_unit(c, src, tiles, cols):
                lin_moved(pe, lin_index[c] - 1)
                pe.wait_ge(w_land[c % RING], 16 * (c // RING + 1))
                bank = lin_bank(c)
                for t, (a, n) in enumerate(tiles):
                    o = PS[0:n, bank, t * P:t * P + cols] if t < 4 else PS[0:n, bank + 1, 0:cols]
                    for k in range(KT):
                        mm = pe.matmul(o, src[:, k, a:a + n], ring[:, c % RING, k * P:k * P + cols],
                                       start=(k == 0), stop=(k == KT - 1))
                mm.then_inc(w_used, 1)

            pe.wait_ge(mem_in, 16)
            for c in range(8):
                if c % 4 < 2:
                    fm_unit(c, memT, [(0, MEM)])
                else:
                    tm_unit(c, memT, [(0, P), (P, P)], P)
            pe.wait_ge(const_in, 16 * len(CONSTS))
            pe.wait_ge(memset_done, 2)
            for i, (a, n) in enumerate(((0, 512), (512, 128))):
                mm = pe.matmul(PS[0:NH, 4 + i, 0:n], tabx[:], ohp[:, a:a + n], start=True, stop=True)
            mm.then_inc(tab_ready, 1)
            mm = pe.matmul(PS[0:ROWS, 6, 0:1], tab96[:], ohd[:, PAST:PAST + 1], start=True, stop=True)
            mm.then_inc(tab_ready, 1)
            lin_moved(pe, 8)
            for i in range(4):
                mm = pe.matmul(PS[0:ROWS, i, :], tab96[:], ohd[:, i * 512:i * 512 + 512], start=True, stop=True)
            mm.then_inc(tab_ready, 1)
            pe.wait_ge(tab_moved, 3)
            for n in range(NREL):
                a = 16 * (NREL - 1 - n)
                mm = pe.matmul(PS[:, n // 28, n % 28 * NH:n % 28 * NH + NH], ohc[:, a:a + P], tabx[:],
                               start=True, stop=True)
            mm.then_inc(tab_ready, 1)
            pe.wait_ge(w1_in, 16)
            for kv in range(2):
                for s in range(16):
                    mm = pe.matmul(PS[:, 5, kv:kv + 1], w1p[:, kv, s, :], pcol("pe", kv * 16 + s),
                                   start=(s == 0), stop=(s == 15))
            mm.then_inc(tab_ready, 1)
            pe.wait_ge(tab_moved, 4)

            def comp_ab(um, u, landed):
                kv = um % 2
                if kv == 0:
                    pe.wait_ge(cc_land[um // 2], landed)
                at_least(pe, hs_done, u - 1)
                v = ccb[um // 2][:, :, kv * 4:kv * 4 + 4, :].rearrange("p a g (c s) -> p g a c s", s=8)
                for h in range(2):
                    for s in range(8):
                        mm = pe.matmul(PS[:, 2 * kv + h, :], w1p[:, kv, 8 * h + s, :], v[:, :, :, :, s],
                                       start=(s == 0), stop=(s == 7))
                mm.then_inc(cmp_ab, 1)

            def comp_w2(um, u):
                kv = um % 2
                pe.wait_ge(hg_done, u + 1)
                at_least(pe, cmp_out, u - 1)
                hg = hsb[kv].rearrange("p (g c) -> p g c", g=4)
                for g in range(4):
                    if kv == 0:
                        r0 = 64 * (g % 2)
                        mm = pe.matmul(PS[r0:r0 + 64, 6, (g // 2) * P:(g // 2) * P + NC], w2s[:, 0, :],
                                       hg[:, g, 0:NC], start=True, stop=True)
                    else:
                        mm = pe.matmul(PS[0:NC, 7, g * 64:g * 64 + 64], hg[:, g, 0:NC], w2s[:, 1, :],
                                       start=True, stop=True)
                mm.then_inc(cmp_w2, 1)

            comp_ab(0, 0, 256)
            for um in range(4):
                comp_ab((um + 1) % 4, um + 1, 512 if um == 3 else 256)
                comp_w2(um, um)
            with pe.Fori(1, 3) as i:
                for um in range(4):
                    comp_ab((um + 1) % 4, i * 4 + (um + 1), i * 256 + (512 if um == 3 else 256))
                    comp_w2(um, i * 4 + um)
            for um in range(4):
                if um < 3:
                    comp_ab(um + 1, 13 + um, 1024)
                comp_w2(um, 12 + um)

            for c in range(C_INA, C_OUT0):
                fm_unit(c, X, both)
            pe.wait_ge(bd_in, 16)
            pe.wait_ge(cmp_out, 16)
            for n in range(12):
                pe.wait_ge(conv_done, n % 6 + 1)
                at_least(pe, gate_sig, n - 1)
                for hf, (a, m) in enumerate(both):
                    mm = pe.matmul(PS[:, 4 + 2 * (n % 2) + hf, 0:m], wbd[:, n // 6, n % 6, :],
                                   xcT[:, n % 6, a:a + m], start=True, stop=True)
                mm.then_inc(gmm_done, 1)

            def sample_mem(layer):
                f = 4 * layer
                pe.wait_ge(qz_done, 1 + layer)
                for b in range(B):
                    if b % 4 == 0:
                        fill_landed(pe, f + b // 4)
                    for pair in range(2):
                        mm = pe.matmul(PS[0:MROWS, 7, 0:MEM],
                                       QZM[layer][:, b * 64 + pair * 32:b * 64 + pair * 32 + 32],
                                       mem_half[b // 4][:, b % 4, pair * MEM:pair * MEM + MEM],
                                       start=(b == 0 and pair == 0), stop=(b == 7 and pair == 1))
                    if b % 4 == 3:
                        mm.then_inc(kv_used, 1)
                pe.wait_ge(dm_p, 1 + layer)
                for kt in range(2):
                    mm = pe.matmul(PS[:, 7, MEM + 32 * kt:MEM + 32 * kt + 32], LM[layer][0:MROWS, kt * P:kt * P + P],
                                   ident[0:MROWS, 0:MROWS], start=True, stop=True)
                mm.then_inc(dm_t, 1)
                pe.wait_ge(dm_pt, 1 + layer)
                for b in range(B):
                    if b % 4 == 0:
                        fill_landed(pe, f + 2 + b // 4)
                    for kt in range(2):
                        for pair in range(2):
                            n = b * 4 + pair * 2
                            mm = pe.matmul(PS[:, 6, n:n + 2],
                                           mem_half[b // 4][:, b % 4, kt * 256 + pair * P:kt * 256 + pair * P + P],
                                           PTM[layer][:, kt, n:n + 2], start=(n == 0 and kt == 0),
                                           stop=(b == 7 and kt == 1), skip_group_check=True)
                    if b % 4 == 3:
                        mm.then_inc(kv_used, 1)

            def job_s(j):
                at_least(pe, exp_done, j - 1)
                q, k = job_place(j)
                pe.matmul(PS[:, j % 2, 0:job_nk(j)], q, k, start=True, stop=True).then_inc(s_done, 1)

            def job_t(j):
                pe.wait_ge(exp_done, j + 1)
                at_least(pe, pt_done, j - 1)
                for kt in range(job_tiles(j)):
                    n = min(P, job_nk(j) - kt * P)
                    mm = pe.transpose(PS[0:n, 2 + j % 2, kt * P:kt * P + P], Pb[j % 2][:, kt * P:kt * P + n], ident[:])
                mm.then_inc(pt_ready, 1)

            def job_v(j):
                pe.wait_ge(pt_done, j + 1)
                at_least(pe, o_done, j - 1)
                last = job_tiles(j) - 1
                for kt in range(last + 1):
                    n = min(P, job_nk(j) - kt * P)
                    mm = pe.matmul(PS[:, 4 + j % 2, 0:64], PTb[j % 2][0:n, kt * P:kt * P + P], job_value(j, kt),
                                   start=(kt == 0), stop=(kt == last))
                mm.then_inc(v_done, 1)

            def mix_t(layer, qt):
                pe.wait_ge(o_done, last_job(layer, qt) + 1)
                for h in range(1 + layer):
                    at_least(pe, mt_done, turns_before(layer, qt) + h)
                    for t in range(4 if layer else 2):
                        mm = pe.transpose(PS[:, 6, t * P:t * P + P],
                                          mixTM[qt % 2][:, (4 * h + t) * P:(4 * h + t) * P + P], ident[:])
                    mm.then_inc(mt_ready, 1)

            def prompt_attention(layer, selected_values=None):
                js = L_JOBS[layer]
                for j in range(js.start, js.stop + 4):
                    if selected_values and j in VALUE_JOBS:
                        selected_values(VALUE_JOBS.index(j))
                    if selected_values and j == VALUE_JOBS[-1] + 8:
                        turn_samples()
                    if j in js:
                        job_s(j)
                    if j - 1 in js:
                        job_t(j - 1)
                    if j - 2 in js:
                        job_v(j - 2)
                    if j - 4 in js and j - 4 in LASTS:
                        mix_t(*LASTS[j - 4])

            def norm(n):
                pe.wait_ge(*((acc_done, 2 * NRT * (n // 2 + 1)) if n % 2 else (lin_dve, KT * (n // 2 + 1))))
                for hf, (a, m) in enumerate(both):
                    for k in range(KT):
                        mm = pe.matmul(PS[:, 4 + hf, 0:m], onesD[:], R[:, k, a:a + m], start=(k == 0), stop=(k == 7))
                    mm.then_inc(mu_ready, 1)
                for hf, (a, m) in enumerate(both):
                    pe.wait_ge(sqr_ready, 2 * n + hf + 1)
                    for k in range(KT):
                        mm = pe.matmul(PS[:, 6 + hf, 0:m], onesD[:], MIX[:, k, a:a + m], start=(k == 0), stop=(k == 7))
                    mm.then_inc(var_ready, 1)

            def moe(layer):
                c0, u0, g0 = C_MOE[layer], UNITS * layer, SLOTS * layer

                def landed(c, b):
                    pe.wait_ge(w_land[c % RING], b * 128 + 16 * (c // RING + 1))
                    return c % RING

                def gate_up(u, b, part):
                    c = c0 + gate_place(u, b) + part
                    if part == 0:
                        at_least(pe, hid_done, b * 16 + (u0 + u - 1))
                    slot = landed(c, b)
                    for k in range(4):
                        mm = pe.matmul(PS[:, u % 2, 0:2 * P], XT[(u // EPG) % 2][:, 4 * part + k, :],
                                       ring[:, slot, k * 256:k * 256 + 256],
                                       start=(part == 0 and k == 0), stop=(part == 1 and k == 3))
                    mm.then_inc(w_used, 1)

                def turn_hidden(u, b):
                    pe.wait_ge(hid_done, b * 16 + (u0 + u + 1))
                    pe.transpose(PS[:, 2 + u % 2, 0:P], hidm[u % 2], ident[:]).then_inc(ht_ready, 1)

                def down(u, b):
                    slot = landed(c0 + down_place(u, b), b)
                    pe.wait_ge(ht_moved, b * 16 + (u0 + u + 1))
                    bank = 4 + 2 * ((u // EPG) % 2)
                    for h in range(2):
                        mm = pe.matmul(PS[:, bank + h, :], hidT[u % 2], ring[:, slot, h * 512:h * 512 + 512],
                                       start=(u % EPG == 0), stop=(u % EPG == EPG - 1))
                    mm.then_inc(w_used, 1)

                def turn_rows(i, b):
                    pe.wait_ge(xg_land[i % 2], b * 16 + 16 * ((g0 + i) // 2 + 1))
                    at_least(pe, y_act, b * 2 + (g0 + i - 1))
                    at_least(pe, y_dve, b * 2 + (g0 + i - 1))
                    for k in range(KT):
                        mm = pe.transpose(PS[:, 4 + 2 * (i % 2) + k // 4, (k % 4) * P:(k % 4) * P + P],
                                          xg[i % 2][:, k * P:k * P + P], ident[:])
                    mm.then_inc(xt_ready, 1)

                def tile_ready(i, b):
                    pe.wait_ge(xt_act, b * 2 + (g0 + i + 1))
                    pe.wait_ge(xt_dve, b * 2 + (g0 + i + 1))

                pe.wait_ge(x_ready, KT * (2 * layer + 1))
                for rt in range(NRT):
                    for k in range(KT):
                        mm = pe.matmul(PS[0:RT, 4, rt * 36:rt * 36 + 36], X[:, k, rt * RT:rt * RT + RT],
                                       wr[:, layer, k, :], start=(k == 0), stop=(k == KT - 1))
                mm.then_inc(lg_ready, 1)
                for n in range(2 * NRT):
                    if n == 6:
                        pe.wait_ge(rk_in, 16 * (1 + layer))
                        pe.wait_ge(og_ready, 1 + layer)
                        ranks = PS[0:RT, 5, 0:EGRP * (NRT + 1)].rearrange("p (t g) -> p t g", g=EGRP)
                        ones = onesD[0:RT, 0:RT]
                        pe.matmul(ranks, ones, OGX[0:RT, 0:NRT + 1], start=True, stop=False)
                        for d in range(2, NRT + 1):
                            pe.matmul(ranks[:, d:], ones, OGX[0:RT, 1:NRT + 2 - d], start=False, stop=False)
                        pe.matmul(ranks, RK[0:RT, RK_UP:RK_UP + RT], OGX[0:RT, 1:], start=False, stop=True
                                  ).then_inc(rank_ready, 1)
                    at_least(pe, xs_moved, 2 * NRT * layer + n - 3)
                    rt, h = divmod(n, 2)
                    for k in range(4):
                        mm = pe.transpose(PS[0:RT, n % 4, k * P:k * P + P],
                                          X[:, 4 * h + k, rt * RT:rt * RT + RT], ident[:])
                    mm.then_inc(xs_ready, 1)
                pe.wait_ge(oneh_ready, 1 + layer)
                for rt in range(NRT):
                    mm = pe.matmul(PS[:, 6, 0:SLOTS * (EPG + 1)], RONE[0:RT, rt, :],
                                   RHS[0:RT, rt].rearrange("p q e -> p (q e)"), start=(rt == 0), stop=(rt == NRT - 1))
                mm.then_inc(slots_mm, 1)

                def body(b):
                    for r in range(1, 17):
                        more = not (isinstance(b, int) and b == 3 and r == 16)
                        if more:
                            if r % 8 == 0:
                                tile_ready(r // 8, b)
                            gate_up(r, b, 0)
                        turn_hidden(r - 1, b)
                        if more:
                            gate_up(r, b, 1)
                        down(r - 1, b)
                        if r in (5, 13) and not (isinstance(b, int) and b == 3 and r == 13):
                            turn_rows((r + 3) // 8, b)

                turn_rows(0, 0)
                tile_ready(0, 0)
                gate_up(0, 0, 0)
                gate_up(0, 0, 1)
                body(0)
                with pe.Fori(1, 3) as b:
                    body(b)
                body(3)
                for rt in range(NRT):
                    pe.wait_ge(yg_land[rt], 16 * (1 + layer))
                    if rt >= 2:
                        pe.wait_ge(acc_done, 2 * (NRT * layer + rt - 1))
                    for k in range(KT):
                        mm = pe.transpose(PS[:, 2 * (rt % 2) + k // 4, (k % 4) * RT:(k % 4) * RT + RT],
                                          rows_tm[rt][0:RT, k * P:k * P + P], ident[0:RT, 0:RT])
                    mm.then_inc(fin_ready, 1)

            pe.wait_ge(gate_sig, 12)
            sample_mem(0)
            pe.wait_ge(dm_out, 1)
            prompt_attention(0)
            pe.wait_ge(mt_done, QT)
            pe.wait_ge(lru_done, 1)
            for c in range(C_OUT0, C_MOE0):
                fm_unit(c, MIX, both)
            norm(0)
            moe(0)
            norm(1)

            pe.wait_ge(x_ready, 2 * KT)
            for n in range(12):
                if n in (6, 7, 10, 11):
                    tm_unit(C_KV + n, X, tiles5, P)
                else:
                    fm_unit(C_KV + n, X, both)
            for n in range(8):
                fm_unit(C_INB + n, X, both)
            tm_unit(C_INB + 8, X, tiles5, 36)
            pe.wait_ge(w1q_in, 16)
            pe.wait_ge(z_done, 1)
            for kv in range(2):
                for n in range(16):
                    mm = pe.matmul(PS[:, 4 + 2 * kv, 0:GRP * NCP].rearrange("p (g c) -> p g c", g=GRP), w1q[:, kv, n, :],
                                   cmpZ[:, kv, :, n:n + 8 * (NCP - 1) + 1:8], start=(n == 0), stop=(n == 15))
                mm.then_inc(cp_h, 1)
            pe.wait_ge(cp_g, 1)
            for g2 in range(2):
                mm = pe.matmul(PS[64 * g2:64 * g2 + 64, 4, P:P + 2 * NCP], w2s[:, 0, :], hgp[:, 0, g2:GRP:2, :],
                               start=True, stop=True)
            mm.then_inc(cp_o, 1)
            pe.wait_ge(cp_g, 2)
            for g in range(GRP):
                mm = pe.matmul(PS[0:NCP, 5, P + g * 64:P + g * 64 + 64],
                               hgp[:, 1, g, :], w2s[:, 1, :],
                               start=True, stop=True)
            mm.then_inc(cp_o, 1)

            pe.wait_ge(cp_done, 2)
            sample_mem(1)
            pe.wait_ge(dm_out, 2)

            def qz(b, pair):
                return QZ[:, b * 192 + pair * 96:b * 192 + pair * 96 + ROWS]

            first, last = (0, 0), (B - 1, 1)
            for b in range(B):
                for pair in range(2):
                    mm = pe.matmul(PS[0:ROWS, 6, 0:NC], qz(b, pair), compK[:, b, pair, 0:NC],
                                   start=(b, pair) == first, stop=(b, pair) == last)
            mm.then_inc(dc_s, 1)
            for i, br in enumerate(("slc", "win")):
                for b in range(B):
                    for pair in range(2):
                        mm = pe.matmul(PS[0:ROWS, 5, i:i + 1], qz(b, pair), KT_[br][:, pair, T + b:T + b + 1],
                                       start=(b, pair) == first, stop=(b, pair) == last)
            for b in range(B):
                fill_landed(pe, F_SLCK + b)
                v = kv_buf(F_SLCK + b).rearrange("p (j a k) -> p j a k", j=PAGES, a=2)
                for pair in range(2):
                    for q4 in range(4):
                        mm = pe.matmul(PS[0:ROWS, q4, :], qz(b, pair), v[:, 4 * q4:4 * q4 + 4, pair, :],
                                       start=(b, pair) == first, stop=(b, pair) == last)
                mm.then_inc(kv_used, 1)
                if b == 1:
                    pe.wait_ge(dc_p, 1)
                    pe.transpose(PS[0:NC, 6, P:P + ROWS], Lc[0:ROWS, 0:NC], ident[0:ROWS, 0:ROWS]).then_inc(dc_t, 1)
                    pe.wait_ge(dc_sum, 1)
                    pe.matmul(PS[0:ROWS, 7, 0:NSB], S3[0:NC], cover[0:NC, :], start=True, stop=True
                              ).then_inc(dc_imp, 1)
            for b in range(B):
                if b % 4 == 0:
                    fill_landed(pe, F_WINK + b // 4)
                v = kv_buf(F_WINK + b // 4).rearrange("p (b j a k) -> p b j a k", b=4, j=4, a=2)[:, b % 4]
                for pair in range(2):
                    mm = pe.matmul(PS[0:ROWS, 4, :], qz(b, pair), v[:, :, pair, :],
                                   start=(b, pair) == first, stop=(b, pair) == last)
                if b % 4 == 3:
                    mm.then_inc(kv_used, 1)
            turns = ([(L96, P * t, P) for t in range(16)] + [(Lw, P * t, P) for t in range(4)] +
                     [(Lc, 0, NC), (L96, PAST, 1), (Lw, T, 1)])
            for t, (src, a, n) in enumerate(turns):
                if t == 0:
                    pe.wait_ge(ds_p, 1)
                if t == 16:
                    pe.wait_ge(ds_p, 2)
                mm = pe.transpose(PS[0:n, t // 5, (t % 5) * ROWS:(t % 5) * ROWS + ROWS], src[0:ROWS, a:a + n],
                                  ident[0:ROWS, 0:ROWS])
            mm.then_inc(ds_t, 1)
            pe.wait_ge(ds_pt, 1)

            def values(out, probs, v, b, start=False, stop=False):
                return pe.matmul(out, probs[:, b * NH:b * NH + NH], v, start=start, stop=stop)

            pe.wait_ge(vrow_in, 48)
            for b in range(B):
                if b % 4 == 0:
                    fill_landed(pe, F_WINV + b // 4)
                out = PS[0:NH, b // 2, (b % 2) * 256:(b % 2) * 256 + 256]
                values(out, PTd[0:NC, 4], compV[0:NC, b, :], b, start=True)
                for i in range(2):
                    values(out, PTd[0:1, 5 + i], vrow(i, b), b)
                v = kv_buf(F_WINV + b // 4).rearrange("p (b j x) -> p b j x", b=4, j=4)[:, b % 4]
                for t in range(4):
                    mm = values(out, PTd[:, t], v[:, t, :], b, stop=(t == 3))
                if b % 4 == 3:
                    mm.then_inc(kv_used, 1)

            def selected_values(b):
                fill_landed(pe, F_SLCV + b)
                at_least(pe, sv_added, b - 1)
                v = kv_buf(F_SLCV + b).rearrange("p (j x) -> p j x", j=PAGES)
                out = PS[0:NH, 7, (b % 2) * 256:(b % 2) * 256 + 256]
                for t in range(PAGES):
                    mm = values(out, PTs[:, t], v[:, t, :], b, start=(t == 0), stop=(t == PAGES - 1))
                mm.then_inc(kv_used, 1)

            def turn_samples():
                pe.wait_ge(sv_added, B)
                for n in range(2 * B):
                    mm = pe.matmul(PS[:, 7, n * NH:n * NH + NH], OS[0:NH, n * P:n * P + P], ident[0:NH, 0:NH],
                                   start=True, stop=True)
                mm.then_inc(os_turned, 1)

            pe.wait_ge(os_moved, 1)
            prompt_attention(1, selected_values)
            pe.wait_ge(mt_done, 3 * QT)
            pe.wait_ge(ds_out, 1)
            for c in range(C_OUT1, C_MOE1):
                fm_unit(c, MIX, both)
            norm(2)
            moe(1)
            norm(3)

        @block.scalar
        def _(act):
            act.dma_start(memT, dr["memT"]).then_inc(mem_in, 16)
            for dst, src in CONSTS:
                act.dma_start(dst, src).then_inc(const_in, 16)
            act.dma_start(w1p, dr["w1p"]).then_inc(w1_in, 16)

            def unit_ready(c):
                act.wait_ge(w_used, c + 1)
                return lin_bank(c)

            def move(out, in_, scale=1.0):
                return act.activation(out, in_, ACT.Copy, scale=scale)

            for c in range(8):
                bank = unit_ready(c)
                layer, kv, pair = c // 4, (c // 2) % 2, c % 2
                if kv == 0:
                    move(memK[:, layer, pair, :], PS[:, bank, 0:MEM]).then_inc(lin_act, 1)
                else:
                    move(memV[:, layer, :, pair * P:pair * P + P],
                         PS[:, bank, 0:MEM].rearrange("p (t x) -> p t x", t=2)).then_inc(lin_act, 1)
            act.wait_ge(lam_abs, 1)
            act.activation(sp8[:, 1, :], sp8[:, 0, :], ACT.Exp, scale=-1.0).then_inc(lam_exp, 1)

            def comp_p2(kv, u):
                act.wait_ge(cmp_ab, u + 1)
                at_least(act, hs_done, u - 1)
                act.activation(p2[kv], PS[:, 2 * kv + 1, :], ACT.Identity, bias=b1e[:, kv:kv + 1]).then_inc(p2_done, 1)

            def comp_gelu(kv, u):
                act.wait_ge(hs_done, u + 1)
                h = hsb[kv].rearrange("p (g c) -> p g c", g=4)[:, :, 0:NC]
                act.activation(h, h, ACT.Gelu_apprx_tanh).then_inc(hg_done, 1)

            act.wait_ge(tab_moved, 5)
            comp_p2(0, 0)
            comp_p2(1, 1)
            comp_gelu(0, 0)
            with act.Fori(0, 7) as i:
                for um in range(2):
                    act.wait_ge(cmp_ab, i * 2 + um + 3)
                    act.wait_ge(hs_done, i * 2 + um + 1)
                    act.activation(p2[um], PS[:, 2 * um + 1, :], ACT.Identity, bias=b1e[:, um:um + 1]
                                   ).then_inc(p2_done, 1)
                    comp_gelu((um + 1) % 2, i * 2 + um + 1)
            comp_gelu(1, 15)

            act.wait_ge(cmp_out, 16)
            for c in range(C_INA, C_OUT0):
                bank = unit_ready(c)
                src = PS[:, bank:bank + 2, 0:HALF]
                n = c - C_INA
                if n < 6:
                    act.activation(halves(gateT[:, n, :]), src, ACT.Gelu_apprx_tanh).then_inc(lin_act, 1)
                elif n < 12:
                    move(halves(xrT[:, n - 6, :]), src).then_inc(lin_act, 1)
                else:
                    move(halves(mq0[:, n - 12, :]), src, SCALE).then_inc(lin_act, 1)
            for n in range(12):
                act.wait_ge(gmm_done, n + 1)
                b0 = 4 + 2 * (n % 2)
                act.activation(halves((rT, iT)[n // 6][:, n % 6, :]), PS[:, b0:b0 + 2, 0:HALF], ACT.Sigmoid,
                               bias=pcol("brg" if n < 6 else "big", n % 6)).then_inc(gate_sig, 1)
            for t in range(RNN):
                act.wait_ge(la_done, t + 1)
                act.activation(xrT[:, t, :], rT[:, t, :], ACT.Exp)
                act.activation(rT[:, t, :], rT[:, t, :], ACT.Tanh).then_inc(at_done, 1)
            for t in range(RNN):
                act.wait_ge(u2_done, t + 1)
                act.activation(MIX[:, t, :], MIX[:, t, :], ACT.Sqrt, scale=-1.0).then_inc(sq_done, 1)

            def sample_mem(layer):
                act.wait_ge(dm_max, 1 + layer)
                act.activation(LM[layer][0:MROWS], PS[0:MROWS, 7, 0:MEM], ACT.Exp, bias=st[0:MROWS, 0:1],
                               accum_out=st[0:MROWS, 1:2]).then_inc(dm_exp, 1)

            def job_exp(j):
                act.wait_ge(max_done, j + 1)
                at_least(act, pt_ready, j - 1)
                nk = job_nk(j)
                src = PS[:, j % 2, 0:nk] if JOBS[j][2] == "mem" else Sb[j % 2][:, 0:nk]
                act.activation(Pb[j % 2][:, 0:nk], src, ACT.Exp, bias=jst[:, j % 4, 1:2],
                               accum_out=jst[:, j % 4, 2:3]).then_inc(exp_done, 1)

            def job_pt(j):
                act.wait_ge(pt_ready, j + 1)
                at_least(act, v_done, j - 1)
                n, w = min(P, job_nk(j)), P * job_tiles(j)
                move(PTb[j % 2][0:n, 0:w], PS[0:n, 2 + j % 2, 0:w]).then_inc(pt_done, 1)

            def mix_move(layer, qt):
                qs = slice(qt * P, qt * P + P)
                if layer == 0:
                    act.wait_ge(mt_ready, qt + 1)
                    move(MIX[:, 6:8, qs], PS[:, 6, 0:MEM].rearrange("p (t x) -> p t x", t=2)).then_inc(mt_done, 1)
                else:
                    for i in range(2):
                        act.wait_ge(mt_ready, turns_before(layer, qt) + i + 1)
                        move(MIX[:, 4 * i:4 * i + 4, qs], PS[:, 6, :].rearrange("p (t x) -> p t x", t=4)
                             ).then_inc(mt_done, 1)

            def prompt_attention(layer):
                js = L_JOBS[layer]
                for j in range(js.start, js.stop + 4):
                    if j in js:
                        job_exp(j)
                    if j - 1 in js:
                        job_pt(j - 1)
                    if j - 4 in js and j - 4 in LASTS:
                        mix_move(*LASTS[j - 4])

            def norm(n):
                for hf, (a, m) in enumerate(both):
                    act.wait_ge(xm_ready, 2 * n + hf + 1)
                    act.activation(MIX[:, :, a:a + m], R[:, :, a:a + m], ACT.Square).then_inc(sqr_ready, 1)
                for hf, (a, m) in enumerate(both):
                    act.wait_ge(ve_ready, 2 * n + hf + 1)
                    act.activation(rs[:, a:a + m], rs[:, a:a + m], ACT.Sqrt).then_inc(std_ready, 1)
                act.wait_ge(nrm_ready, 2 * n + 2)
                g, b = ("ln2g", "ln2b") if n % 2 else ("ln1g", "ln1b")
                for k in range(KT):
                    act.activation(X[:, k, :], R[:, k, :], ACT.Identity, bias=pcol(b, 8 * (n // 2) + k),
                                   scale=pcol(g, 8 * (n // 2) + k)).then_inc(x_ready, 1)

            def moe(layer):
                c0, u0, g0 = C_MOE[layer], UNITS * layer, SLOTS * layer
                for n in range(2 * NRT):
                    act.wait_ge(xs_ready, 2 * NRT * layer + n + 1)
                    rt, h = divmod(n, 2)
                    move(rows_tm[rt][0:RT, h * 512:h * 512 + 512], PS[0:RT, n % 4, :]).then_inc(xs_moved, 1)
                    if n == 5:
                        act.wait_ge(rmax_ready, 1 + layer)
                        act.activation(TG[0:RT], TG[0:RT], ACT.Exp)
                        act.activation(SC[0:RT, 4, :], SC[0:RT, 3, :], ACT.Exp).then_inc(rexp_ready, 1)

                def silu(u, b):
                    act.wait_ge(w_used, b * 48 + (c0 + gate_place(u, b) + 2))
                    at_least(act, hid_done, b * 16 + (u0 + u - 1))
                    act.activation(sg[u % 2], PS[:, u % 2, 0:P], ACT.Silu).then_inc(sg_done, 1)

                def rows_turned(i, b):
                    act.wait_ge(xt_ready, b * 2 + (g0 + i + 1))
                    move(XT[i % 2][:, 0:4, :], PS[:, 4 + 2 * (i % 2), :].rearrange("p (k t) -> p k t", k=4)
                         ).then_inc(xt_act, 1)

                def output(i, b):
                    act.wait_ge(w_used, b * 48 + (c0 + down_place(EPG * i + EPG - 1, b) + 1))
                    at_least(act, y_stored[i % 2], b * 16 + 16 * ((g0 + i) // 2))
                    move(ytm[i % 2][:, 0:512], PS[:, 4 + 2 * (i % 2), :]).then_inc(y_act, 1)

                def body(b):
                    last = isinstance(b, int) and b == 3
                    for r in range(1, 17):
                        if not (last and r == 16):
                            silu(r, b)
                        if r in (5, 13) and not (last and r == 13):
                            rows_turned((r + 3) // 8, b)
                        if r % 8 == 0:
                            output(r // 8 - 1, b)

                rows_turned(0, 0)
                silu(0, 0)
                body(0)
                with act.Fori(1, 3) as b:
                    body(b)
                body(3)

            sample_mem(0)
            prompt_attention(0)
            norm(0)
            moe(0)
            norm(1)

            for n in range(12):
                bank = unit_ready(C_KV + n)
                br, kv, pair = n // 4, (n // 2) % 2, n % 2
                src = PS[:, bank:bank + 2, 0:HALF]
                if br == 0:
                    move(halves(cmpT[:, kv, pair, :]), src).then_inc(lin_act, 1)
                elif kv == 0:
                    move(halves(KT_[("", "slc", "win")[br]][:, pair, :]), src).then_inc(lin_act, 1)
                else:
                    v = VT_[("", "slc", "win")[br]]
                    move(v[:, 0:QT, pair * P:pair * P + P], PS[:, bank, :].rearrange("p (t x) -> p t x", t=QT))
                    move(v[0:B, QT, pair * P:pair * P + P], PS[0:B, bank + 1, 0:P]).then_inc(lin_act, 1)
            for n in range(8):
                bank = unit_ready(C_INB + n)
                dst = qT[:, n, :] if n < 6 else mq1[:, n - 6, :]
                move(halves(dst), PS[:, bank:bank + 2, 0:HALF], SCALE).then_inc(lin_act, 1)
            bank = unit_ready(C_INB + 8)
            act.activation(gates[:, 0:QT, :], PS[:, bank, :].rearrange("p (t x) -> p t x", t=QT)[:, :, 0:36],
                           ACT.Sigmoid)
            act.activation(gates[0:B, QT, :], PS[0:B, bank + 1, 0:36], ACT.Sigmoid).then_inc(lin_act, 1)
            lin_moved(act, lin_index[C_INB + 8] + 1)
            act.dma_start(dr["gd"], gates[0:B, QT, :]).then_inc(g_stored, 16)
            for kv in range(2):
                act.wait_ge(cp_h, kv + 1)
                act.activation(hgp[:, kv].rearrange("p g c -> p (g c)"), PS[:, 4 + 2 * kv, 0:GRP * NCP],
                               ACT.Gelu_apprx_tanh, bias=b1e[:, kv:kv + 1]).then_inc(cp_g, 1)
            act.wait_ge(g_stored, 16)
            act.dma_start(g96[0:ROWS], dr["gd"].rearrange("b (h x) -> (b h) x", x=3)).then_inc(g96_in, 16)
            sample_mem(1)
            act.wait_ge(pages_in, 16)
            half_fill(act, F_SLCK, 1)
            half_fill(act, F_SLCK + 1, 1)
            act.wait_ge(dc_max, 1)
            act.activation(Lc[0:ROWS, 0:NC], Lc[0:ROWS, 0:NC], ACT.Exp, bias=st[0:ROWS, 4:5],
                           accum_out=st[0:ROWS, 5:6]).then_inc(dc_exp, 1)
            for f in range(F_SLCK + 2, F_SLCK + B):
                half_fill(act, f, 1)
            act.wait_ge(ds_max, 1)
            act.activation(L96[0:ROWS, 0:PAST + 1], L96[0:ROWS, 0:PAST + 1], ACT.Exp, bias=st[0:ROWS, 8:9],
                           accum_out=st[0:ROWS, 9:10]).then_inc(ds_exp, 1)
            act.wait_ge(ds_max, 2)
            act.activation(Lw[0:ROWS, 0:T + 1], Lw[0:ROWS, 0:T + 1], ACT.Exp, bias=st[0:ROWS, 12:13],
                           accum_out=st[0:ROWS, 13:14]).then_inc(ds_exp, 1)
            prompt_attention(1)
            norm(2)
            moe(1)
            norm(3)

        @block.vector
        def _(dve):
            chain = [0]

            def link(ins):
                chain[0] += 1
                ins.then_inc(dve_chain, 1)
                dve.wait_ge(dve_chain, chain[0])

            dve.memset(onesD[:], 1.0 / D).then_inc(memset_done, 1)
            dve.memset(tabx[32:33, :], NEG).then_inc(memset_done, 1)
            dve.wait_ge(const_in, 16 * len(CONSTS))
            lam = pcol("lam", 0, 6)
            s = [sp8[:, i, :] for i in range(6)]
            link(dve.tensor_scalar(s[2], lam, -1.0, None, ALU.mult))
            dve.tensor_tensor(s[0], lam, s[2], ALU.max).then_inc(lam_abs, 1)
            dve.wait_ge(tab_ready, 1)
            dve.tensor_copy(rrow[:, 0:512], PS[0:NH, 4, 0:512])
            dve.tensor_copy(rrow[:, 512:640], PS[0:NH, 5, 0:128]).then_inc(tab_moved, 1)
            dve.wait_ge(tab_ready, 2)
            dve.tensor_copy(bias96[0:ROWS, PAST:PAST + 1], PS[0:ROWS, 6, 0:1]).then_inc(tab_moved, 1)
            dve.wait_ge(tab_ready, 3)
            dve.tensor_copy(bias96[0:ROWS, 0:PAST].rearrange("p (a b) -> p a b", a=4), PS[0:ROWS, 0:4, :]
                            ).then_inc(tab_moved, 1)
            dve.wait_ge(tab_ready, 4)
            dve.tensor_copy(cmpB[:, 0:28].rearrange("p n h -> p (n h)"), PS[:, 0, 0:28 * NH])
            dve.tensor_copy(cmpB[:, 28:].rearrange("p n h -> p (n h)"), PS[:, 1, 0:(NREL - 28) * NH]
                            ).then_inc(tab_moved, 1)
            dve.wait_ge(tab_ready, 5)
            dve.tensor_tensor(b1e[:], PS[:, 5, 0:2], pcol("b1", 0, 2), ALU.add).then_inc(tab_moved, 1)

            dve.wait_ge(lam_exp, 1)
            link(dve.tensor_scalar(s[3], s[1], 2.0, None, ALU.add))
            link(dve.reciprocal(s[4], s[3]))
            link(dve.tensor_tensor(s[3], s[1], s[4], ALU.mult))
            link(dve.tensor_tensor(s[4], s[3], s[3], ALU.mult))
            link(dve.tensor_scalar(s[5], s[4], 1.0 / 17, None, ALU.mult))
            for k in range(7, 0, -1):
                link(dve.scalar_tensor_tensor(out=s[5], in0=s[5], scalar=1.0 / (2 * k + 1), in1=s[4],
                                              op0=ALU.add, op1=ALU.mult))
            link(dve.scalar_tensor_tensor(out=s[5], in0=s[5], scalar=1.0, in1=s[3], op0=ALU.add, op1=ALU.mult))
            link(dve.tensor_scalar(s[2], s[2], 0.0, None, ALU.max))
            link(dve.scalar_tensor_tensor(out=s[5], in0=s[5], scalar=2.0, in1=s[2], op0=ALU.mult, op1=ALU.add))
            link(dve.tensor_scalar(s[5], s[5], -8.0, None, ALU.mult))

            def comp_hs(kv, u):
                dve.wait_ge(p2_done, u + 1)
                at_least(dve, cmp_w2, u - 1)
                a = PS[:, 2 * kv, :].rearrange("p (g c) -> p g c", g=4)
                b = p2[kv].rearrange("p (g c) -> p g c", g=4)
                h = hsb[kv].rearrange("p (g c) -> p g c", g=4)
                dve.tensor_tensor(h[:, :, 0:NC], a[:, :, 0:NC], b[:, :, 1:NC + 1], ALU.add).then_inc(hs_done, 1)

            def comp_out(kv, u, b):
                dve.wait_ge(cmp_w2, u + 1)
                if kv == 0:
                    dve.tensor_copy(compK[:, bass.ds(b, 1), :, 0:NC].rearrange("p o a c -> p (o a) c"),
                                    PS[:, 6, 0:2 * P].rearrange("p (a c) -> p a c", a=2)[:, :, 0:NC]
                                    ).then_inc(cmp_out, 1)
                else:
                    dve.tensor_copy(compV[0:NC, bass.ds(b, 1), :].rearrange("p o x -> p (o x)"),
                                    PS[0:NC, 7, 0:256]).then_inc(cmp_out, 1)

            comp_hs(0, 0)
            comp_hs(1, 1)
            comp_out(0, 0, 0)
            with dve.Fori(1, 8) as i:
                comp_hs(0, i * 2)
                comp_out(1, i * 2 - 1, i - 1)
                comp_hs(1, i * 2 + 1)
                comp_out(0, i * 2, i)
            comp_out(1, 15, 7)

            for t in range(RNN):
                lin_moved(dve, lin_index[C_INA] + 7 + t)
                w = [pcol("cw", k * 6 + t) for k in range(4)]
                sx = pcol("st", t * 24, 24).rearrange("p (k b) -> p k b", k=3)
                link(dve.tensor_scalar(xcT[:, t, :], xrT[:, t, :], w[3], pcol("cb", t), ALU.mult, ALU.add))
                dve.tensor_copy(xtail[:, t, :], xrT[:, t, T - 3:TOK])
                for k in range(3):
                    d = 3 - k
                    dve.scalar_tensor_tensor(out=xcT[:, t, T:TOK], in0=sx[:, k, :], scalar=w[k],
                                             in1=xcT[:, t, T:TOK], op0=ALU.mult, op1=ALU.add).then_inc(dve_chain, 1)
                    chain[0] += 1
                    link(dve.scalar_tensor_tensor(out=xcT[:, t, d:T], in0=xrT[:, t, 0:T - d], scalar=w[k],
                                                  in1=xcT[:, t, d:T], op0=ALU.mult, op1=ALU.add)) if k < 2 else \
                        dve.scalar_tensor_tensor(out=xcT[:, t, d:T], in0=xrT[:, t, 0:T - d], scalar=w[k],
                                                 in1=xcT[:, t, d:T], op0=ALU.mult, op1=ALU.add).then_inc(conv_done, 1)

            def sample_queries(layer):
                z, q = QZM[layer], (mq0, mq1)[layer]
                link(dve.memset(z, 0.0))
                for h2 in range(2):
                    r0 = 64 * h2
                    for pair in range(2):
                        v = z[r0:r0 + 64].rearrange("p (b x) -> p b x", x=68)
                        ins = dve.tensor_copy(v[:, :, pair * 34 + h2:pair * 34 + h2 + 1],
                                              q[r0:r0 + 64, pair, T:TOK].rearrange("p (b o) -> p b o", o=1))
                return ins

            def sample_mem(layer):
                L = LM[layer][0:MROWS]
                dve.wait_ge(kv_used, 4 * layer + 2)
                dve.tensor_reduce(st[0:MROWS, 0:1], PS[0:MROWS, 7, 0:MEM], AX.X, ALU.max, negate=True
                                  ).then_inc(dm_max, 1)
                dve.wait_ge(dm_exp, 1 + layer)
                link(dve.reciprocal(st[0:MROWS, 2:3], st[0:MROWS, 1:2]))
                dve.tensor_scalar(L, L, st[0:MROWS, 2:3], None, ALU.mult).then_inc(dm_p, 1)
                dve.wait_ge(dm_t, 1 + layer)
                dve.tensor_copy(PTM[layer], PS[:, 7, MEM:MEM + 64].rearrange("p (t x) -> p t x", t=2)
                                ).then_inc(dm_pt, 1)
                dve.wait_ge(kv_used, 4 * layer + 4)
                for h2 in range(2):
                    r0 = 64 * h2
                    v = PS[r0:r0 + 64, 6, 0:MROWS].rearrange("p (b a x) -> p a b x", a=2, x=2)
                    ins = dve.tensor_copy(MIX[r0:r0 + 64, 6:8, T:TOK], v[:, :, :, h2])
                ins.then_inc(dm_out, 1)

            def job_max(j):
                layer, qt, br, h = JOBS[j]
                dve.wait_ge(s_done, j + 1)
                at_least(dve, exp_done, j - 1)
                nk, sj = job_nk(j), jst[:, j % 4]
                if br == "mem":
                    dve.tensor_reduce(sj[:, 1:2], PS[:, j % 2, 0:nk], AX.X, ALU.max, negate=True).then_inc(max_done, 1)
                    return
                bias = cmpB[:, 8 * (QT - 1 - qt):8 * (QT - 1 - qt) + NCP, h] if br == "cmp" else TH[:, h, T - nk:T]
                link(dve.tensor_tensor_reduce(out=Sb[j % 2][:, 0:nk], in0=PS[:, j % 2, 0:nk], in1=bias, scale=1.0,
                                              scalar=-3.0e38, op0=ALU.add, op1=ALU.max, accum_out=sj[:, 0:1]))
                dve.tensor_scalar(sj[:, 1:2], sj[:, 0:1], -1.0, None, ALU.mult).then_inc(max_done, 1)

            def job_out(j):
                layer, qt, br, h = JOBS[j]
                dve.wait_ge(v_done, j + 1)
                sj = jst[:, j % 4]
                link(dve.reciprocal(sj[:, 3:4], sj[:, 2:3]))
                coef = sj[:, 3:4]
                if br != "mem":
                    n = 3 * h + ("cmp", "slc", "win").index(br)
                    coef = sj[:, 4:5]
                    if br == "cmp" and qt == 0:
                        link(dve.tensor_scalar(coef, sj[:, 3:4], gates[:, qt, n:n + 1], pcol("valid", 0),
                                               ALU.mult, ALU.mult))
                    else:
                        link(dve.tensor_scalar(coef, sj[:, 3:4], gates[:, qt, n:n + 1], None, ALU.mult))
                if j == L_JOBS[layer].start or j - 1 in LASTS:
                    at_least(dve, mt_ready, turns_before(layer, max(qt - 1, 0)))
                out = mixTM[qt % 2][:, job_column(j):job_column(j) + 64]
                o = PS[:, 4 + j % 2, 0:64]
                if br in ("mem", "cmp"):
                    dve.tensor_scalar(out, o, coef, None, ALU.mult).then_inc(o_done, 1)
                else:
                    dve.wait_ge(o_done, j)
                    dve.scalar_tensor_tensor(out=out, in0=o, scalar=coef, in1=out, op0=ALU.mult, op1=ALU.add
                                             ).then_inc(o_done, 1)

            def prompt_attention(layer, add_values=None):
                js = L_JOBS[layer]
                for j in range(js.start, js.stop + 2):
                    if add_values and j - 2 in VALUE_JOBS:
                        add_values(VALUE_JOBS.index(j - 2))
                    if j in js:
                        job_max(j)
                    if j - 2 in js:
                        job_out(j - 2)

            def out_units(c0):
                for m in range(KT):
                    dve.wait_ge(w_used, c0 + m + 1)
                    bank = lin_bank(c0 + m)
                    dve.scalar_tensor_tensor(out=halves(R[:, m, :]), in0=halves(X[:, m, :]), scalar=ALPHA,
                                             in1=PS[:, bank:bank + 2, 0:HALF], op0=ALU.mult, op1=ALU.add
                                             ).then_inc(lin_dve, 1)

            def norm(n):
                for hf, (a, m) in enumerate(both):
                    dve.wait_ge(mu_ready, 2 * n + hf + 1)
                    dve.tensor_tensor(R[:, :, a:a + m], R[:, :, a:a + m], bcast(PS[:, 4 + hf, 0:m], 0, KT),
                                      ALU.subtract).then_inc(xm_ready, 1)
                for hf, (a, m) in enumerate(both):
                    dve.wait_ge(var_ready, 2 * n + hf + 1)
                    dve.tensor_scalar(rs[:, a:a + m], PS[:, 6 + hf, 0:m], EPS, None, ALU.add).then_inc(ve_ready, 1)
                dve.wait_ge(xm_ready, 2 * n + 2)
                for hf, (a, m) in enumerate(both):
                    dve.wait_ge(std_ready, 2 * n + hf + 1)
                    link(dve.reciprocal(rs[:, a:a + m], rs[:, a:a + m]))
                    dve.tensor_tensor(R[:, :, a:a + m], R[:, :, a:a + m], bcast(rs[:, a:a + m], 0, KT),
                                      ALU.mult).then_inc(nrm_ready, 1)

            def router(layer):
                rampg = bcast(rowc[0:RT, 2 * NSB:2 * NSB + EGRP], 0, NRT)
                ramp8 = bcast(rowc[0:RT, 2 * NSB + EGRP:ROWC], 0, NRT)
                dve.wait_ge(lg_ready, 1 + layer)
                lg = LG[0:RT]
                sc = [SC[0:RT, i, :] for i in range(12)]
                og, tg, le, o1, o2, t8 = OG[0:RT], TG[0:RT], LE[0:RT], O1[0:RT], O2[0:RT], T8[0:RT]
                link(dve.tensor_tensor(lg, PS[0:RT, 4, 0:NRT * 36].rearrange("p (t x) -> p t x", t=NRT),
                                       bcast(rb[0:RT, layer, :], 0, NRT), ALU.add))

                def top(vals, width, ramp, onehot, tmp, mx, mr):
                    link(dve.tensor_reduce(mx, vals, AX.X, ALU.max))
                    link(dve.tensor_tensor(tmp, vals, bcast(mx, 1, width), ALU.is_equal))
                    link(dve.tensor_tensor(tmp, tmp, ramp, ALU.mult))
                    link(dve.tensor_reduce(mr, tmp, AX.X, ALU.max))
                    link(dve.tensor_tensor(onehot, tmp, bcast(mr, 1, width), ALU.is_equal))

                top(lg[:, :, 0:EGRP], EGRP, rampg, og, tg, sc[0], sc[1])
                dve.memset(OGX[0:RT, 0], 0.0)
                dve.memset(OGX[0:RT, NRT + 1], 0.0)
                dve.tensor_copy(OGX[0:RT, 1:NRT + 1], og).then_inc(og_ready, 1)
                lex = lg[:, :, EGRP:36].rearrange("p t (g e) -> p t g e", g=EGRP)
                m1 = M1[0:RT]
                link(dve.tensor_tensor(m1, lex, bcast(og, 2, EPG), ALU.mult))
                link(dve.tensor_reduce(le, m1.rearrange("p t g e -> p t e g"), AX.X, ALU.add))
                top(le, EPG, ramp8, o1, t8, sc[2], sc[1])
                link(dve.scalar_tensor_tensor(out=le, in0=o1, scalar=NEG, in1=le, op0=ALU.mult, op1=ALU.add))
                top(le, EPG, ramp8, o2, t8, sc[5], sc[1])
                link(dve.tensor_tensor(sc[3], sc[5], sc[2], ALU.subtract))
                dve.tensor_tensor(tg, lg[:, :, 0:EGRP], bcast(sc[0], 1, EGRP), ALU.subtract).then_inc(rmax_ready, 1)
                dve.wait_ge(rexp_ready, 1 + layer)
                link(dve.tensor_reduce(sc[6], tg, AX.X, ALU.add))
                link(dve.reciprocal(sc[7], sc[6]))
                link(dve.tensor_scalar(sc[8], sc[4], 1.0, None, ALU.add))
                link(dve.reciprocal(sc[9], sc[8]))
                link(dve.tensor_tensor(sc[10], sc[9], sc[7], ALU.mult))
                link(dve.tensor_tensor(sc[11], sc[10], sc[4], ALU.mult))
                link(dve.tensor_tensor(o1, o1, bcast(sc[10], 1, EPG), ALU.mult))
                link(dve.tensor_tensor(o2, o2, bcast(sc[11], 1, EPG), ALU.mult))
                dve.wait_ge(rk_in, 16 * (1 + layer))
                v9, w5 = V9[0:RT], [W5[0:RT, i, :] for i in range(6)]
                link(dve.tensor_tensor(v9[:, :, 0:EPG], o1, o2, ALU.add))
                link(dve.tensor_copy(v9[:, :, EPG], RK[0:RT, RK_TOK:RK_TOK + NRT]))
                dve.wait_ge(rank_ready, 1 + layer)
                ng, base = NG[0:RT, 0, :], NG[0:RT, 1, :]
                link(dve.tensor_scalar(ng, PS[0:RT, 5, EGRP * NRT:EGRP * NRT + EGRP], float(D), None, ALU.mult))
                link(dve.tensor_tensor(N5[0:RT], bcast(ng, 1, 5), bcast(RK[0:RT, RK_T5:RK_T5 + 5], 0, EGRP),
                                       ALU.is_gt))
                link(dve.tensor_reduce(ng, N5[0:RT], AX.X, ALU.add))
                link(dve.memset(base[:, 0:1], 0.0))
                for g in range(EGRP - 1):
                    link(dve.tensor_tensor(base[:, g + 1:g + 2], base[:, g:g + 1], ng[:, g:g + 1], ALU.add))
                t20 = T20[0:RT]
                link(dve.scalar_tensor_tensor(out=t20, in0=PS[0:RT, 5, 0:EGRP * NRT].rearrange(
                    "p (t g) -> p t g", g=EGRP), scalar=float(D), in1=og, op0=ALU.mult, op1=ALU.mult))
                link(dve.tensor_reduce(w5[0], t20, AX.X, ALU.add))
                link(dve.tensor_tensor(t20, bcast(w5[0], 1, 4), bcast(RK[0:RT, RK_T4:RK_T4 + 4], 0, NRT), ALU.is_ge))
                link(dve.tensor_reduce(w5[1], t20, AX.X, ALU.add))
                link(dve.scalar_tensor_tensor(out=w5[2], in0=w5[1], scalar=-float(P), in1=w5[0],
                                              op0=ALU.mult, op1=ALU.add))
                link(dve.tensor_tensor(t20, og, bcast(base, 0, NRT), ALU.mult))
                link(dve.tensor_reduce(w5[3], t20, AX.X, ALU.add))
                link(dve.tensor_tensor(w5[3], w5[3], w5[1], ALU.add))
                link(dve.tensor_tensor(QONE[0:RT], bcast(RK[0:RT, RK_8:RK_8 + 8], 0, NRT), bcast(w5[3], 1, SLOTS),
                                       ALU.is_equal))
                dve.tensor_tensor(RONE[0:RT], bcast(RK[0:RT, RK_128:RK_128 + P], 0, NRT), bcast(w5[2], 1, P),
                                  ALU.is_equal)
                dve.tensor_tensor(RHS[0:RT], bcast(QONE[0:RT], 2, EPG + 1), bcast(v9, 1, SLOTS), ALU.mult
                                  ).then_inc(oneh_ready, 1)
                link(dve.scalar_tensor_tensor(out=w5[4], in0=w5[3], scalar=float(P), in1=w5[2],
                                              op0=ALU.mult, op1=ALU.add))
                dve.tensor_copy(slot_i[0:RT], w5[4])
                link(dve.tensor_tensor(TG3[0:1], bcast(RK[0:1, RK_8:RK_8 + 8], 1, 3), bcast(NG[0:1, 1, 1:4], 0, SLOTS),
                                       ALU.is_ge))
                link(dve.tensor_reduce(TGF[0:1], TG3[0:1], AX.X, ALU.add))
                dve.tensor_scalar(place_i[:], TGF[0:1], float(3 * EPG), float(D_MOE[layer]), ALU.mult, ALU.add)
                dve.wait_ge(slots_mm, 1 + layer)
                link(dve.tensor_copy(CP, PS[:, 6, 0:SLOTS * (EPG + 1)]))
                dve.tensor_copy(tok_i[:], CP.rearrange("p (q e) -> p q e", e=EPG + 1)[:, :, EPG]
                                ).then_inc(slots_ready, 1)

            def moe(layer):
                c0, u0, g0 = C_MOE[layer], UNITS * layer, SLOTS * layer

                def hidden(u, b):
                    dve.wait_ge(sg_done, b * 16 + (u0 + u + 1))
                    at_least(dve, ht_ready, b * 16 + (u0 + u - 1))
                    w = (u // EPG) * (EPG + 1) + u % EPG
                    dve.scalar_tensor_tensor(out=hidm[u % 2], in0=sg[u % 2], scalar=CP[:, bass.ds(b * 18 + w, 1)],
                                             in1=PS[:, u % 2, P:2 * P], op0=ALU.mult, op1=ALU.mult
                                             ).then_inc(hid_done, 1)

                def hidden_turned(u, b):
                    dve.wait_ge(ht_ready, b * 16 + (u0 + u + 1))
                    dve.tensor_copy(hidT[u % 2], PS[:, 2 + u % 2, 0:P]).then_inc(ht_moved, 1)

                def rows_turned(i, b):
                    dve.wait_ge(xt_ready, b * 2 + (g0 + i + 1))
                    dve.tensor_copy(XT[i % 2][:, 4:8, :], PS[:, 5 + 2 * (i % 2), :].rearrange("p (k t) -> p k t", k=4)
                                    ).then_inc(xt_dve, 1)

                def output(i, b):
                    dve.wait_ge(w_used, b * 48 + (c0 + down_place(EPG * i + EPG - 1, b) + 1))
                    at_least(dve, y_stored[i % 2], b * 16 + 16 * ((g0 + i) // 2))
                    dve.tensor_copy(ytm[i % 2][:, 512:1024], PS[:, 5 + 2 * (i % 2), :]).then_inc(y_dve, 1)

                def body(b):
                    last = isinstance(b, int) and b == 3
                    for r in range(1, 17):
                        hidden_turned(r - 1, b)
                        if not (last and r == 16):
                            hidden(r, b)
                        if r in (5, 13) and not (last and r == 13):
                            rows_turned((r + 3) // 8, b)
                        if r % 8 == 0:
                            output(r // 8 - 1, b)
                        if isinstance(b, int) and b == 0 and r <= KT:
                            ins = dve.tensor_scalar(R[:, r - 1, :], X[:, r - 1, :], ALPHA, None, ALU.mult)
                            if r == KT:
                                link(ins)

                rows_turned(0, 0)
                hidden(0, 0)
                body(0)
                with dve.Fori(1, 3) as b:
                    body(b)
                body(3)
                for rt in range(NRT):
                    dve.wait_ge(fin_ready, NRT * layer + rt + 1)
                    for h in range(2):
                        v = R[:, 4 * h:4 * h + 4, rt * RT:rt * RT + RT]
                        dve.tensor_tensor(v, v, PS[:, 2 * (rt % 2) + h, 0:4 * RT].rearrange("p (k t) -> p k t", k=4),
                                          ALU.add).then_inc(acc_done, 1)

            lin_moved(dve, lin_index[C_OUT0])
            sample_queries(0).then_inc(qz_done, 1)
            for t in range(RNN):
                dve.wait_ge(gate_sig, t + 1)
                dve.tensor_scalar(rT[:, t, :], rT[:, t, :], sp8[:, 5, t:t + 1], None, ALU.mult).then_inc(la_done, 1)
            for t in range(RNN):
                dve.wait_ge(at_done, t + 1)
                u = MIX[:, t, :]
                link(dve.tensor_tensor(u, xrT[:, t, :], xrT[:, t, :], ALU.mult))
                link(dve.scalar_tensor_tensor(out=u, in0=u, scalar=1.0, in1=rT[:, t, :], op0=ALU.add, op1=ALU.mult))
                dve.tensor_scalar(u, u, -1.0e-34, None, ALU.min).then_inc(u2_done, 1)
            dve.wait_ge(gate_sig, 12)
            for t in range(RNN):
                link(dve.tensor_tensor(iT[:, t, :], iT[:, t, :], xcT[:, t, :], ALU.mult))
                dve.wait_ge(sq_done, t + 1)
                link(dve.tensor_tensor(iT[:, t, :], iT[:, t, :], MIX[:, t, :], ALU.mult))
                h0 = pcol("h0", t * 8, 8)
                link(dve.tensor_tensor_scan(rT[:, t, 0:T], xrT[:, t, 0:T], iT[:, t, 0:T], 0.0, ALU.mult, ALU.add))
                link(dve.tensor_tensor(rT[:, t, T:TOK], xrT[:, t, T:TOK], h0, ALU.mult))
                link(dve.tensor_tensor(rT[:, t, T:TOK], rT[:, t, T:TOK], iT[:, t, T:TOK], ALU.add))
                ins = dve.tensor_tensor(MIX[:, t, :], gateT[:, t, :], rT[:, t, :], ALU.mult)
            ins.then_inc(lru_done, 1)
            sample_mem(0)
            prompt_attention(0)
            out_units(C_OUT0)
            norm(0)
            dve.wait_ge(x_ready, KT)
            dve.wait_ge(stores, 16 * 6)
            router(0)
            moe(0)
            norm(1)

            lin_moved(dve, lin_index[C_KV] + 4)
            dve.wait_ge(x_ready, 2 * KT)
            for g2 in range(2):
                for odd in range(2):
                    for kv in range(2):
                        ins = dve.tensor_copy(cmpZ[64 * odd:64 * odd + 64, kv, g2:GRP:2, :],
                                              cmpT[64 * g2:64 * g2 + 64, kv, :, odd:T:2])
            ins.then_inc(z_done, 1)
            dve.wait_ge(cp_o, 1)
            dve.tensor_copy(kcT, PS[:, 4, P:P + 2 * NCP].rearrange("p (a c) -> p a c", a=2)).then_inc(cp_done, 1)
            dve.wait_ge(cp_o, 2)
            dve.tensor_copy(vcp[0:NCP], PS[0:NCP, 5, P:P + 256]).then_inc(cp_done, 1)
            lin_moved(dve, lin_index[C_OUT1])
            link(dve.memset(QZ, 0.0))
            for g2 in range(2):
                r0 = 64 * g2
                v = QZ[r0:r0 + 64].rearrange("p (b x) -> p b x", x=204)
                for pair in range(2):
                    a = pair * 102 + g2 * HPG
                    dve.tensor_copy(v[:, :, a:a + HPG],
                                    qT[r0:r0 + 64, pair * HPG:pair * HPG + HPG, T:TOK].rearrange("p h b -> p b h"))
            sample_queries(1).then_inc(qz_done, 1)
            dve.wait_ge(stores, 16 * 13)
            sample_mem(1)
            dve.wait_ge(dc_s, 1)
            r = slice(0, ROWS)
            s1 = lambda i: st[r, i:i + 1]
            link(dve.tensor_tensor(Lc[r, 0:NC], PS[r, 6, 0:NC], bias96[0:ROWS, 31:31 + 16 * (NC - 1) + 1:16], ALU.add))
            dve.tensor_reduce(s1(4), Lc[r, 0:NC], AX.X, ALU.max, negate=True).then_inc(dc_max, 1)
            dve.wait_ge(dc_exp, 1)
            link(dve.reciprocal(s1(6), s1(5)))
            dve.tensor_scalar(Lc[r, 0:NC], Lc[r, 0:NC], s1(6), None, ALU.mult).then_inc(dc_p, 1)
            dve.wait_ge(dc_t, 1)
            link(dve.tensor_reduce(st[0:NC, 16:48], PS[0:NC, 6, P:P + ROWS].rearrange("p (r h) -> p r h", h=HPG),
                                   AX.X, ALU.add))
            dve.tensor_copy(S3[0:NC].rearrange("p (r h) -> p r h", h=HPG), bcast(st[0:NC, 16:48], 1, HPG)
                            ).then_inc(dc_sum, 1)
            dve.wait_ge(g96_in, 16)
            dve.tensor_scalar(Lc[r, 0:NC], Lc[r, 0:NC], g96[r, 0:1], None, ALU.mult)
            dve.wait_ge(dc_imp, 1)
            dve.wait_ge(tri_in, 16)
            score, sel = SEL[r, 0, 0:NSB], SEL[r, 1, 0:NSB]
            r1, r2 = SEL[r, 2, 0:NSB], SEL[r, 3, 0:NSB]
            link(dve.tensor_tensor(r1, PS[r, 7, 0:NSB], rowc[r, 0:NSB], ALU.mult))
            link(dve.tensor_tensor(score, r1, rowc[r, NSB:2 * NSB], ALU.add))
            link(dve.tensor_tensor(cube[r], bcast(score, 0, NSB), bcast(score, 1, NSB), ALU.is_gt))
            link(dve.tensor_reduce(r1, cube[r], AX.X, ALU.add))
            link(dve.tensor_tensor(cube[r], bcast(score, 0, NSB), bcast(score, 1, NSB), ALU.is_equal))
            link(dve.tensor_tensor(cube[r], cube[r], tri[r], ALU.mult))
            link(dve.tensor_reduce(r2, cube[r], AX.X, ALU.add))
            link(dve.tensor_tensor(r1, r1, r2, ALU.add))
            link(dve.tensor_scalar(sel, r1, float(NSEL), NEG, ALU.is_ge, ALU.mult))
            dve.wait_ge(kv_used, F_SLCK + B)
            link(dve.tensor_tensor(L96[r, 0:PAST].rearrange("p (a b) -> p a b", a=4), PS[r, 0:4, :],
                                   bias96[0:ROWS, 0:PAST].rearrange("p (a b) -> p a b", a=4), ALU.add))
            link(dve.tensor_tensor(L96[r, 0:PAST].rearrange("p (s x) -> p s x", x=64),
                                   L96[r, 0:PAST].rearrange("p (s x) -> p s x", x=64),
                                   bcast(sel[:, 0:NSB - 1], 1, 64), ALU.add))
            link(dve.tensor_tensor(L96[r, PAST:PAST + 1], PS[r, 5, 0:1], bias96[0:ROWS, PAST:PAST + 1], ALU.add))
            dve.tensor_reduce(s1(8), L96[r, 0:PAST + 1], AX.X, ALU.max, negate=True).then_inc(ds_max, 1)
            dve.wait_ge(kv_used, F_WINK + 2)
            link(dve.tensor_tensor(Lw[r, 0:T], PS[r, 4, :], bias96[0:ROWS, PAST - T:PAST], ALU.add))
            link(dve.tensor_tensor(Lw[r, T:T + 1], PS[r, 5, 1:2], bias96[0:ROWS, PAST:PAST + 1], ALU.add))
            link(dve.memset(Lw[r, 0:1], NEG))
            dve.tensor_reduce(s1(12), Lw[r, 0:T + 1], AX.X, ALU.max, negate=True).then_inc(ds_max, 1)
            for i, (L, n) in enumerate(((L96, PAST + 1), (Lw, T + 1))):
                a = 8 + 4 * i
                dve.wait_ge(ds_exp, i + 1)
                link(dve.reciprocal(s1(a + 2), s1(a + 1)))
                link(dve.tensor_tensor(s1(a + 3), s1(a + 2), g96[r, i + 1:i + 2], ALU.mult))
                dve.tensor_scalar(L[r, 0:n], L[r, 0:n], s1(a + 3), None, ALU.mult).then_inc(ds_p, 1)
            dve.wait_ge(ds_t, 1)
            dve.tensor_copy(PTs[:, 0:15].rearrange("p (a b) x -> p a (b x)", a=3), PS[:, 0:3, 0:5 * ROWS])
            dve.tensor_copy(PTs[:, 15], PS[:, 3, 0:ROWS])
            dve.tensor_copy(PTd[:, 0:4].rearrange("p a x -> p (a x)"), PS[:, 3, ROWS:5 * ROWS])
            dve.tensor_copy(PTd[0:NC, 4], PS[0:NC, 4, 0:ROWS])
            dve.tensor_copy(PTd[0:1, 5:7].rearrange("p a x -> p (a x)"), PS[0:1, 4, ROWS:3 * ROWS]
                            ).then_inc(ds_pt, 1)
            dve.wait_ge(kv_used, F_SLCV)
            dve.tensor_copy(OS[0:NH].rearrange("p (a x) -> p a x", a=4), PS[0:NH, 0:4, :]).then_inc(os_moved, 1)
            dve.wait_ge(th_in, 16)

            def add_values(b):
                dve.wait_ge(kv_used, F_SLCV + b + 1)
                o = OS[0:NH, b * 256:b * 256 + 256]
                dve.tensor_tensor(o, o, PS[0:NH, 7, (b % 2) * 256:(b % 2) * 256 + 256], ALU.add).then_inc(sv_added, 1)

            prompt_attention(1, add_values)
            dve.wait_ge(os_turned, 1)
            for g2 in range(2):
                r0 = 64 * g2
                v = PS[r0:r0 + 64, 7, 0:2 * ROWS].rearrange("p (b a r) -> p a b r", a=2, r=NH)
                for pair in range(2):
                    a = pair * 6 + g2 * HPG
                    ins = dve.tensor_copy(MIX[r0:r0 + 64, pair * HPG:pair * HPG + HPG, T:TOK],
                                          v[:, pair, :, a:a + HPG].rearrange("p b h -> p h b"))
            ins.then_inc(ds_out, 1)
            out_units(C_OUT1)
            norm(2)
            dve.wait_ge(x_ready, 3 * KT)
            router(1)
            moe(1)
            norm(3)


def bucket(dist):
    n = np.maximum(dist, 0)
    nf = np.maximum(n, 1).astype(np.float32)
    large = 16 + (np.log(nf / np.float32(16)) / np.float32(math.log(64)) * np.float32(16)).astype(np.int32)
    return np.where(n < 16, n, np.minimum(large, 31))


def one_hot(dist, rows):
    at = np.where(dist < 0, 32, bucket(dist))
    return (np.arange(rows)[:, None] == at[None, :]).astype(np.float32)


def chunk(w):
    out = np.zeros((KT, P, P), np.float32)
    out[:, :, :w.shape[1]] = w.reshape(KT, P, -1)
    return out.transpose(1, 0, 2).reshape(P, D)


def fm(a):
    return a.T.reshape(-1, P, a.shape[0]).transpose(1, 0, 2)


def kernel(**inputs):
    import concourse.bacc as bacc
    from concourse.bass_utils import run_bass_kernel_spmd

    x = {k: np.asarray(v) for k, v in inputs.items()}
    f = np.ascontiguousarray
    perm = np.arange(768).reshape(2, 2, HPG, HD).transpose(0, 2, 1, 3).reshape(-1)

    w = np.empty((NCH, P, D), np.float32)
    n = 0

    def put(*blocks):
        nonlocal n
        for blk in blocks:
            w[n] = blk
            n += 1

    def columns(a):
        return [chunk(a[:, i:i + P]) for i in range(0, a.shape[1], P)]

    def experts(layer):
        for e in range(EXPERTS):
            gu = np.stack([x["w_exp_gate"][layer, e], x["w_exp_up"][layer, e]], axis=1).reshape(2, 4, P, 256)
            put(*gu.transpose(0, 2, 1, 3).reshape(2, P, D), x["w_exp_down"][layer, e])

    for layer in range(2):
        put(*columns(x["w_mem_kv"][layer]))
    put(*columns(x["w_in_a"][0]))
    put(*columns(x["w_out"][0]))
    experts(0)
    put(*columns(x["w_kv_shared"]))
    wb = x["w_in_b"][0]
    put(*columns(wb[:, :768][:, perm]), *columns(wb[:, 804:1060]), *columns(wb[:, 768:804]))
    put(*columns(x["w_out"][1][np.concatenate([perm, np.arange(768, D)])]))
    experts(1)
    assert n == NCH

    def cols(a):
        return a.reshape(-1, P).T

    pk = np.empty((P, NPK), np.float32)
    w1 = x["cmp_w1"]
    valid = (np.arange(P) >= 31).astype(np.float32)[:, None]
    parts = {"ln1g": cols(x["ln1_g"]), "ln1b": cols(x["ln1_b"]), "ln2g": cols(x["ln2_g"]), "ln2b": cols(x["ln2_b"]),
             "cb": cols(x["conv_b"][0]), "cw": cols(x["conv_w"][0]), "brg": cols(x["b_rg"][0]),
             "big": cols(x["b_ig"][0]), "lam": cols(x["lru_lambda"][0]), "b1": x["cmp_b1"].T,
             "pe": x["cmp_pe"].reshape(32, P).T, "valid": valid,
             "h0": fm(x["state_lru_h"][0]).reshape(P, -1),
             "st": x["state_conv"][0].transpose(2, 1, 0).reshape(RNN, P, 3, B).transpose(1, 0, 2, 3).reshape(P, -1)}
    for k, v in parts.items():
        pk[:, PK[k][0]:PK[k][1]] = v

    def block_diagonal(a):
        out = np.zeros((P, RNN, P), np.float32)
        for t in range(RNN):
            out[:64, t, :64], out[64:, t, 64:] = a[2 * t], a[2 * t + 1]
        return out

    blocks = np.arange(NSB)
    forced = (blocks == 0) | (blocks >= NSB - 2)
    rowc = np.concatenate([~forced, forced * 1e9, np.arange(EGRP, 0, -1), np.arange(EPG, 0, -1)]
                          ).astype(np.float32)[None]
    c0, s0 = np.arange(NC) * 16, blocks * 64
    cover = ((c0[:, None] < s0[None] + 64) & (c0[:, None] + 32 > s0[None])).astype(np.float32)
    tri = (blocks[None, :] < blocks[:, None]).astype(np.float32).reshape(1, NSB, NSB)

    rk = np.zeros((P, NRK), np.float32)
    rk[:RT, RK_UP:RK_UP + RT] = np.triu(np.ones((RT, RT), np.float32), 1) / D
    rk[:, RK_128:RK_128 + P] = np.arange(P)
    rk[:, RK_8:RK_8 + 8] = np.arange(8)
    rk[:, RK_T4:RK_T4 + 4] = np.arange(1, 5) * P
    rk[:, RK_T5:RK_T5 + 5] = np.arange(5) * P
    rk[:, RK_TOK:RK_TOK + NRT] = np.arange(NRT) * RT + np.arange(P)[:, None]

    cc, cs, cw, cm = x["cache_cmp_kv"], x["cache_slc_kv"], x["cache_win_kv"], x["cache_mem_kv"]
    wr = np.concatenate([x["w_router_g"], x["w_router_e"]], axis=2).reshape(2, KT, P, 36).transpose(2, 0, 1, 3)
    dram = {
        "pages": x["page_table"].reshape(1, P).astype(np.int32),
        "wstream": w,
        "xT": fm(np.concatenate([x["x_prompt"][0], x["x_sample"][:, 0]])),
        "memT": fm(x["mem_prompt"][0]),
        "pk": pk, "rowc": rowc, "ident": np.eye(P, dtype=np.float32), "wr": wr,
        "rb": np.concatenate([x["b_router_g"], x["b_router_e"]], axis=1)[None],
        "tab": x["rel_bias"], "tab96": np.tile(x["rel_bias"], (1, B)), "cover": cover,
        "w2s": x["cmp_w2"].transpose(1, 0, 2),
        "ohp": one_hot(511 - np.arange(640), 33), "ohc": one_hot(np.arange(992) - 511, 33),
        "ohd": one_hot(np.maximum(PAST - np.arange(PAST + 8), 0), 32),
        "tri": tri, "rk": rk,
        "w1p": w1.reshape(2, 16, P, P).transpose(2, 0, 1, 3),
        "wbd": np.stack([block_diagonal(x["w_rg"][0]), block_diagonal(x["w_ig"][0])], axis=1),
        "cc": cc.reshape(NPOOL, 64, 2, 2, GRP, HD).transpose(0, 2, 5, 3, 4, 1).reshape(NPOOL, P, 512),
        "slck": cs[:, :, 0].reshape(NPOOL, P, 2, 2, HD).transpose(0, 3, 4, 2, 1).reshape(NPOOL, P, 256),
        "slcv": cs[:, :, 1].reshape(NPOOL, P, 256),
        "wink": cw[:, :, 0].reshape(B, 4, P, 2, 2, HD).transpose(0, 4, 5, 1, 3, 2).reshape(B, P, 1024),
        "winv": cw[:, :, 1].reshape(B, 4, P, 256).transpose(0, 2, 1, 3).reshape(B, P, 1024),
        "winnat": cw.reshape(B, T, 512),
        "memk": cm[:, :, :, 0].reshape(2, B, MEM, 2, 2, HD).transpose(0, 1, 4, 5, 3, 2).reshape(2, B, P, 512),
        "memv": cm[:, :, :, 1].reshape(2, B, 2, P, 256).transpose(0, 1, 3, 2, 4).reshape(2, B, P, 512),
    }
    dram = {k: f(v) for k, v in dram.items()}
    outs = {"o_y": [P, KT, TOK], "o_memk": [P, 2, 2, MEM], "o_memv": [P, 2, 2, 256], "o_st": [P, 144],
            "o_xr": [P, RNN, 3 + B], "o_h": [P, RNN, 1 + B], "o_cmp": [P, 2, 2, TOK], "o_k": [2, P, 2, TOK],
            "o_v": [2, P, QT, 256], "o_vd": [2, B, 256], "o_winold": [B, T - 1, 512]}
    scratch = {"x_tm": [TOK, D], "y_tm": [SLOTS * P, D], "rd": [NH, 640], "rd_rows": [P, NH * 640], "gd": [B, 36]}

    nc = bacc.Bacc("TRN2", target_bir_lowering=False, num_devices=1)
    dr = {k: nc.dram_tensor(k, list(v.shape), mybir.dt.from_np(v.dtype), kind="ExternalInput").ap()
          for k, v in dram.items()}
    dr.update({k: nc.dram_tensor(k, s, F32, kind="ExternalOutput").ap() for k, s in outs.items()})
    dr.update({k: nc.dram_tensor(k, s, F32, kind="Internal").ap() for k, s in scratch.items()})
    build(nc, dr)
    res = run_bass_kernel_spmd(nc, [dram], core_ids=[0]).results[0]
    o = {k: np.asarray(res[k]).reshape(s) for k, s in outs.items()}

    def tokens(a):
        return a.transpose(2, 1, 0).reshape(a.shape[2], -1)

    y = tokens(o["o_y"])
    mem = np.stack([np.stack([tokens(o["o_memk"][:, layer]),
                              o["o_memv"][:, layer].transpose(1, 0, 2).reshape(MEM, 256)], axis=1)
                    for layer in range(2)]).reshape(2, 1, MEM, 2, 4, HD)
    cmp_ = np.stack([tokens(o["o_cmp"][:, 0]), tokens(o["o_cmp"][:, 1])], axis=1).reshape(TOK, 2, GRP, HD)
    rows = []
    for i in range(2):
        v = np.concatenate([o["o_v"][i].transpose(1, 0, 2).reshape(T, 256), o["o_vd"][i]])
        rows.append(np.stack([tokens(o["o_k"][i]), v], axis=1).reshape(TOK, 2, GRP, HD))
    slc, win = rows
    xr = tokens(o["o_xr"])
    h = tokens(o["o_h"])
    state = o["o_st"].reshape(P, RNN, 3, B).transpose(3, 2, 1, 0).reshape(B, 3, 768)
    s_win = np.concatenate([o["o_winold"].reshape(B, T - 1, 2, GRP, HD), win[T:, None]], axis=1)
    s_conv = np.concatenate([state[:, 1:], xr[3:, None]], axis=1)
    leaves = (y[None, :T], y[T:, None], cmp_[None, :T], slc[None, :T], win[None, :T], mem, h[None, :1],
              xr[None, None, :3], cmp_[T:, None], slc[T:, None], s_win, h[None, 1:], s_conv[None])
    return tuple(f(a) for a in leaves)
```
